# Optimizing a Trainium2 kernel written in Bass

```python
import math
import jax, jax.numpy as jnp
from jax import lax
import numpy as np

D_MODEL = 1024
BATCH = 1
SEQ = 256
DEPTH = 2

BLOCK = 128
A_WIDTH = D_MODEL // 2
A_HEAD_DIM = 64
A_HEADS = A_WIDTH // A_HEAD_DIM
A_KV_HEADS = A_HEADS // 4
WINDOW = 128
B_WIDTH = D_MODEL - A_WIDTH
SSM_GROUP = 16
SSM_GROUPS = B_WIDTH // SSM_GROUP
SSM_STATE = 64
DT_MIN = 0.001
DT_MAX = 0.1
C_WIDTH = D_MODEL
C_HEADS = A_HEADS
C_HEAD_DIM = C_WIDTH // C_HEADS
C_KV_HEADS = C_HEADS // 4
IDX_HEADS = 8
IDX_DIM = 64
TOPK_MAX = 256
NUM_BUCKETS = 32
REL_MAX_DIST = 1024
EPS = 1e-6
NEG_INF = -1e30

EVEN_SPLITS = (A_WIDTH, A_KV_HEADS * A_HEAD_DIM, A_KV_HEADS * A_HEAD_DIM, A_WIDTH, B_WIDTH, B_WIDTH)
ODD_SPLITS = (C_WIDTH, C_KV_HEADS * C_HEAD_DIM, C_KV_HEADS * C_HEAD_DIM, C_WIDTH,
              IDX_HEADS * IDX_DIM, IDX_DIM, IDX_HEADS)
N_EVEN = (DEPTH + 1) // 2
N_ODD = DEPTH // 2


def rms_norm(x, g):
    xf = x.astype(jnp.float32)
    y = xf * lax.rsqrt(jnp.mean(xf * xf, axis=-1, keepdims=True) + EPS)
    return (y * g.astype(jnp.float32)).astype(x.dtype)

def split_cols(z, sizes):
    idx = np.cumsum(sizes)[:-1].tolist()
    return jnp.split(z, idx, axis=-1)

def t5_bucket(dist):
    n = jnp.maximum(dist, 0)
    max_exact = NUM_BUCKETS // 2
    nf = jnp.maximum(n, 1).astype(jnp.float32)
    large = max_exact + (jnp.log(nf / max_exact) / math.log(REL_MAX_DIST / max_exact)
                         * (NUM_BUCKETS - max_exact)).astype(jnp.int32)
    large = jnp.minimum(large, NUM_BUCKETS - 1)
    return jnp.where(n < max_exact, n, large)

def swa_sink_attention(q, k, v, sinks, rel_bias):
    bsz, L, H, Dh = q.shape
    hkv = k.shape[2]
    G = H // hkv
    nb = L // BLOCK
    qb = q.reshape(bsz, nb, BLOCK, hkv, G, Dh)
    kb = k.reshape(bsz, nb, BLOCK, hkv, Dh)
    vb = v.reshape(bsz, nb, BLOCK, hkv, Dh)
    k_band = jnp.concatenate([jnp.concatenate([jnp.zeros_like(kb[:, :1]), kb[:, :-1]], axis=1), kb], axis=2)
    v_band = jnp.concatenate([jnp.concatenate([jnp.zeros_like(vb[:, :1]), vb[:, :-1]], axis=1), vb], axis=2)
    logits = jnp.einsum('bnqhgd,bnkhd->bnhgqk', qb, k_band).astype(jnp.float32) * (Dh ** -0.5)
    i = jnp.arange(BLOCK, dtype=jnp.int32)[:, None]
    j = jnp.arange(2 * BLOCK, dtype=jnp.int32)[None, :]
    d = i + BLOCK - j
    in_window = (d >= 0) & (d < WINDOW)
    first = (jnp.arange(nb) == 0)[:, None, None] & (j < BLOCK)[None]
    mask = in_window[None] & ~first
    bias = rel_bias[t5_bucket(d)].astype(jnp.float32)
    bias = bias.transpose(2, 0, 1).reshape(hkv, G, BLOCK, 2 * BLOCK)
    logits = jnp.where(mask[None, :, None, None], logits + bias, NEG_INF)
    sink = jnp.broadcast_to(sinks.astype(jnp.float32).reshape(1, 1, hkv, G, 1, 1), logits.shape[:-1] + (1,))
    p = jax.nn.softmax(jnp.concatenate([logits, sink], axis=-1), axis=-1)[..., :-1]
    out = jnp.einsum('bnhgqk,bnkhd->bnqhgd', p.astype(v.dtype), v_band)
    return out.reshape(bsz, L, H * Dh)

def ssm_combine(e1, e2):
    a1r, a1i, b1r, b1i = e1
    a2r, a2i, b2r, b2i = e2
    ar = a1r * a2r - a1i * a2i
    ai = a1r * a2i + a1i * a2r
    br = a2r * b1r - a2i * b1i + b2r
    bi = a2r * b1i + a2i * b1r + b2i
    return (ar, ai, br, bi)

def s5_mixer(u, log_dt, a_re, a_im, b_re, b_im, c_re, c_im, d_skip, glu_w, glu_b):
    bsz, L, W = u.shape
    G, P = a_re.shape
    ug = u.reshape(bsz, L, G, W // G)
    dt = jnp.exp(log_dt)[:, None]
    mag = jnp.exp(a_re * dt)
    ang = a_im * dt
    ab_re = mag * jnp.cos(ang)
    ab_im = mag * jnp.sin(ang)
    den = a_re * a_re + a_im * a_im
    n_re = ab_re - 1.0
    n_im = ab_im
    f_re = (n_re * a_re + n_im * a_im) / den
    f_im = (n_im * a_re - n_re * a_im) / den
    bb_re = f_re[..., None] * b_re - f_im[..., None] * b_im
    bb_im = f_re[..., None] * b_im + f_im[..., None] * b_re
    bu_re = jnp.einsum('blgh,gph->blgp', ug, bb_re)
    bu_im = jnp.einsum('blgh,gph->blgp', ug, bb_im)
    at_re = jnp.broadcast_to(ab_re[None, None], (1, L, G, P))
    at_im = jnp.broadcast_to(ab_im[None, None], (1, L, G, P))
    _, _, x_re, x_im = lax.associative_scan(ssm_combine, (at_re, at_im, bu_re, bu_im), axis=1)
    y = (jnp.einsum('blgp,ghp->blgh', x_re, c_re) - jnp.einsum('blgp,ghp->blgh', x_im, c_im)
         + d_skip * ug)
    y = jax.nn.gelu(y.reshape(bsz, L, W))
    h = y @ glu_w + glu_b
    return h[..., :W] * jax.nn.sigmoid(h[..., W:])

def dsa_attention(q, k, v, qi, ki, wi, rel_bias):
    bsz, L, H, Dh = q.shape
    hkv = k.shape[2]
    G = H // hkv
    nb = L // BLOCK
    topk = min(TOPK_MAX, L // 4)
    qb = q.reshape(bsz, nb, BLOCK, hkv, G, Dh).transpose(1, 0, 2, 3, 4, 5)
    qib = qi.reshape(bsz, nb, BLOCK, IDX_HEADS, IDX_DIM).transpose(1, 0, 2, 3, 4)
    wib = wi.reshape(bsz, nb, BLOCK, IDX_HEADS).transpose(1, 0, 2, 3)
    starts = jnp.arange(nb, dtype=jnp.int32) * BLOCK
    key_pos = jnp.arange(L, dtype=jnp.int32)

    def one_block(args):
        q_blk, qi_blk, w_blk, start = args
        t = start + jnp.arange(BLOCK, dtype=jnp.int32)
        rel = jax.nn.relu(jnp.einsum('bqhd,bsd->bqhs', qi_blk, ki).astype(jnp.float32) * (IDX_DIM ** -0.5))
        score = jnp.einsum('bqhs,bqh->bqs', rel, w_blk.astype(jnp.float32))
        score = jnp.where(key_pos[None, None, :] <= t[None, :, None], score, NEG_INF)
        _, idx = lax.top_k(score, topk)
        valid = idx <= t[None, :, None]
        k_sel = jax.vmap(lambda kk, ii: kk[ii])(k, idx)
        v_sel = jax.vmap(lambda vv, ii: vv[ii])(v, idx)
        logits = jnp.einsum('bqhgd,bqkhd->bqhgk', q_blk, k_sel).astype(jnp.float32) * (Dh ** -0.5)
        bias = rel_bias[t5_bucket(t[None, :, None] - idx)].astype(jnp.float32)
        bias = bias.reshape(bsz, BLOCK, topk, hkv, G).transpose(0, 1, 3, 4, 2)
        logits = jnp.where(valid[:, :, None, None, :], logits + bias, NEG_INF)
        p = jax.nn.softmax(logits, axis=-1).astype(v.dtype)
        return jnp.einsum('bqhgk,bqkhd->bqhgd', p, v_sel)

    out = lax.map(one_block, (qb, qib, wib, starts))
    return out.transpose(1, 0, 2, 3, 4, 5).reshape(bsz, L, H * Dh)

def even_layer(hn, rel_bias, w_in, w_out, q_g, k_g, sinks, log_dt, a_re, a_im, b_re, b_im,
               c_re, c_im, d_skip, glu_w, glu_b):
    bsz, L, _ = hn.shape
    q, k, v, gate_a, u, gate_b = split_cols(hn @ w_in, EVEN_SPLITS)
    q = rms_norm(q.reshape(bsz, L, A_HEADS, A_HEAD_DIM), q_g)
    k = rms_norm(k.reshape(bsz, L, A_KV_HEADS, A_HEAD_DIM), k_g)
    v = v.reshape(bsz, L, A_KV_HEADS, A_HEAD_DIM)
    att = swa_sink_attention(q, k, v, sinks, rel_bias) * jax.nn.silu(gate_a)
    ssm = s5_mixer(u, log_dt, a_re, a_im, b_re, b_im, c_re, c_im, d_skip, glu_w, glu_b) * jax.nn.silu(gate_b)
    return jnp.concatenate([att, ssm], axis=-1) @ w_out

def odd_layer(hn, rel_bias, w_in, w_out, q_g, k_g):
    bsz, L, _ = hn.shape
    q, k, v, gate, qi, ki, wi = split_cols(hn @ w_in, ODD_SPLITS)
    q = rms_norm(q.reshape(bsz, L, C_HEADS, C_HEAD_DIM), q_g)
    k = rms_norm(k.reshape(bsz, L, C_KV_HEADS, C_HEAD_DIM), k_g)
    v = v.reshape(bsz, L, C_KV_HEADS, C_HEAD_DIM)
    qi = qi.reshape(bsz, L, IDX_HEADS, IDX_DIM)
    wi = wi * (IDX_HEADS ** -0.5)
    att = dsa_attention(q, k, v, qi, ki, wi, rel_bias)
    return (att * jax.nn.silu(gate)) @ w_out

def first_inputs(seed: int = 0) -> dict:
    key = jax.random.key(seed)
    ks = jax.random.split(key, 24)
    f32 = jnp.float32

    def nrm(k, shape, s):
        return jax.random.normal(k, shape, f32) * s

    ev_in = sum(EVEN_SPLITS)
    od_in = sum(ODD_SPLITS)
    ssm_n = jnp.arange(SSM_STATE, dtype=f32)
    return {
        'x': nrm(ks[0], (BATCH, SEQ, D_MODEL), 1.0),
        'rel_bias': nrm(ks[1], (NUM_BUCKETS, A_HEADS), 0.5),
        'norm_g': 1.0 + nrm(ks[2], (DEPTH, D_MODEL), 0.02),
        'ev_w_in': nrm(ks[3], (N_EVEN, D_MODEL, ev_in), D_MODEL ** -0.5),
        'ev_w_out': nrm(ks[4], (N_EVEN, A_WIDTH + B_WIDTH, D_MODEL), (A_WIDTH + B_WIDTH) ** -0.5),
        'ev_q_norm_g': 1.0 + nrm(ks[5], (N_EVEN, A_HEAD_DIM), 0.02),
        'ev_k_norm_g': 1.0 + nrm(ks[6], (N_EVEN, A_HEAD_DIM), 0.02),
        'ev_sinks': nrm(ks[7], (N_EVEN, A_HEADS), 1.0),
        'ev_ssm_log_dt': jax.random.uniform(ks[8], (N_EVEN, SSM_GROUPS), f32, math.log(DT_MIN), math.log(DT_MAX)),
        'ev_ssm_a_re': -0.5 + nrm(ks[9], (N_EVEN, SSM_GROUPS, SSM_STATE), 0.01),
        'ev_ssm_a_im': jnp.pi * ssm_n + nrm(ks[10], (N_EVEN, SSM_GROUPS, SSM_STATE), 0.01),
        'ev_ssm_b_re': nrm(ks[11], (N_EVEN, SSM_GROUPS, SSM_STATE, SSM_GROUP), (2 * SSM_GROUP) ** -0.5),
        'ev_ssm_b_im': nrm(ks[12], (N_EVEN, SSM_GROUPS, SSM_STATE, SSM_GROUP), (2 * SSM_GROUP) ** -0.5),
        'ev_ssm_c_re': nrm(ks[13], (N_EVEN, SSM_GROUPS, SSM_GROUP, SSM_STATE), (2 * SSM_STATE) ** -0.5),
        'ev_ssm_c_im': nrm(ks[14], (N_EVEN, SSM_GROUPS, SSM_GROUP, SSM_STATE), (2 * SSM_STATE) ** -0.5),
        'ev_ssm_d': nrm(ks[15], (N_EVEN, SSM_GROUPS, SSM_GROUP), 1.0),
        'ev_glu_w': nrm(ks[16], (N_EVEN, B_WIDTH, 2 * B_WIDTH), B_WIDTH ** -0.5),
        'ev_glu_b': nrm(ks[17], (N_EVEN, 2 * B_WIDTH), 0.01),
        'od_w_in': nrm(ks[18], (N_ODD, D_MODEL, od_in), D_MODEL ** -0.5),
        'od_w_out': nrm(ks[19], (N_ODD, C_WIDTH, D_MODEL), C_WIDTH ** -0.5),
        'od_q_norm_g': 1.0 + nrm(ks[20], (N_ODD, C_HEAD_DIM), 0.02),
        'od_k_norm_g': 1.0 + nrm(ks[21], (N_ODD, C_HEAD_DIM), 0.02),
    }

def first_block(x, rel_bias, norm_g, ev_w_in, ev_w_out, ev_q_norm_g, ev_k_norm_g, ev_sinks,
              ev_ssm_log_dt, ev_ssm_a_re, ev_ssm_a_im, ev_ssm_b_re, ev_ssm_b_im, ev_ssm_c_re,
              ev_ssm_c_im, ev_ssm_d, ev_glu_w, ev_glu_b, od_w_in, od_w_out, od_q_norm_g, od_k_norm_g):
    h = x
    for layer in range(DEPTH):
        hn = rms_norm(h, norm_g[layer])
        j = layer // 2
        if layer % 2 == 0:
            out = even_layer(hn, rel_bias, ev_w_in[j], ev_w_out[j], ev_q_norm_g[j], ev_k_norm_g[j],
                             ev_sinks[j], ev_ssm_log_dt[j], ev_ssm_a_re[j], ev_ssm_a_im[j],
                             ev_ssm_b_re[j], ev_ssm_b_im[j], ev_ssm_c_re[j], ev_ssm_c_im[j],
                             ev_ssm_d[j], ev_glu_w[j], ev_glu_b[j])
        else:
            out = odd_layer(hn, rel_bias, od_w_in[j], od_w_out[j], od_q_norm_g[j], od_k_norm_g[j])
        h = h + out
    return h


GRID_W = 64
CTX_LEN = 256
N_MIXERS = 2
N_ATTN_LAYERS = (DEPTH + 1) // 2
N_SSM_LAYERS = DEPTH // 2

HEAD_DIM = 64
N_HEADS = D_MODEL // HEAD_DIM
N_KV_HEADS = N_HEADS // 4
Q_PER_KV = N_HEADS // N_KV_HEADS
Q_DIM = N_HEADS * HEAD_DIM
QKV_DIM = (N_HEADS + 2 * N_KV_HEADS) * HEAD_DIM
ROPE_FREQS = HEAD_DIM // 4
ROPE_BASE = 10000.0

D_INNER = 2 * D_MODEL
SSM_HEAD_DIM = 64
SSM_HEADS = D_INNER // SSM_HEAD_DIM
SSM_GROUPS_2 = 8
HEADS_PER_GROUP = SSM_HEADS // SSM_GROUPS_2
D_STATE = 128
D_CONV = 3
CHUNK = 128
CONV_DIM = D_INNER + 2 * SSM_GROUPS_2 * D_STATE
IN_PROJ_DIM = D_INNER + CONV_DIM + 2 * SSM_HEADS

D_FF = ((8 * D_MODEL // 3 + 255) // 256) * 256


F32 = jnp.float32

def rmsnorm(x, g):
    x32 = x.astype(F32)
    y = x32 * lax.rsqrt(jnp.mean(x32 * x32, axis=-1, keepdims=True) + EPS)
    return (y * g.astype(F32)).astype(x.dtype)

def modulate(x, g, shift, scale):
    return rmsnorm(x, g) * (1 + scale) + shift

def swiglu(h, w_gate, w_up, w_down):
    return (jax.nn.silu(h @ w_gate) * (h @ w_up)) @ w_down

def axial_rope_tables(L):
    rows = L // GRID_W
    row = jnp.repeat(jnp.arange(rows, dtype=F32), GRID_W)
    col = jnp.tile(jnp.arange(GRID_W, dtype=F32), rows)
    inv = ROPE_BASE ** (-jnp.arange(ROPE_FREQS, dtype=F32) / ROPE_FREQS)
    ang = jnp.stack([row, col], axis=-1)[:, :, None] * inv
    return jnp.cos(ang), jnp.sin(ang)

def axial_rope(x, cos, sin):
    xs = x.reshape(x.shape[:-1] + (2, 2, ROPE_FREQS))
    x1, x2 = xs[..., 0, :], xs[..., 1, :]
    c, s = cos[None, :, None], sin[None, :, None]
    out = jnp.stack([x1 * c - x2 * s, x2 * c + x1 * s], axis=-2)
    return out.reshape(x.shape).astype(x.dtype)

def softmax_with_sink(logits, sink):
    full = jnp.concatenate([logits, jnp.broadcast_to(sink, logits.shape[:-1] + (1,))], axis=-1)
    return jax.nn.softmax(full, axis=-1)[..., :-1]

def attention_mixer(h, hc, w_qkv, w_o, sinks, cos, sin, with_ctx_out):
    b, L, _ = h.shape
    C = hc.shape[1]
    q, k, v = jnp.split(h @ w_qkv, [Q_DIM, Q_DIM + N_KV_HEADS * HEAD_DIM], axis=-1)
    q = axial_rope(q.reshape(b, L, N_HEADS, HEAD_DIM), cos, sin)
    k = axial_rope(k.reshape(b, L, N_KV_HEADS, HEAD_DIM), cos, sin)
    v = v.reshape(b, L, N_KV_HEADS, HEAD_DIM)
    q = q.reshape(b, L, N_KV_HEADS, Q_PER_KV, HEAD_DIM)
    kc, vc = jnp.split(hc @ w_qkv[:, Q_DIM:], 2, axis=-1)
    kc = kc.reshape(b, C, N_KV_HEADS, HEAD_DIM)
    vc = vc.reshape(b, C, N_KV_HEADS, HEAD_DIM)
    sink = sinks.astype(F32).reshape(1, N_KV_HEADS, Q_PER_KV, 1, 1)
    scale = HEAD_DIM ** -0.5
    pad = ((0, 0), (BLOCK, BLOCK), (0, 0), (0, 0))
    kp, vp = jnp.pad(k, pad), jnp.pad(v, pad)
    offs_q = jnp.arange(BLOCK)
    offs_k = jnp.arange(3 * BLOCK) - BLOCK

    def block(n):
        start = n * BLOCK
        qb = lax.dynamic_slice_in_dim(q, start, BLOCK, axis=1)
        kb = lax.dynamic_slice_in_dim(kp, start, 3 * BLOCK, axis=1)
        vb = lax.dynamic_slice_in_dim(vp, start, 3 * BLOCK, axis=1)
        q_pos = start + offs_q
        k_pos = start + offs_k
        valid = ((jnp.abs(k_pos[None, :] - q_pos[:, None]) <= WINDOW)
                 & (k_pos >= 0)[None, :] & (k_pos < L)[None, :])
        s_ctx = jnp.einsum('bqgrd,bkgd->bgrqk', qb, kc).astype(F32) * scale
        s_win = jnp.einsum('bqgrd,bkgd->bgrqk', qb, kb).astype(F32) * scale
        s_win = jnp.where(valid, s_win, -jnp.inf)
        p = softmax_with_sink(jnp.concatenate([s_ctx, s_win], axis=-1), sink).astype(v.dtype)
        return (jnp.einsum('bgrqk,bkgd->bqgrd', p[..., :C], vc)
                + jnp.einsum('bgrqk,bkgd->bqgrd', p[..., C:], vb))

    o = lax.map(block, jnp.arange(L // BLOCK))
    o = jnp.moveaxis(o, 0, 1).reshape(b, L, Q_DIM)
    y = o @ w_o
    if not with_ctx_out:
        return y, None
    qc = (hc @ w_qkv[:, :Q_DIM]).reshape(b, C, N_KV_HEADS, Q_PER_KV, HEAD_DIM)
    sc = jnp.einsum('bqgrd,bkgd->bgrqk', qc, kc).astype(F32) * scale
    pc = softmax_with_sink(sc, sink).astype(vc.dtype)
    oc = jnp.einsum('bgrqk,bkgd->bqgrd', pc, vc).reshape(b, C, Q_DIM)
    return y, oc @ w_o

def centred_depthwise_conv(u, w, bias):
    K = w.shape[0]
    out = lax.conv_general_dilated(u, w[:, None, :], window_strides=(1,),
                                   padding=[(K // 2, K // 2)],
                                   dimension_numbers=('NWC', 'WIO', 'NWC'),
                                   feature_group_count=u.shape[-1])
    return out + bias

def ssm_project(u, w_in, conv_w, conv_b, dt_bias):
    b, L, _ = u.shape
    z, xbc, dt = jnp.split(u @ w_in, [D_INNER, D_INNER + CONV_DIM], axis=-1)
    xbc = jax.nn.silu(centred_depthwise_conv(xbc, conv_w, conv_b))
    xs, Bm, Cm = jnp.split(xbc, [D_INNER, D_INNER + SSM_GROUPS_2 * D_STATE], axis=-1)
    dt = jax.nn.softplus(dt.reshape(b, L, 2, SSM_HEADS).astype(F32) + dt_bias.astype(F32))
    return (z,
            xs.reshape(b, L, SSM_GROUPS_2, HEADS_PER_GROUP, SSM_HEAD_DIM),
            Bm.reshape(b, L, SSM_GROUPS_2, D_STATE),
            Cm.reshape(b, L, SSM_GROUPS_2, D_STATE),
            dt.reshape(b, L, 2, SSM_GROUPS_2, HEADS_PER_GROUP))

def ssd_chunked(xs, dt, A, Bm, Cm, h0):
    b, L, G, HG, P = xs.shape
    nc = L // CHUNK
    x = xs.astype(F32).reshape(b, nc, CHUNK, G, HG, P)
    dt = dt.reshape(b, nc, CHUNK, G, HG)
    Bc = Bm.astype(F32).reshape(b, nc, CHUNK, G, D_STATE)
    Cc = Cm.astype(F32).reshape(b, nc, CHUNK, G, D_STATE)
    cum = jnp.cumsum(jnp.moveaxis(dt * A, 2, -1), axis=-1)
    xdt = x * dt[..., None]
    tri = jnp.tril(jnp.ones((CHUNK, CHUNK), dtype=bool))
    decay = jnp.exp(jnp.where(tri, cum[..., :, None] - cum[..., None, :], -jnp.inf))
    cb = jnp.einsum('bcign,bcjgn->bcgij', Cc, Bc)
    y_diag = jnp.einsum('bcghij,bcjghp->bcighp', cb[:, :, :, None] * decay, xdt)
    to_end = jnp.exp(cum[..., -1:] - cum)
    states = jnp.einsum('bcghj,bcjgn,bcjghp->bcghpn', to_end, Bc, xdt)
    chunk_decay = jnp.exp(cum[..., -1])

    def step(hs, inp):
        s, d = inp
        return d[..., None, None] * hs + s, hs

    h_final, h_start = lax.scan(step, h0.astype(F32),
                                (jnp.moveaxis(states, 1, 0), jnp.moveaxis(chunk_decay, 1, 0)))
    h_start = jnp.moveaxis(h_start, 0, 1)
    y_off = jnp.einsum('bcign,bcghpn,bcghi->bcighp', Cc, h_start, jnp.exp(cum))
    return (y_diag + y_off).reshape(b, L, G, HG, P).astype(xs.dtype), h_final

def ssd_final_state(xs, dt, A, Bm):
    cum = jnp.cumsum(dt * A, axis=1)
    decay = jnp.exp(cum[:, -1:] - cum)
    return jnp.einsum('blgh,blgn,blghp->bghpn', decay * dt, Bm.astype(F32), xs.astype(F32))

def bidirectional_ssd(xs, dt, A, Bm, Cm, h0_fwd, h0_bwd):
    flip = lambda u: jnp.flip(u, axis=1)
    y_f, h_f = ssd_chunked(xs, dt[:, :, 0], A[0], Bm, Cm, h0_fwd)
    y_b, h_b = ssd_chunked(flip(xs), flip(dt[:, :, 1]), A[1], flip(Bm), flip(Cm), h0_bwd)
    return y_f + flip(y_b), h_f, h_b

def ssm_output(y, xs, z, D_skip, norm_g, w_out):
    b, L = y.shape[:2]
    y = y + D_skip.reshape(SSM_GROUPS_2, HEADS_PER_GROUP)[:, :, None] * xs
    y = y.reshape(b, L, SSM_GROUPS_2, D_INNER // SSM_GROUPS_2) * jax.nn.silu(z).reshape(b, L, SSM_GROUPS_2, -1)
    y = rmsnorm(y, norm_g.reshape(SSM_GROUPS_2, -1))
    return y.reshape(b, L, D_INNER) @ w_out

def ssm_mixer(h, hc, w_in, conv_w, conv_b, dt_bias, A_log, D_skip, norm_g, w_out, with_ctx_out):
    A = -jnp.exp(A_log.astype(F32)).reshape(2, SSM_GROUPS_2, HEADS_PER_GROUP)
    zc, xc, Bc, Cc, dtc = ssm_project(hc, w_in, conv_w, conv_b, dt_bias)
    if with_ctx_out:
        zeros = jnp.zeros((hc.shape[0], SSM_GROUPS_2, HEADS_PER_GROUP, SSM_HEAD_DIM, D_STATE), F32)
        yc, hc_f, hc_b = bidirectional_ssd(xc, dtc, A, Bc, Cc, zeros, zeros)
        out_c = ssm_output(yc, xc, zc, D_skip, norm_g, w_out)
    else:
        hc_f = ssd_final_state(xc, dtc[:, :, 0], A[0], Bc)
        hc_b = ssd_final_state(jnp.flip(xc, 1), jnp.flip(dtc[:, :, 1], 1), A[1], jnp.flip(Bc, 1))
        out_c = None
    z, xs, Bm, Cm, dt = ssm_project(h, w_in, conv_w, conv_b, dt_bias)
    y, _, _ = bidirectional_ssd(xs, dt, A, Bm, Cm, hc_f, hc_b)
    return ssm_output(y, xs, z, D_skip, norm_g, w_out), out_c

def second_inputs(seed: int = 0) -> dict:
    key = jax.random.key(seed)
    ks = jax.random.split(key, 24)
    nrm = lambda k, shape, s: jax.random.normal(k, shape, F32) * s
    dt_init = jnp.exp(jax.random.uniform(ks[16], (N_SSM_LAYERS, 2, SSM_HEADS), F32,
                                         minval=math.log(1e-3), maxval=math.log(1e-1)))
    return {
        "x": nrm(ks[0], (BATCH, SEQ, D_MODEL), 1.0),
        "c": nrm(ks[1], (BATCH, D_MODEL), 1.0),
        "ctx": nrm(ks[2], (BATCH, CTX_LEN, D_MODEL), 1.0),
        "c_ctx": nrm(ks[3], (D_MODEL,), 1.0),
        "ada_w": nrm(ks[4], (DEPTH, D_MODEL, 6 * D_MODEL), 0.5 * D_MODEL ** -0.5),
        "ada_b": nrm(ks[5], (DEPTH, 6 * D_MODEL), 0.01),
        "norm_mix_g": 1.0 + nrm(ks[6], (DEPTH, D_MODEL), 0.05),
        "norm_ffn_g": 1.0 + nrm(ks[7], (DEPTH, D_MODEL), 0.05),
        "attn_w_qkv": nrm(ks[8], (N_ATTN_LAYERS, D_MODEL, QKV_DIM), D_MODEL ** -0.5),
        "attn_w_o": nrm(ks[9], (N_ATTN_LAYERS, Q_DIM, D_MODEL), Q_DIM ** -0.5),
        "attn_sinks": nrm(ks[10], (N_ATTN_LAYERS, N_HEADS), 1.0),
        "ssm_w_in": nrm(ks[11], (N_SSM_LAYERS, D_MODEL, IN_PROJ_DIM), D_MODEL ** -0.5),
        "ssm_conv_w": nrm(ks[12], (N_SSM_LAYERS, D_CONV, CONV_DIM), D_CONV ** -0.5),
        "ssm_conv_b": nrm(ks[13], (N_SSM_LAYERS, CONV_DIM), 0.01),
        "ssm_dt_bias": dt_init + jnp.log(-jnp.expm1(-dt_init)),
        "ssm_A_log": jnp.log(jax.random.uniform(ks[14], (N_SSM_LAYERS, 2, SSM_HEADS), F32, minval=1.0, maxval=16.0)),
        "ssm_D": 1.0 + nrm(ks[15], (N_SSM_LAYERS, SSM_HEADS), 0.1),
        "ssm_norm_g": 1.0 + nrm(ks[17], (N_SSM_LAYERS, D_INNER), 0.05),
        "ssm_w_out": nrm(ks[18], (N_SSM_LAYERS, D_INNER, D_MODEL), D_INNER ** -0.5),
        "ffn_w_gate": nrm(ks[19], (DEPTH, D_MODEL, D_FF), D_MODEL ** -0.5),
        "ffn_w_up": nrm(ks[20], (DEPTH, D_MODEL, D_FF), D_MODEL ** -0.5),
        "ffn_w_down": nrm(ks[21], (DEPTH, D_FF, D_MODEL), D_FF ** -0.5),
        "final_norm_g": 1.0 + nrm(ks[22], (D_MODEL,), 0.05),
    }

def second_block(x, c, ctx, c_ctx, ada_w, ada_b, norm_mix_g, norm_ffn_g, attn_w_qkv, attn_w_o,
              attn_sinks, ssm_w_in, ssm_conv_w, ssm_conv_b, ssm_dt_bias, ssm_A_log, ssm_D,
              ssm_norm_g, ssm_w_out, ffn_w_gate, ffn_w_up, ffn_w_down, final_norm_g):
    L = x.shape[1]
    cos, sin = axial_rope_tables(L)
    for i in range(DEPTH):
        last = i == DEPTH - 1
        j = i // N_MIXERS
        mod = jax.nn.silu(c) @ ada_w[i] + ada_b[i]
        sh1, sc1, g1, sh2, sc2, g2 = jnp.split(mod[:, None, :], 6, axis=-1)
        mod_c = jax.nn.silu(c_ctx) @ ada_w[i] + ada_b[i]
        csh1, csc1, cg1, csh2, csc2, cg2 = jnp.split(mod_c, 6)
        h = modulate(x, norm_mix_g[i], sh1, sc1)
        hc = modulate(ctx, norm_mix_g[i], csh1, csc1)
        if i % N_MIXERS == 0:
            y, yc = attention_mixer(h, hc, attn_w_qkv[j], attn_w_o[j], attn_sinks[j],
                                    cos, sin, not last)
        else:
            y, yc = ssm_mixer(h, hc, ssm_w_in[j], ssm_conv_w[j], ssm_conv_b[j], ssm_dt_bias[j],
                              ssm_A_log[j], ssm_D[j], ssm_norm_g[j], ssm_w_out[j], not last)
        x = x + g1 * y
        x = x + g2 * swiglu(modulate(x, norm_ffn_g[i], sh2, sc2),
                            ffn_w_gate[i], ffn_w_up[i], ffn_w_down[i])
        if not last:
            ctx = ctx + cg1 * yc
            ctx = ctx + cg2 * swiglu(modulate(ctx, norm_ffn_g[i], csh2, csc2),
                                     ffn_w_gate[i], ffn_w_up[i], ffn_w_down[i])
    return rmsnorm(x, final_norm_g)


def setup_inputs(seed=0):
    out = dict(first_inputs(seed))
    for name, value in second_inputs(seed + 1).items():
        if name != "x":
            out[name + "_2"] = value
    return out


def reference(
    x, rel_bias, norm_g, ev_w_in, ev_w_out, ev_q_norm_g, ev_k_norm_g, ev_sinks, ev_ssm_log_dt,
    ev_ssm_a_re, ev_ssm_a_im, ev_ssm_b_re, ev_ssm_b_im, ev_ssm_c_re, ev_ssm_c_im, ev_ssm_d,
    ev_glu_w, ev_glu_b, od_w_in, od_w_out, od_q_norm_g, od_k_norm_g, c_2, ctx_2, c_ctx_2,
    ada_w_2, ada_b_2, norm_mix_g_2, norm_ffn_g_2, attn_w_qkv_2, attn_w_o_2, attn_sinks_2,
    ssm_w_in_2, ssm_conv_w_2, ssm_conv_b_2, ssm_dt_bias_2, ssm_A_log_2, ssm_D_2, ssm_norm_g_2,
    ssm_w_out_2, ffn_w_gate_2, ffn_w_up_2, ffn_w_down_2, final_norm_g_2,
):
    x = first_block(
        x, rel_bias, norm_g, ev_w_in, ev_w_out, ev_q_norm_g, ev_k_norm_g, ev_sinks,
        ev_ssm_log_dt, ev_ssm_a_re, ev_ssm_a_im, ev_ssm_b_re, ev_ssm_b_im, ev_ssm_c_re,
        ev_ssm_c_im, ev_ssm_d, ev_glu_w, ev_glu_b, od_w_in, od_w_out, od_q_norm_g, od_k_norm_g,
    )
    return second_block(
        x, c_2, ctx_2, c_ctx_2, ada_w_2, ada_b_2, norm_mix_g_2, norm_ffn_g_2, attn_w_qkv_2,
        attn_w_o_2, attn_sinks_2, ssm_w_in_2, ssm_conv_w_2, ssm_conv_b_2, ssm_dt_bias_2,
        ssm_A_log_2, ssm_D_2, ssm_norm_g_2, ssm_w_out_2, ffn_w_gate_2, ffn_w_up_2, ffn_w_down_2,
        final_norm_g_2,
    )


_drawn_inputs = setup_inputs


def setup_inputs(seed=0):
    import zlib

    import numpy as np

    out = dict(_drawn_inputs(seed))
    spreads = {}
    factors = {'norm_g': 2.772,
     'ev_q_norm_g': 8.0,
     'ev_k_norm_g': 8.0,
     'ev_sinks': 4.818,
     'ev_ssm_log_dt': 3.976,
     'ev_ssm_a_re': 200.0,
     'ev_ssm_a_im': 4.087,
     'ev_ssm_b_re': 5.222,
     'ev_ssm_b_im': 5.128,
     'ev_ssm_c_re': 5.246,
     'ev_ssm_c_im': 5.494,
     'ev_glu_b': 8.0,
     'od_q_norm_g': 8.0,
     'od_k_norm_g': 8.0,
     'ada_b_2': 3.453,
     'norm_mix_g_2': 2.819,
     'norm_ffn_g_2': 2.704,
     'attn_sinks_2': 64.0,
     'ssm_conv_b_2': 64.0,
     'ssm_D_2': 120.782,
     'ssm_norm_g_2': 23.52}
    for name, (base, spread) in spreads.items():
        noise = np.random.default_rng([zlib.crc32(name.encode()), seed]).standard_normal(out[name].shape)
        drawn = base * np.exp(spread * noise) if base else spread * noise
        out[name] = __import__('jax').numpy.asarray(drawn.astype(out[name].dtype))
    for name, factor in factors.items():
        out[name] = (out[name] * factor).astype(out[name].dtype)
    return out
```

```python
import math
from contextlib import ExitStack

import numpy as np

import concourse.bass as bass
from concourse import mybir

F32 = mybir.dt.float32
BF16 = mybir.dt.bfloat16
ACT = mybir.ActivationFunctionType
ALU = mybir.AluOpType
AX_X = mybir.AxisListType.X

P = 128
D = 1024
KT = D // P
L = 256
QT = L // P
EPS = 1e-6
NEG = -1e30
TAKEN = -3e38
TOPK = 64
BUCKETS = 32
EV_HEADS = 8
OD_HEADS = 8
SSM_TILES = 16
AT_HEADS = 16
FF = 2816
FT = FF // P
DI = 2048
DT_ = DI // P
GROUPS = 8
M_HEADS = 32
RING = 4
AUX = 3
AT_SCALE = 64 ** -0.5
ROUND = 1.5 * 2.0 ** 23
TWO_PI = 2.0 * math.pi
PI2_A = 6.28125
PI2_B = round((TWO_PI - PI2_A) * 2 ** 20) / 2 ** 20
PI2_C = TWO_PI - PI2_A - PI2_B

STREAM = [
    ("ev_in", 9, 2 * KT * P), ("ada0", 24, 2 * KT * P), ("glu", 2, 4 * 4 * P), ("ev_out", 4, 2 * KT * P),
    ("od_small", 1, KT * P + KT * OD_HEADS), ("od_in", 12, 2 * KT * P), ("ada1", 24, 2 * KT * P),
    ("od_out", 4, 2 * KT * P), ("qkv", 6, 2 * KT * P), ("w_o", 4, 2 * KT * P),
    ("ffn0_in", FT, 2 * KT * P), ("ffn0_out", KT, FT * P),
    ("ssm_dt", 1, KT * 2 * M_HEADS), ("ssm_in", 24, 2 * KT * P), ("ssm_out", KT, DT_ * P),
    ("ffn1_in", FT, 2 * KT * P), ("ffn1_out", KT, FT * P),
]
SLOT = FT * P
LIN_TILES = [
    ("ev_in", 18), ("s5_y", 4), ("glu", 8), ("ev_out", 8), ("od_ki", 1), ("od_in", 24), ("od_out", 8),
    ("qkv", 12), ("attn", 8), ("w_o", 8), ("ffn0_in", 2 * FT), ("ffn0_out", 8), ("ssm_dt", 1), ("ssm_in", 48),
    ("ssm_y", 16), ("ssm_out", 8), ("ffn1_in", 2 * FT), ("ffn1_out", 8),
]
AUX_TILES = [
    ("bias", 8), ("norm0", 2), ("s5_bb", 2), ("qk_norm0", 3), ("v_tok0", 1), ("scores0", 6), ("probs0", 8),
    ("out0", 4), ("s5_bu", 16),
    ("norm1", 2), ("wi", 1), ("index", 6), ("kq_norm1", 5), ("v_tok1", 1), ("scores1", 6), ("probs1", 8),
    ("out1", 8),
    ("norm2", 2), ("rope", 5), ("v_tok2", 2), ("attention", 6 * AT_HEADS), ("norm3", 2),
    ("norm4", 2), ("ssm_rows", 1), ("bc_tok", 4), ("xc_tok", 8), ("states", GROUPS), ("x_tok", 8),
    ("ssm_heads", M_HEADS + GROUPS), ("y_norm", GROUPS // 2), ("norm5", 2), ("norm6", 2),
]


def bases(table):
    at, out = 0, {}
    for name, n in table:
        out[name] = at
        at += n
    return out


def t5_bucket(dist):
    n = np.maximum(dist, 0)
    nf = np.maximum(n, 1).astype(np.float32)
    half = BUCKETS // 2
    scaled = np.log(nf / np.float32(half)) / np.float32(math.log(1024 / half)) * np.float32(half)
    return np.where(n < half, n, np.minimum(half + scaled.astype(np.int32), BUCKETS - 1))


class Count:

    def __init__(self, eng, sem):
        self.eng, self.sem, self.n = eng, sem, 0

    def mark(self, ins):
        ins.then_inc(self.sem, 1)
        self.n = self.n + 1

    def settle(self):
        self.eng.wait_ge(self.sem, self.n)

    def link(self, ins):
        self.mark(ins)
        self.settle()


class Memory:

    def __init__(self, tensor, at=0):
        self.tensor, self.at = tensor, at

    def take(self, *shape, rows=P):
        n = int(np.prod(shape))
        ap = self.tensor[0:rows, self.at:self.at + n]
        self.at += n
        assert self.at <= self.tensor.shape[1], self.at
        if len(shape) == 2:
            ap = ap.rearrange("p (a b) -> p a b", a=shape[0])
        elif len(shape) == 3:
            ap = ap.rearrange("p (a b c) -> p a b c", a=shape[0], b=shape[1])
        return ap


def rounds(eng, count, body):
    whole = count // RING
    for k in range(min(count, RING)):
        body(0, k)
    if whole > 2:
        with eng.Fori(1, whole) as i:
            for k in range(RING):
                body(i, k)
    else:
        for n in range(RING, whole * RING):
            body(n // RING, n % RING)
    for n in range(max(whole, 1) * RING, count):
        body(n // RING, n % RING)


def twice(ap):
    return ap.unsqueeze(1).to_broadcast([ap.shape[0], 2, ap.shape[1]])


def each(ap, n):
    return ap.unsqueeze(2).to_broadcast([ap.shape[0], ap.shape[1], n])


def program(nc, t):
    with ExitStack() as ctx:
        def sb(name, shape, dt=F32):
            return ctx.enter_context(nc.sbuf_tensor(name, shape, dt))

        sems = {}

        def sig(name):
            if name not in sems:
                sems[name] = ctx.enter_context(nc.semaphore(name))
            return sems[name]

        block_of = bases([(n, c) for n, c, _ in STREAM])
        lin_of = bases(LIN_TILES)
        aux_of = bases(AUX_TILES)

        ring = sb("ring", [P, RING, SLOT])
        xres = sb("xres", [P, KT, 2 * L])
        hn = sb("hn", [P, KT, 2 * L])
        rcol = sb("rcol", [P, 2 * QT])
        ident = sb("ident", [P, P])
        ones = sb("ones", [P, P])
        pair = sb("pair", [P, P])
        gcol = sb("gcol", [P, 2, KT])
        mod = sb("mod", [P, 2, 48, 2])
        modb = sb("modb", [P, 2, 48])
        sc_c = sb("sc_c", [P, KT, 32])
        ada_sb = sb("ada_sb", [P, L])
        group_sum = sb("group_sum", [P, 2])
        eps = sb("eps", [P, 1])
        half_pi = sb("half_pi", [P, 1])
        arena = sb("arena", [P, 28416])
        lin = ctx.enter_context(nc.psum_tensor("lin", [P, RING, 2 * L], F32))
        aux = ctx.enter_context(nc.psum_tensor("aux", [P, AUX, 2 * L], F32))
        modp = ctx.enter_context(nc.psum_tensor("modp", [P, 2 * L], F32))

        mem = Memory(arena)
        bias_a = mem.take(EV_HEADS, L)
        bias_b = mem.take(OD_HEADS, L)
        base = mem.at
        qa = mem.take(4, L)
        ka = mem.take(L)
        va = mem.take(L)
        v_tok = mem.take(QT, P)
        gate_a = mem.take(4, L)
        u = mem.take(4, L)
        gate_b = mem.take(4, L)
        at = mem.at
        sq0 = mem.take(5, L)
        r0 = mem.take(5, L)
        sq_end = mem.at
        mem.at = at
        lg0 = mem.take(EV_HEADS, P)
        lg1 = mem.take(EV_HEADS, L)
        pt = mem.take(EV_HEADS, 3 * P)
        end = mem.at
        mem.at = at
        table = mem.take(EV_HEADS, 3 * P)
        mem.at = max(end, mem.at, sq_end)
        cos_t = mem.take(SSM_TILES, L)
        sin_t = mem.take(SSM_TILES, L)
        s5w = mem.take(2, 2, L)
        s5z = mem.take(2, 2, L)
        s5q = mem.take(2, 2 * L).rearrange("p a (b c) -> p a b c", b=2)
        s5x = mem.take(2, 2, L)
        s5t = mem.take(2, 2 * L)
        cat = hn[:, :, L:2 * L]
        
        par = sb("par", [P, 32, SSM_TILES])
        consts = sb("consts", [P, L + L + L])
        mask_a, mask_b, steps = (consts[:, n * L:(n + 1) * L] for n in range(3))
        b_in = sb("b_in", [P, 2, SSM_TILES, 16])
        bd = s5x.rearrange("p a b c -> p (a b c)").rearrange("p (a b c) -> p a b c", a=2, b=SSM_TILES)
        bb_t = sb("bb_t", [P, 2, 4, P])
        c_bd = sb("c_bd", [P, 2, SSM_TILES, 32])
        d_col = sb("d_col", [P, 4])
        glu_b = sb("glu_b", [P, 8])
        qk_g = sb("qk_g", [P, 4])
        sink = sb("sink", [P, EV_HEADS])
        relb = s5z.rearrange("p a b c -> p (a b c)")[0:BUCKETS].rearrange("p (a b) -> p a b", a=EV_HEADS)
        hot = s5q.rearrange("p a b c -> p (a b c)")[0:BUCKETS, 0:3 * P]
        small = sb("small", [P, 12, 8])
        g2 = sb("g2", [P, 5, KT])
        nsink2_in = sb("nsink2_in", [P, AT_HEADS])
        a_col = sb("a_col", [P, KT, 2])
        ssm_cols = sb("ssm_cols", [P, 2, DT_])
        dt_cols = sb("dt_cols", [2 * M_HEADS, 2])
        stat_ssm = sb("stat_ssm", [P, 4])

        mem = Memory(arena, base)
        q1 = mem.take(OD_HEADS, L)
        k1 = mem.take(2, L)
        v1 = mem.take(2, L)
        gate1 = mem.take(OD_HEADS, L)
        qi = mem.take(4, L)
        ki = mem.take(L)
        wi = mem.take(QT, OD_HEADS)
        v_tok1 = mem.take(QT, 2 * P)
        rel = mem.take(2, 2 * L)
        idx = mem.take(QT, L)
        top = mem.take(QT, 8)
        sel = mem.take(QT, L)
        at = mem.at
        sq1 = mem.take(10, L)
        r1 = mem.take(10, L)
        end = mem.at
        mem.at = at
        lh0 = mem.take(OD_HEADS, P)
        lh1 = mem.take(OD_HEADS, L)
        pt1 = mem.take(OD_HEADS, 3 * P)
        mem.at = max(end, mem.at)

        mem = Memory(arena)
        q2 = mem.take(8, 2 * L)
        k2 = mem.take(2, 2 * L)
        v2 = mem.take(2, 2 * L)
        v_tok2 = mem.take(4, 2 * P)
        rope_cs = mem.take(2, L)
        rope_tmp = mem.take(2, L)
        mask2 = mem.take(2, P)
        rope_perm = mem.take(P)
        p2 = mem.take(3, 3, 2 * L)
        pt2 = mem.take(2, 3, 2 * L)
        stat2 = mem.take(6, AT_HEADS, 4)
        nsink2 = mem.take(2, AT_HEADS)
        ident_b = mem.take(P // 2).bitcast(BF16)
        mask_b2 = mem.take(P).bitcast(BF16).rearrange("p (a b) -> p a b", a=2)
        mem = Memory(arena)
        hid = mem.take(FT, 2 * L)
        silu_g = mem.take(RING, 2 * L)
        mem = Memory(arena)
        zs = mem.take(DT_, L)
        ys = mem.take(DT_, L)
        at = mem.at
        xc = mem.take(DT_, L)
        mem.at = at
        state = mem.take(GROUPS, 2, L)
        bm = mem.take(GROUPS, 2 * L)
        cm = mem.take(GROUPS, L)
        x_tok = mem.take(QT, DI)
        at = mem.at
        xc_tok = mem.take(QT, DI)
        end = mem.at
        mem.at = at
        cb = mem.take(2, 3 * L)
        decay = mem.take(2, 3 * L)
        from_start = mem.take(2, 2, L)
        mem.at = end
        tri = mem.take(2, P)
        rows_g = mem.take(L)
        cols_g = mem.take(3, QT, 2 * M_HEADS)
        conv_w = mem.take(32, 4)
        mem2 = Memory(hn[:].rearrange("p a b -> p (a b)"))
        bc_tok = mem2.take(QT, GROUPS * P)
        xw = mem2.take(2, QT, L)
        y_sq = hn[:].rearrange("p a b -> p (a b)").rearrange("p (a b) -> p a b", a=DT_)
        y_rs = cm
        xs_pair = arena[:, DT_ * L:3 * DT_ * L].rearrange("p (s n c) -> p n s c", s=2, n=DT_)
        dt_rows = c_bd[:].rearrange("p a b c -> p (a b c)")[0:64].rearrange("p (a b) -> p a b", a=2)
        dt2, da = dt_rows[:, 0, :], dt_rows[:, 1, :]
        spare = bb_t[:].rearrange("p a b c -> p (a b c)")[0:64].rearrange("p (a b) -> p a b", a=2)
        dt_tmp, dt_tmp2 = spare[:, 0, :], spare[:, 1, :]
        dt_tmp3 = b_in[:].rearrange("p a b c -> p (a b c)")[0:64]
        tot = stat_ssm[0:64, 0:2]
        a_neg = stat_ssm[0:64, 2:3]

        w_in = [sig(f"w_in{n}") for n in range(RING)]
        lin_free = [sig(f"lin_free{n}") for n in range(RING)]
        aux_free = [sig(f"aux_free{n}") for n in range(AUX)]

        def lin_count(tile):
            return tile + 1 - (4 if tile >= lin_of["s5_y"] + 4 else 0)

        def full(eng, banks, tile, later=0):
            eng.wait_ge(sig(banks + "_full"), later + (lin_count(tile) if banks == "lin" else tile + 1))

        def frees(ins, banks, tile):
            sems_, n = (lin_free, RING) if banks == "lin" else (aux_free, AUX)
            ins.then_inc(sems_[tile % n], 1)

        def taken(eng, banks, tile, turns=0):
            sems_, n = (lin_free, RING) if banks == "lin" else (aux_free, AUX)
            eng.wait_ge(sems_[tile % n], turns + (tile // n + 1))

        def score_tile(h, n):
            return aux_of["attention"] + max(6 * h - 3, 0) + n

        def turned_tile(h, n):
            return aux_of["attention"] + (6 * h + 6 if h < AT_HEADS - 1 else 6 * h + 3) + n

        def cb_tile(g):
            return aux_of["ssm_heads"] + 5 * g

        def bc_tile(h):
            return aux_of["ssm_heads"] + 5 * (h // 4) + 1 + h % 4

        def head_done(eng, layer, h):
            if h % 2:
                full(eng, "lin", lin_of[layer] + h // 2)
            else:
                eng.wait_ge(sig(f"{layer}_even"), h // 2 + 1)

        used = []
        for name, n, _ in STREAM:
            if name[:3] == "ada":
                used += [("ada_used", int(name[3]) * 24 + m + 1) for m in range(n)]
            else:
                stage = {"od_small": "od_ki"}.get(name, name)
                tiles = dict(LIN_TILES)[stage] // n
                used += [("lin_full", lin_count(lin_of[stage] + tiles * (m + 1) - 1)) for m in range(n)]

        def index_heads(m):
            return (1, (m % 2 + 4 * (m // 2), m % 2 + 4 * (m // 2) + 2), L) if m < 4 else \
                (0, range(m - 4, OD_HEADS, 2), P)

        block = ctx.enter_context(nc.Block())

        @block.sync
        def _(sp):
            sp.dma_start(xres[:, :, 0:L], t["x"]).then_inc(sig("x_in"), 16)
            for name, n, cols in STREAM:
                first = block_of[name]

                def load(i, k):
                    b = first + k
                    if isinstance(i, int):
                        b, i = b + i * RING, 0
                    if b >= RING or not isinstance(i, int):
                        which, value = used[b - RING] if isinstance(i, int) else used[b]
                        if not isinstance(i, int):
                            value = value + (i - 1) * (used[b + RING][1] - used[b][1])
                        sp.wait_ge(sig(which), value)
                    at = b - first + i * RING
                    source = t[name][at] if isinstance(i, int) else \
                        t[name][bass.ds(at, 1)].rearrange("a p n -> p (a n)")
                    sp.dma_start(ring[:, b % RING, 0:cols], source).then_inc(w_in[b % RING], 16)

                rounds(sp, n, load)
            sp.wait_ge(sig("hn_ready"), 7 * KT)
            sp.dma_start(t["out"], hn[:, :, 0:L]).then_inc(sig("stored"), 16)
            sp.wait_ge(sig("stored"), 16)

        def sum_squares(pool, own, k, width):
            total = hn[:, 0, 0:width]
            for kt in range(1, KT):
                pool.wait_ge(sig("squares"), KT * k + kt + 1)
                ins = nc.gpsimd.tensor_tensor(total, total, hn[:, kt, 0:width], ALU.add)
                if kt < KT - 1:
                    own.link(ins)
            ins.then_inc(sig("square_sums"), 1)

        @block.gpsimd
        def _(pool):
            own = Count(pool, sig("pool_own"))
            for dst, name in ((relb, "relb"), (hot, "hot")):
                pool.dma_start(dst, t[name]).then_inc(sig("rel_in"), 16)
            for dst, name in ((pair[:], "pair"), (consts[:], "consts"),
                              (qk_g[:], "qk_g"), (sink[:], "sink"), (d_col[:], "d_col"), (glu_b[:], "glu_b"),
                              (sc_c[:], "cc"), (group_sum[:], "group_sum"), (modb[:], "modb"), (g2[:], "g2"), (ssm_cols[:], "ssm_cols"),
                              (dt_cols[:], "dt_cols"), (nsink2_in[:], "sink2"),
                              (xres[:, :, L:2 * L], "ctx")):
                pool.dma_start(dst, t[name]).then_inc(sig("const_in"), 16)
            pool.dma_start(par[:, 0:3, :], t["s5_par"]).then_inc(sig("s5_in"), 16)
            pool.dma_start(b_in[:], t["s5_b"]).then_inc(sig("s5_in"), 16)
            nc.gpsimd.memset(eps[:], EPS)
            nc.gpsimd.memset(half_pi[:], math.pi / 2)
            nc.gpsimd.memset(ones[:], 1.0)
            nc.gpsimd.memset(bd, 0.0)
            nc.gpsimd.memset(c_bd[:], 0.0).then_inc(sig("made"), 1)
            pool.wait_ge(sig("made"), 1)
            for n in range(2):
                for part in range(2):
                    rows = slice(64 * n, 64 * n + 64)
                    pool.dma_start(c_bd[rows, part, :, 16 * n:16 * n + 16], t["s5_c"][rows, part])\
                        .then_inc(sig("c_in"), 16)
            sum_squares(pool, own, 0, L)
            taken(pool, "aux", aux_of["bias"] + EV_HEADS - 1)
            pool.dma_start(t["skew"].rearrange("h p n -> p h n"), table).then_inc(sig("table_out"), 16)
            pool.wait_ge(sig("table_out"), 16)
            skewed = bass.AP(t["skew"].tensor, P - 1, [[3 * P - 1, P], [3 * P * P, EV_HEADS], [1, L]])
            pool.dma_start(bias_b, skewed).then_inc(sig("table_back"), 16)
            for j in range(SSM_TILES):
                p = j % 2
                turned, back = s5q[:, 0], s5q[:, 1]
                z = s5z[:, p]
                pool.wait_ge(sig("z_ready"), j + 1)
                own.mark(nc.gpsimd.tensor_tensor(turned, z, twice(cos_t[:, j, :]), ALU.mult))
                own.link(nc.gpsimd.tensor_tensor(back, z, twice(sin_t[:, j, :]), ALU.mult))
                if j >= 2:
                    pool.wait_ge(sig("s5_used"), j - 1)
                own.mark(nc.gpsimd.tensor_tensor(s5x[:, p, 0, :], turned[:, 0], back[:, 1], ALU.subtract))
                nc.gpsimd.tensor_tensor(s5x[:, p, 1, :], turned[:, 1], back[:, 0], ALU.add)\
                    .then_inc(sig("x_states"), 1)
                pool.wait_ge(sig("x_states"), j + 1)
            sum_squares(pool, own, 1, L)
            sum_squares(pool, own, 2, 2 * L)
            taken(pool, "lin", lin_of["od_out"] + KT - 1)
            for dst, name in ((rope_cs, "rope_cs"), (rope_perm, "rope_perm"), (mask2, "mask2")):
                pool.dma_start(dst, t[name]).then_inc(sig("at_in"), 16)
            sum_squares(pool, own, 3, 2 * L)
            sum_squares(pool, own, 4, 2 * L)
            taken(pool, "lin", lin_of["ffn0_out"] + KT - 1)
            for dst, name in ((conv_w, "conv_w"), (tri, "tri")):
                pool.dma_start(dst, t[name]).then_inc(sig("ssm_in"), 16)
            for h in range(M_HEADS):
                taken(pool, "aux", bc_tile(h))
                rows = cm[:, h // 4, :]
                nc.gpsimd.tensor_tensor(from_start[:, h % 2], from_start[:, h % 2], twice(rows), ALU.mult)\
                    .then_inc(sig("c_decayed"), 1)
            sum_squares(pool, own, 5, L)
            sum_squares(pool, own, 6, L)

        def ada_copies(act, first, n):
            for m in range(first, first + n):
                act.wait_ge(sig("ada_used"), m + 1)
                if m:
                    act.wait_ge(sig("ada_summed"), m)
                act.activation(ada_sb[:], modp[:, 0:L], ACT.Copy).then_inc(sig("ada_copied"), 1)

        def act_norm(act, k, width, after=None, shift=None):
            for kt in range(KT):
                if after is not None:
                    taken(act, "lin", lin_of[after] + kt)
                act.activation(hn[:, kt, 0:width], xres[:, kt, 0:width], ACT.Square).then_inc(sig("squares"), 1)
            tile = aux_of[f"norm{k}"]
            full(act, "aux", tile)
            n = width // P
            frees(act.activation(rcol[:, 0:n], aux[:, tile % AUX, 0:n], ACT.Sqrt, scale=1.0 / D, bias=eps[:]), "aux",
                  tile)
            if shift is not None:
                layer, chunk, nth = shift
                for kt in range(KT):
                    act.wait_ge(sig("scaled"), KT * nth + kt + 1)
                    for s in range(width // L):
                        cols = hn[:, kt, s * L:(s + 1) * L]
                        ins = act.activation(cols, cols, ACT.Identity,
                                             bias=mod[:, layer, chunk * KT + kt, s:s + 1])
                    ins.then_inc(sig("hn_ready"), 1)

        def softmax_exps(act, own, layer, logits, stats, sinks):
            act.wait_ge(sig(f"maxima{layer}"), 1)
            for qt in range(QT):
                for h in range(8):
                    ins = act.activation(logits[qt][:, h, :], logits[qt][:, h, :], ACT.Exp,
                                         bias=stats[:, 2 + qt, h:h + 1], accum_out=stats[:, 6 + qt, h:h + 1])
            if sinks:
                own.mark(ins)
                ins = act.activation(stats[:, 8:10, :], stats[:, 4:6, :], ACT.Exp)
            ins.then_inc(sig(f"exps{layer}"), 1)

        def roots(act, name, widths, scale, dst):
            for n, width in enumerate(widths):
                tile = aux_of[name] + n
                full(act, "aux", tile)
                frees(act.activation(dst(n), aux[:, tile % AUX, 0:width], ACT.Sqrt, scale=scale, bias=eps[:]),
                      "aux", tile)

        def copies(act, name, n, src, dst):
            for m in range(n):
                tile = aux_of[name] + m
                full(act, "aux", tile)
                frees(act.activation(dst(m), src(aux[:, tile % AUX]), ACT.Copy), "aux", tile)

        def ffn_scalar(act, n, width):
            tile0 = lin_of[f"ffn{n}_in"]

            def gate(i, k):
                tile = tile0 + 2 * k
                full(act, "lin", tile, i * 2 * RING)
                if not isinstance(i, int) or i > 0:
                    taken(act, "lin", tile + 1, (i - 1) * 2)
                frees(act.activation(silu_g[:, k, 0:width], lin[:, tile % RING, 0:width], ACT.Silu), "lin", tile)

            rounds(act, FT, gate)


        def second_block_scalar(act, own):
            act_norm(act, 2, 2 * L, "od_out", (0, 0, 0))
            into = [k2[:, n] for n in range(2)] + [v2[:, n] for n in range(2)] + [q2[:, n] for n in range(8)]
            for n, dst in enumerate(into):
                tile = lin_of["qkv"] + n
                full(act, "lin", tile)
                frees(act.activation(dst, lin[:, tile % RING, :], ACT.Copy), "lin", tile)
            copies(act, "v_tok2", 2, lambda ps: ps,
                   lambda n: v_tok2[:, 2 * n:2 * n + 2, :].rearrange("p a b -> p (a b)"))
            for i in range(AT_HEADS + 1):
                if i < AT_HEADS:
                    act.wait_ge(sig("maxima2"), i + 1)
                    for n, (part, cols) in enumerate(((0, slice(0, 2 * L)), (1, slice(0, 2 * L)),
                                                      (2, slice(0, L)), (2, slice(L, 2 * L)))):
                        tile = score_tile(i, part)
                        ins = act.activation(p2[:, i % 3, part, cols], aux[:, tile % AUX, cols], ACT.Exp,
                                             scale=AT_SCALE, bias=stat2[:, 1, i, n:n + 1],
                                             accum_out=stat2[:, 2, i, n:n + 1])
                        if n != 2:
                            frees(ins, "aux", tile)
                    act.activation(stat2[:, 3, i, :], stat2[:, 1, i, :], ACT.Exp, bias=nsink2[:, 0, i:i + 1])\
                        .then_inc(sig("exps2"), 1)
                if i >= 1:
                    h = i - 1
                    for n in range(3):
                        tile = turned_tile(h, n)
                        full(act, "aux", tile)
                        if n == 0 and h >= 2:
                            head_done(act, "attn", h - 2)
                        frees(act.activation(pt2[:, h % 2, n, :], aux[:, tile % AUX, :], ACT.Copy), "aux", tile)
            act_norm(act, 3, 2 * L, "w_o", (0, 3, 1))
            ffn_scalar(act, 0, 2 * L)
            act_norm(act, 4, 2 * L, "ffn0_out", (1, 0, 2))
            act.wait_ge(sig("dt_abs"), 1)
            own.link(act.activation(dt_tmp, dt_tmp, ACT.Exp, scale=-1.0))
            own.mark(act.activation(dt_tmp2, dt_tmp, ACT.Ln, bias=ones[0:64, 0:1]))
            act.activation(a_neg, dt_cols[:, 1:2], ACT.Exp).then_inc(sig("dt_exp"), 1)
            act.wait_ge(sig("dt_summed"), 1)
            act.activation(dt_tmp[:, L:2 * L], dt_tmp[:, L:2 * L], ACT.Exp, scale=-1.0, bias=tot[:, 1:2])\
                .then_inc(sig("dt_weights"), 1)
            for n in range(48):
                tile = lin_of["ssm_in"] + n
                if n < 32:
                    taken(act, "lin", tile)
                    dst = bm[:, n, :] if n < 8 else xs_pair[:, n - 8] if n < 24 else cm[:, n - 24, :]
                    act.activation(dst, dst, ACT.Silu).then_inc(sig("convolved"), 1)
                else:
                    full(act, "lin", tile)
                    frees(act.activation(zs[:, n - 32, :], lin[:, tile % RING, 0:L], ACT.Silu), "lin", tile)
            copies(act, "ssm_rows", 1, lambda ps: ps[:, 0:6 * 64], lambda n: cols_g.rearrange("p a b c -> p (a b c)"))
            turned_copies(act, "bc_tok", 4, bc_tok, 2, 0, act.activation)
            turned_copies(act, "xc_tok", 8, xc_tok, 4, 0, act.activation)
            for g in range(GROUPS):
                tile = aux_of["states"] + g
                full(act, "aux", tile)
                frees(act.activation(state[:, g].rearrange("p a b -> p (a b)"), aux[:, tile % AUX, :], ACT.Copy),
                      "aux", tile)
            turned_copies(act, "x_tok", 8, x_tok, 4, 0, act.activation)
            for h in range(M_HEADS):
                act.wait_ge(sig("gaps"), h + 1)
                act.activation(decay[:, h % 2], decay[:, h % 2], ACT.Exp).then_inc(sig("decays"), 1)
                if h >= 2:
                    head_done(act, "ssm_y", h - 2)
                tile = bc_tile(h)
                frees(act.activation(from_start[:, h % 2].rearrange("p a b -> p (a b)"), aux[:, tile % AUX, :],
                                     ACT.Exp), "aux", tile)
            act.wait_ge(sig("y_gated"), 1)
            act.activation(y_sq, ys, ACT.Square).then_inc(sig("y_squares"), 1)
            roots(act, "y_norm", [2 * L] * 4, 1.0 / L,
                  lambda n: y_rs[:, 2 * n:2 * n + 2, :].rearrange("p a b -> p (a b)"))
            act_norm(act, 5, L, "ssm_out", (1, 3, 3))
            ffn_scalar(act, 1, L)
            act_norm(act, 6, L, "ffn1_out")

        def turned_copies(eng, name, n, dst, per_row, parity, copy):
            for q in range(parity, n, 2):
                tile = aux_of[name] + q
                full(eng, "aux", tile)
                out, src = dst[:, q // per_row, (q % per_row) * 2 * L:(q % per_row + 1) * 2 * L], aux[:, tile % AUX, :]
                frees(copy(out, src, ACT.Copy) if parity == 0 else copy(out, src), "aux", tile)

        def normed(dve, k, width, a, shifted=False):
            tile = aux_of[f"norm{k}"]
            taken(dve, "aux", tile)
            dve.reciprocal(rcol[:, 0:width // P], rcol[:, 0:width // P]).then_inc(sig("rms"), 1)
            full(dve, "aux", tile + 1)
            for kt in range(KT):
                for s in range(width // L):
                    cols = slice(s * L, (s + 1) * L)
                    ins = dve.scalar_tensor_tensor(
                        out=hn[:, kt, cols], in0=xres[:, kt, cols], scalar=a(kt, s),
                        in1=aux[:, (tile + 1) % AUX, cols], op0=ALU.mult, op1=ALU.mult)
                ins.then_inc(sig("scaled" if shifted else "hn_ready"), 1)
            frees(dve.tensor_copy(rcol[:, 0:1], rcol[:, 0:1]), "aux", tile + 1)

        def maxima(dve, own, layer, logits, stats, sinks):
            own.settle()
            own.mark(dve.tensor_reduce(stats[:, 0, :], logits[0], AX_X, ALU.max))
            own.link(dve.tensor_reduce(stats[:, 1, :], logits[1], AX_X, ALU.max))
            if sinks is not None:
                own.link(dve.tensor_tensor(stats[:, 0:2, :], stats[:, 0:2, :], twice(sinks), ALU.max))
            ins = dve.tensor_scalar(stats[:, 2:4, :], stats[:, 0:2, :], -1.0, None, ALU.mult)
            if sinks is not None:
                own.link(ins)
                ins = dve.tensor_tensor(stats[:, 4:6, :], stats[:, 2:4, :], twice(sinks), ALU.add)
            ins.then_inc(sig(f"maxima{layer}"), 1)

        def probabilities(dve, own, layer, logits, stats, sinks):
            dve.wait_ge(sig(f"exps{layer}"), 1)
            if sinks:
                own.link(dve.tensor_tensor(stats[:, 6:8, :], stats[:, 6:8, :], stats[:, 8:10, :], ALU.add))
            own.link(dve.reciprocal(stats[:, 10:12, :], stats[:, 6:8, :]))
            own.mark(dve.tensor_tensor(logits[0], logits[0], each(stats[:, 10, :], P), ALU.mult))
            dve.tensor_tensor(logits[1], logits[1], each(stats[:, 11, :], L), ALU.mult)\
                .then_inc(sig(f"probs{layer}"), 1)

        def scaled_logits(dve, own, layer, bias, logits, scale):
            for n in range(6):
                tile = aux_of[f"scores{layer}"] + n
                full(dve, "aux", tile)
                if n < 2:
                    heads = slice(4 * n, 4 * n + 4)
                    out, add = logits[0][:, heads, :], bias[:, heads, P:L]
                else:
                    heads = slice(2 * (n - 2), 2 * (n - 2) + 2)
                    out, add = logits[1][:, heads, :], bias[:, heads, :]
                frees(dve.scalar_tensor_tensor(
                    out=out, in0=aux[:, tile % AUX].rearrange("p (a b) -> p a b", a=out.shape[1]), scalar=scale,
                    in1=add, op0=ALU.mult, op1=ALU.add), "aux", tile)
            for n in range(3, 6):
                taken(dve, "aux", aux_of[f"scores{layer}"] + n)

        def gated_add(dve, own, name, layer, chunk, parts):
            for n in range(KT):
                tile = lin_of[name] + n
                full(dve, "lin", tile)
                for s in range(parts):
                    cols = slice(s * L, (s + 1) * L)
                    ins = dve.scalar_tensor_tensor(
                        out=xres[:, n, cols], in0=lin[:, tile % RING, cols],
                        scalar=mod[:, layer, chunk * KT + n, s:s + 1], in1=xres[:, n, cols], op0=ALU.mult, op1=ALU.add)
                frees(ins, "lin", tile)
            for n in range(RING):
                taken(dve, "lin", lin_of[name] + KT - 1 - n)

        def modulated(dve, own, k, width, layer, chunk):
            own.link(dve.scalar_tensor_tensor(
                out=a_col[:], in0=mod[:, layer, (chunk + 1) * KT:(chunk + 2) * KT, :], scalar=1.0,
                in1=each(g2[:, k - 2, :], 2), op0=ALU.add, op1=ALU.mult))
            normed(dve, k, width, lambda kt, s: a_col[:, kt, s:s + 1], True)

        def ffn_vector(dve, n, width):
            tile0 = lin_of[f"ffn{n}_in"]

            def up(i, k):
                tile = tile0 + 2 * k + 1
                full(dve, "lin", tile, i * 2 * RING)
                taken(dve, "lin", tile - 1, i * 2)
                dst = hid[:, i * RING + k, 0:width] if isinstance(i, int) else \
                    hid[:, bass.ds(i * RING + k, 1), 0:width].rearrange("p a b -> p (a b)")
                frees(dve.tensor_tensor(dst, lin[:, tile % RING, 0:width], silu_g[:, k, 0:width], ALU.mult), "lin", tile)

            rounds(dve, FT, up)

        def convolve(dve, own, n):
            tile = lin_of["ssm_in"] + n
            full(dve, "lin", tile)
            if n < 8:
                dst = bm[:, n, :].rearrange("p (a b) -> p a b", a=2)
            elif n < 24:
                dst = xs_pair[:, n - 8]
            else:
                dst = cm[:, n - 24, :].unsqueeze(1)
            src = lin[:, tile % RING, 0:L * dst.shape[1]].rearrange("p (a b) -> p a b", b=L)
            w = lambda m: conv_w[:, n, m:m + 1]
            own.link(dve.tensor_scalar(dst, src, w(1), w(3), ALU.mult, ALU.add))
            own.link(dve.scalar_tensor_tensor(out=dst[:, :, 1:L], in0=src[:, :, 0:L - 1], scalar=w(0),
                                              in1=dst[:, :, 1:L], op0=ALU.mult, op1=ALU.add))
            frees(dve.scalar_tensor_tensor(out=dst[:, :, 0:L - 1], in0=src[:, :, 1:L], scalar=w(2),
                                           in1=dst[:, :, 0:L - 1], op0=ALU.mult, op1=ALU.add), "lin", tile)

        def second_block_vector(dve, own):
            tt, ts, stt = dve.tensor_tensor, dve.tensor_scalar, dve.scalar_tensor_tensor
            dve.wait_ge(sig("ada_summed"), 48)
            own.link(tt(mod[:].rearrange("p a b c -> p (a b) c"), modp[:, L:L + 192].rearrange("p (a b) -> p a b", b=2),
                        each(modb[:].rearrange("p a b -> p (a b)"), 2), ALU.add))
            own.mark(dve.tensor_copy(nsink2[:, 0, :], nsink2_in[:]))
            own.mark(ts(nsink2[:, 1, :], nsink2_in[:], -1.0, None, ALU.mult))
            modulated(dve, own, 2, 2 * L, 0, 0)
            dve.wait_ge(sig("at_in"), 48)
            own.mark(dve.tensor_copy(ident_b, ident[:]))
            dve.tensor_copy(mask_b2, mask2).then_inc(sig("masks2"), 1)
            for n in (0, 1, 2, 3, 4):
                tile = aux_of["rope"] + n
                part = (k2 if n == 0 else q2[:, 2 * n - 2:2 * n])[:, :, 0:L]
                full(dve, "aux", tile)
                frees(tt(rope_tmp, aux[:, tile % AUX].rearrange("p (a b) -> p a b", a=2), twice(rope_cs[:, 1, :]),
                         ALU.mult), "aux", tile)
                own.link(tt(part, part, twice(rope_cs[:, 0, :]), ALU.mult))
                taken(dve, "aux", tile)
                own.link(tt(part, part, rope_tmp, ALU.add))
            dve.sem_inc(sig("roped"), 1)
            for i in range(AT_HEADS + 3):
                if i < AT_HEADS:
                    for n in range(3):
                        tile = score_tile(i, n)
                        full(dve, "aux", tile)
                        if n < 2:
                            own.mark(dve.tensor_reduce(stat2[:, 0, i, n:n + 1], aux[:, tile % AUX, :], AX_X, ALU.max))
                        else:
                            own.link(dve.tensor_reduce(
                                stat2[:, 0, i, 2:4], aux[:, tile % AUX].rearrange("p (a b) -> p a b", a=2), AX_X, ALU.max))
                    ts(stat2[:, 1, i, :], stat2[:, 0, i, :], -AT_SCALE, nsink2[:, 1, i:i + 1], ALU.mult, ALU.min)\
                        .then_inc(sig("maxima2"), 1)
                if 1 <= i <= AT_HEADS:
                    h = i - 1
                    dve.wait_ge(sig("exps2"), h + 1)
                    own.link(tt(stat2[:, 4, h, :], stat2[:, 2, h, :], stat2[:, 3, h, :], ALU.add))
                    own.link(dve.reciprocal(stat2[:, 5, h, :], stat2[:, 4, h, :]))
                    for n, (part, cols) in enumerate(((0, slice(0, 2 * L)), (1, slice(0, 2 * L)),
                                                      (2, slice(0, L)), (2, slice(L, 2 * L)))):
                        p = p2[:, h % 3, part, cols]
                        ins = ts(p, p, stat2[:, 5, h, n:n + 1], None, ALU.mult)
                    ins.then_inc(sig("probs2"), 1)
                if i >= 4 and i % 2 == 0:
                    n = i // 2 - 2
                    tile = lin_of["attn"] + n
                    full(dve, "lin", tile)
                    frees(dve.tensor_copy(q2[:, n, :], lin[:, tile % RING, :]), "lin", tile)
            gated_add(dve, own, "w_o", 0, 2, 2)
            modulated(dve, own, 3, 2 * L, 0, 3)
            ffn_vector(dve, 0, 2 * L)
            gated_add(dve, own, "ffn0_out", 0, 5, 2)
            modulated(dve, own, 4, 2 * L, 1, 0)
            tile = lin_of["ssm_dt"]
            full(dve, "lin", tile)
            frees(ts(dt2, lin[0:64, tile % RING, :], dt_cols[:, 0:1], None, ALU.add), "lin", tile)
            taken(dve, "lin", tile)
            stt(out=dt_tmp, in0=dt2, scalar=-1.0, in1=dt2, op0=ALU.mult, op1=ALU.max).then_inc(sig("dt_abs"), 1)
            dve.wait_ge(sig("dt_exp"), 1)
            own.mark(ts(dt2, dt2, 0.0, None, ALU.max))
            own.link(ts(da, dt_tmp, 1.0, None, ALU.add))
            own.mark(tt(dt2, dt2, dt_tmp2, ALU.add))
            own.link(ts(dt_tmp3, da, 1.0, None, ALU.subtract))
            own.link(tt(dt_tmp, dt_tmp, dt_tmp3, ALU.subtract))
            own.link(dve.reciprocal(da, da))
            own.link(tt(da, da, dt_tmp, ALU.mult))
            own.link(tt(dt2, dt2, da, ALU.add))
            own.link(ts(da, dt2, a_neg, -1.0, ALU.mult, ALU.mult))
            one = ones[0:64, 0:1].to_broadcast([64, L])
            own.mark(dve.tensor_tensor_scan(rows_g[0:64], one, da[:, 0:L], 0.0, ALU.mult, ALU.add))
            own.link(dve.tensor_tensor_scan(dt_tmp[:, L:2 * L], one, da[:, L:2 * L], 0.0, ALU.mult, ALU.add))
            own.mark(dve.tensor_copy(tot[:, 0:1], rows_g[0:64, L - 1:L]))
            own.link(dve.tensor_copy(tot[:, 1:2], dt_tmp[:, 2 * L - 1:2 * L]))
            back = slice(32, 64)
            own.mark(ts(rows_g[back], rows_g[back], -1.0, tot[back, 0:1], ALU.mult, ALU.add))
            own.link(ts(dt_tmp[back, L:2 * L], dt_tmp[back, L:2 * L], -1.0, tot[back, 1:2], ALU.mult, ALU.add))
            own.mark(tt(rows_g[back], rows_g[back], da[back, 0:L], ALU.add))
            tt(dt_tmp[back, L:2 * L], dt_tmp[back, L:2 * L], da[back, L:2 * L], ALU.add).then_inc(sig("dt_summed"), 1)
            dve.wait_ge(sig("dt_weights"), 1)
            tt(dt2[:, L:2 * L], dt_tmp[:, L:2 * L], dt2[:, L:2 * L], ALU.mult).then_inc(sig("dt_rows"), 1)
            dve.wait_ge(sig("ssm_in"), 32)
            for n in range(32):
                convolve(dve, own, n)
            turned_copies(dve, "bc_tok", 4, bc_tok, 2, 1, dve.tensor_copy)
            turned_copies(dve, "xc_tok", 8, xc_tok, 4, 1, dve.tensor_copy)
            for n in range(AUX):
                taken(dve, "aux", aux_of["xc_tok"] + 7 - n)
            taken(dve, "aux", aux_of["ssm_rows"])
            for g in range(GROUPS):
                if g >= 1:
                    full(dve, "aux", aux_of["states"] + g - 1)
                for d in range(2):
                    for qt in range(QT):
                        heads = cols_g[:, 2, qt, d * 32 + 4 * g:d * 32 + 4 * g + 4]
                        ins = tt(xw[:, d, qt].rearrange("p (a b) -> p a b", a=4),
                                 xc_tok[:, qt, g * L:(g + 1) * L].rearrange("p (a b) -> p a b", a=4),
                                 each(heads, 64), ALU.mult)
                ins.then_inc(sig("x_weighted"), 1)
            turned_copies(dve, "x_tok", 8, x_tok, 4, 1, dve.tensor_copy)

            def y_out(n):
                tile = lin_of["ssm_y"] + n
                full(dve, "lin", tile)
                frees(stt(out=ys[:, n], in0=ys[:, n], scalar=ssm_cols[:, 0, n:n + 1], in1=lin[:, tile % RING, 0:L],
                          op0=ALU.mult, op1=ALU.add), "lin", tile)
                taken(dve, "lin", tile)
                return tt(ys[:, n], ys[:, n], zs[:, n], ALU.mult)

            parts = ((0, 0, 0, L, 0), (0, 1, P, L, L), (1, 0, 0, P, 3 * P), (1, 1, 0, L, 4 * P))
            for h in range(M_HEADS + 1):
                if h < M_HEADS:
                    g = h // 4
                    if h % 4 == 0:
                        tile = cb_tile(g)
                        full(dve, "aux", tile)
                        c, pb_ = cb[:, g % 2], aux[:, tile % AUX]
                        if g == 0:
                            for n in range(AUX):
                                taken(dve, "aux", aux_of["states"] + GROUPS - 1 - n)
                        own.mark(tt(c[:, 0:P], pb_[:, 0:P], tri[:, 0], ALU.mult))
                        own.mark(dve.tensor_copy(c[:, P:L], pb_[:, P:L]))
                        own.mark(tt(c[:, L:3 * P], pb_[:, 3 * P:4 * P], tri[:, 0], ALU.mult))
                        own.mark(tt(c[:, 3 * P:4 * P], pb_[:, 0:P], tri[:, 1], ALU.mult))
                        own.mark(dve.tensor_copy(c[:, 4 * P:5 * P], pb_[:, L:3 * P]))
                        frees(tt(c[:, 5 * P:6 * P], pb_[:, 3 * P:4 * P], tri[:, 1], ALU.mult), "aux", tile)
                    tile = bc_tile(h)
                    full(dve, "aux", tile)
                    if h >= 2:
                        head_done(dve, "ssm_y", h - 2)
                    for d, qt, lo_, hi_, at in parts:
                        ins = ts(decay[:, h % 2, at:at + hi_ - lo_], aux[:, tile % AUX, d * L + lo_:d * L + hi_],
                                 cols_g[:, 0, qt, d * 32 + h:d * 32 + h + 1], 0.0, ALU.subtract, ALU.min)
                    ins.then_inc(sig("gaps"), 1)
                if h >= 1:
                    q = h - 1
                    taken(dve, "aux", cb_tile(q // 4))
                    dve.wait_ge(sig("decays"), q + 1)
                    for d, qt, lo_, hi_, at in parts:
                        m = decay[:, q % 2, at:at + hi_ - lo_]
                        ins = stt(out=m, in0=m, scalar=cols_g[:, 1, qt, d * 32 + q:d * 32 + q + 1],
                                  in1=cb[:, (q // 4) % 2, at:at + hi_ - lo_], op0=ALU.mult, op1=ALU.mult)
                    ins.then_inc(sig("mixed"), 1)
                if h >= 3 and h % 2 == 1:
                    y_out((h - 3) // 2)
            y_out(DT_ - 1).then_inc(sig("y_gated"), 1)
            for n in range(3):
                taken(dve, "aux", aux_of["y_norm"] + 3 - n)
            own.link(dve.reciprocal(y_rs, y_rs))
            for n in range(DT_):
                ins = stt(out=ys[:, n], in0=ys[:, n], scalar=ssm_cols[:, 1, n:n + 1], in1=y_rs[:, n // 2],
                          op0=ALU.mult, op1=ALU.mult)
            ins.then_inc(sig("y_normed"), 1)
            gated_add(dve, own, "ssm_out", 1, 2, 1)
            modulated(dve, own, 5, L, 1, 3)
            ffn_vector(dve, 1, L)
            gated_add(dve, own, "ffn1_out", 1, 5, 1)
            normed(dve, 6, L, lambda kt, s: g2[:, 4, kt:kt + 1])

        @block.scalar
        def _(act):
            own = Count(act, sig("act_own"))
            act.dma_start(ident[:], t["ident"]).then_inc(sig("norm_in"), 16)
            act.dma_start(gcol[:], t["gcol"]).then_inc(sig("norm_in"), 16)
            copies(act, "bias", EV_HEADS, lambda ps: ps[:, 0:3 * P], lambda h: table[:, h, :])
            act.wait_ge(sig("x_in"), 16)
            act.wait_ge(sig("made"), 1)
            act_norm(act, 0, L)
            act.wait_ge(sig("s5_in"), 32)
            act.activation(par[:, 3, :], par[:, 0, :], ACT.Exp).then_inc(sig("s5_dt"), 1)
            act.wait_ge(sig("s5_phase"), 1)
            own.mark(act.activation(par[:, 8, :], par[:, 4, :], ACT.Exp))
            own.mark(act.activation(par[:, 9, :], par[:, 6, :], ACT.Sin))
            act.activation(par[:, 10, :], par[:, 7, :], ACT.Sin, scale=-1.0, bias=half_pi[:])\
                .then_inc(sig("s5_trig"), 1)
            into = [u[:, n] for n in range(4)] + [ka, va] + [qa[:, n] for n in range(4)] + \
                [gate_a[:, n] for n in range(4)] + [gate_b[:, n] for n in range(4)]
            for n, dst in enumerate(into):
                tile = lin_of["ev_in"] + n
                full(act, "lin", tile)
                frees(act.activation(dst, lin[:, tile % RING, 0:L], ACT.Silu if n >= 10 else ACT.Copy), "lin", tile)
                if 2 <= n < 10:
                    for j in range(2 * (n - 2), 2 * (n - 2) + 2):
                        act.wait_ge(sig("turns"), j + 1)
                        own.mark(act.activation(cos_t[:, j, :], cos_t[:, j, :], ACT.Sin, scale=-TWO_PI,
                                                bias=half_pi[:]))
                        act.activation(sin_t[:, j, :], sin_t[:, j, :], ACT.Sin, scale=TWO_PI * (1 - 2e-7))\
                            .then_inc(sig("phases"), 1)
            act.wait_ge(sig("const_in"), 224)
            act.activation(sc_c[:], sc_c[:], ACT.Silu).then_inc(sig("silu_c"), 1)
            copies(act, "s5_bb", 2, lambda ps: ps, lambda n: bb_t[:, n].rearrange("p a b -> p (a b)"))
            taken(act, "lin", lin_of["ev_in"] + 17)
            act.wait_ge(sig("table_out"), 16)
            own.mark(act.activation(sq0[:, 0, :], ka, ACT.Square))
            act.activation(sq0[:, 1:5, :], qa, ACT.Square).then_inc(sig("squares_qk0"), 1)
            roots(act, "qk_norm0", [2 * L, 2 * L, L], 1.0 / 64,
                  lambda n: r0[:, 2 * n:min(2 * n + 2, 5), :].rearrange("p a b -> p (a b)"))
            copies(act, "v_tok0", 1, lambda ps: ps[:, 0:L], lambda n: v_tok.rearrange("p a b -> p (a b)"))
            ada_copies(act, 0, 4)
            softmax_exps(act, own, 0, (lg0, lg1), small, True)
            copies(act, "probs0", EV_HEADS, lambda ps: ps[:, 0:3 * P], lambda h: pt[:, h, :])
            ada_copies(act, 4, 20)
            taken(act, "lin", lin_of["s5_y"] + 3)
            act.activation(u, u, ACT.Gelu_apprx_tanh).then_inc(sig("s5_gelu"), 1)
            for n in range(4):
                tile = lin_of["glu"] + 2 * n + 1
                full(act, "lin", tile)
                frees(act.activation(qa[:, n], lin[:, tile % RING, 0:L], ACT.Sigmoid, bias=glu_b[:, 4 + n:5 + n]),
                      "lin", tile)
            act_norm(act, 1, L, "ev_out")
            into = [ki] + [qi[:, n] for n in range(4)] + [k1[:, n] for n in range(2)] + \
                [v1[:, n] for n in range(2)] + [q1[:, n] for n in range(8)] + [gate1[:, n] for n in range(8)]
            for n, dst in enumerate(into):
                tile = lin_of["od_ki"] + n
                full(act, "lin", tile)
                frees(act.activation(dst, lin[:, tile % RING, 0:L], ACT.Silu if n >= 17 else ACT.Copy), "lin", tile)
                if n >= 6 and n % 2 == 0 and (n - 6) // 2 < 6:
                    m = (n - 6) // 2
                    tile = aux_of["index"] + m
                    full(act, "aux", tile)
                    if m >= 2:
                        act.wait_ge(sig("rel_used"), m - 1)
                    frees(act.activation(rel[:, m % 2], aux[:, tile % AUX], ACT.Relu, scale=64 ** -0.5), "aux", tile)
            taken(act, "lin", lin_of["od_in"] + 23)
            own.mark(act.activation(sq1[:, 0:2, :], k1, ACT.Square))
            act.activation(sq1[:, 2:10, :], q1, ACT.Square).then_inc(sig("squares_qk1"), 1)
            roots(act, "kq_norm1", [2 * L] * 5, 1.0 / P,
                  lambda n: r1[:, 2 * n:2 * n + 2, :].rearrange("p a b -> p (a b)"))
            copies(act, "v_tok1", 1, lambda ps: ps, lambda n: v_tok1.rearrange("p a b -> p (a b)"))
            ada_copies(act, 24, 24)
            softmax_exps(act, own, 1, (lh0, lh1), small, False)
            copies(act, "probs1", OD_HEADS, lambda ps: ps[:, 0:3 * P], lambda h: pt1[:, h, :])
            second_block_scalar(act, own)

        @block.vector
        def _(dve):
            own = Count(dve, sig("dve_own"))
            tt, ts, stt = dve.tensor_tensor, dve.tensor_scalar, dve.scalar_tensor_tensor
            dve.wait_ge(sig("norm_in"), 32)
            normed(dve, 0, L, lambda kt, s: gcol[:, 0, kt:kt + 1])
            dve.wait_ge(sig("const_in"), 224)
            (log_dt, a_re, a_im, dt, z, turn, phase, phase_abs, mag, sin1, cos1, hi, lo, k, den, n_re, n_im,
             f_re, f_im, tmp, tmp2) = (par[:, n, :] for n in range(21))
            dve.wait_ge(sig("s5_dt"), 1)
            own.mark(tt(z, a_re, dt, ALU.mult))
            own.link(tt(phase, a_im, dt, ALU.mult))
            own.link(ts(k, phase, 1.0 / TWO_PI, ROUND, ALU.mult, ALU.add))
            own.link(ts(k, k, ROUND, None, ALU.subtract))
            for part in (PI2_A, PI2_B, PI2_C):
                own.link(stt(out=phase, in0=k, scalar=-part, in1=phase, op0=ALU.mult, op1=ALU.add))
            own.link(ts(phase, phase, math.pi * (1 - 1e-7), -math.pi * (1 - 1e-7), ALU.min, ALU.max))
            own.link(ts(turn, phase, 1.0 / TWO_PI, None, ALU.mult))
            stt(out=phase_abs, in0=phase, scalar=-1.0, in1=phase, op0=ALU.mult, op1=ALU.max).then_inc(sig("s5_phase"), 1)
            own.link(ts(tmp, turn, 4097.0, None, ALU.mult))
            own.link(tt(tmp2, tmp, turn, ALU.subtract))
            own.link(tt(hi, tmp, tmp2, ALU.subtract))
            own.link(tt(lo, turn, hi, ALU.subtract))
            for j in range(SSM_TILES):
                frac, whole = sin_t[:, j, :], cos_t[:, j, :]
                own.link(ts(frac, steps, hi[:, j:j + 1], None, ALU.mult))
                own.link(ts(whole, frac, ROUND, ROUND, ALU.add, ALU.subtract))
                own.link(tt(frac, frac, whole, ALU.subtract))
                own.link(stt(out=frac, in0=steps, scalar=lo[:, j:j + 1], in1=frac, op0=ALU.mult, op1=ALU.add))
                own.link(ts(whole, frac, ROUND, ROUND, ALU.add, ALU.subtract))
                own.link(tt(frac, frac, whole, ALU.subtract))
                stt(out=whole, in0=frac, scalar=-1.0, in1=frac, op0=ALU.mult, op1=ALU.max).then_inc(sig("turns"), 1)
            dve.wait_ge(sig("s5_trig"), 1)
            own.mark(tt(n_re, mag, cos1, ALU.mult))
            own.mark(tt(n_im, mag, sin1, ALU.mult))
            own.mark(tt(den, a_re, a_re, ALU.mult))
            own.link(tt(tmp, a_im, a_im, ALU.mult))
            own.mark(ts(n_re, n_re, 1.0, None, ALU.subtract))
            own.link(tt(den, den, tmp, ALU.add))
            own.mark(dve.reciprocal(den, den))
            own.mark(tt(f_re, n_re, a_re, ALU.mult))
            own.mark(tt(tmp, n_im, a_im, ALU.mult))
            own.mark(tt(f_im, n_im, a_re, ALU.mult))
            own.link(tt(tmp2, n_re, a_im, ALU.mult))
            own.mark(tt(f_re, f_re, tmp, ALU.add))
            own.link(tt(f_im, f_im, tmp2, ALU.subtract))
            own.mark(tt(f_re, f_re, den, ALU.mult))
            own.link(tt(f_im, f_im, den, ALU.mult))
            bt = s5w[:, 0].rearrange("p a b -> p (a b)")[:, 0:256].rearrange("p (a b) -> p a b", a=16)
            for part, (f1, b1, f2, b2, op) in enumerate(((f_re, 0, f_im, 1, ALU.subtract), (f_re, 1, f_im, 0, ALU.add))):
                s5p = s5t[:, part, 0:256].rearrange("p (a b) -> p a b", a=16)
                own.mark(tt(bt, each(f1, 16), b_in[:, b1], ALU.mult))
                own.link(tt(s5p, each(f2, 16), b_in[:, b2], ALU.mult))
                for n in range(2):
                    rows = slice(64 * n, 64 * n + 64)
                    own.link(tt(bd[rows, part, :, 16 * n:16 * n + 16], bt[rows], s5p[rows], op))
            dve.wait_ge(sig("c_in"), 64)
            ts(c_bd[:, 1], c_bd[:, 1], -1.0, None, ALU.mult).then_inc(sig("bd_ready"), 1)
            dve.wait_ge(sig("table_back"), 16)
            own.link(tt(bias_a, bias_b, mask_a.unsqueeze(1).to_broadcast([P, EV_HEADS, L]), ALU.add))
            own.link(tt(bias_b, bias_b, mask_b.unsqueeze(1).to_broadcast([P, EV_HEADS, L]), ALU.add))
            taken(dve, "aux", aux_of["qk_norm0"] + 2)
            own.link(dve.reciprocal(r0, r0))
            stt(out=ka, in0=ka, scalar=qk_g[:, 1:2], in1=r0[:, 0, :], op0=ALU.mult, op1=ALU.mult)
            stt(out=qa, in0=qa, scalar=qk_g[:, 0:1], in1=r0[:, 1:5, :], op0=ALU.mult, op1=ALU.mult)\
                .then_inc(sig("qk0_ready"), 1)
            scaled_logits(dve, own, 0, bias_a, (lg0, lg1), 64 ** -0.5)
            maxima(dve, own, 0, (lg0, lg1), small, sink[:])
            probabilities(dve, own, 0, (lg0, lg1), small, True)
            for n in range(4):
                tile = aux_of["out0"] + n
                full(dve, "aux", tile)
                frees(tt(cat[:, n, :], aux[:, tile % AUX, 0:L], gate_a[:, n, :], ALU.mult), "aux", tile)

            dve.wait_ge(sig("phases"), SSM_TILES)
            for j in range(SSM_TILES):
                p = j % 2
                tile = aux_of["s5_bu"] + j
                bu = aux[:, tile % AUX].rearrange("p (a b) -> p a b", a=2)
                w, ti, z2 = s5w[:, p], s5t[:, p].rearrange("p (a b) -> p a b", a=2), s5z[:, p]
                full(dve, "aux", tile)
                own.mark(tt(w, bu, twice(cos_t[:, j, :]), ALU.mult))
                frees(tt(ti, bu, twice(sin_t[:, j, :]), ALU.mult), "aux", tile)
                taken(dve, "aux", tile)
                own.mark(tt(w[:, 0], w[:, 0], ti[:, 1], ALU.add))
                own.link(tt(w[:, 1], w[:, 1], ti[:, 0], ALU.subtract))
                if j >= 2:
                    dve.wait_ge(sig("x_states"), j - 1)
                decay = mag[:, j:j + 1].to_broadcast([P, L])
                own.mark(dve.tensor_tensor_scan(z2[:, 0], decay, w[:, 0], 0.0, ALU.mult, ALU.add))
                dve.tensor_tensor_scan(z2[:, 1], decay, w[:, 1], 0.0, ALU.mult, ALU.add)\
                    .then_inc(sig("z_ready"), 1)
            for n in range(4):
                tile = lin_of["s5_y"] + n
                dve.wait_ge(sig("s5_used"), 4 * (n + 1))
                frees(stt(out=u[:, n], in0=u[:, n], scalar=d_col[:, n:n + 1], in1=lin[:, tile % RING, 0:L],
                          op0=ALU.mult, op1=ALU.add), "lin", tile)
                taken(dve, "lin", tile)
            for n in range(4):
                tile = lin_of["glu"] + 2 * n
                full(dve, "lin", tile)
                taken(dve, "lin", tile + 1)
                frees(stt(out=qa[:, n], in0=lin[:, tile % RING, 0:L], scalar=glu_b[:, n:n + 1], in1=qa[:, n],
                          op0=ALU.add, op1=ALU.mult), "lin", tile)
                taken(dve, "lin", tile)
                tt(cat[:, 4 + n, :], qa[:, n], gate_b[:, n], ALU.mult).then_inc(sig("cat_ready"), 1)

            def add_to_x(name):
                for n in range(KT):
                    tile = lin_of[name] + n
                    full(dve, "lin", tile)
                    frees(tt(xres[:, n, 0:L], lin[:, tile % RING, 0:L], xres[:, n, 0:L], ALU.add), "lin", tile)
                    taken(dve, "lin", tile)

            add_to_x("ev_out")
            normed(dve, 1, L, lambda kt, s: gcol[:, 1, kt:kt + 1])
            tile = aux_of["wi"]
            full(dve, "aux", tile)
            frees(ts(wi, aux[:, tile % AUX, 0:16].rearrange("p (a b) -> p a b", a=2), OD_HEADS ** -0.5, None,
                     ALU.mult), "aux", tile)
            taken(dve, "aux", tile)
            own.mark(dve.tensor_copy(idx[:, 0, 0:P], mask_b[:, P:L]))
            own.link(dve.tensor_copy(idx[:, 1, :], mask_b))
            for m in range(6):
                taken(dve, "aux", aux_of["index"] + m)
                qt, heads, width = index_heads(m)
                for n, h in enumerate(heads):
                    ins = stt(out=idx[:, qt, 0:width], in0=rel[:, m % 2, n * width:(n + 1) * width],
                              scalar=wi[:, qt, h:h + 1], in1=idx[:, qt, 0:width], op0=ALU.mult, op1=ALU.add)
                    if n < len(heads) - 1:
                        own.link(ins)
                ins.then_inc(sig("rel_used"), 1)
                dve.wait_ge(sig("rel_used"), m + 1)
            for r in range(TOPK // 8):
                for qt, width in ((0, P), (1, L)):
                    own.mark(dve.max(top[:, qt, :], idx[:, qt, 0:width]))
                own.settle()
                for qt, width in ((0, P), (1, L)):
                    own.mark(dve.match_replace(idx[:, qt, 0:width], top[:, qt, :], idx[:, qt, 0:width], TAKEN))
                own.settle()
            for qt, width in ((0, P), (1, L)):
                own.mark(ts(sel[:, qt, 0:width], idx[:, qt, 0:width], TAKEN / 2, NEG, ALU.is_gt, ALU.mult))
            taken(dve, "aux", aux_of["kq_norm1"] + 4)
            own.link(dve.reciprocal(r1, r1))
            stt(out=k1, in0=k1, scalar=qk_g[:, 3:4], in1=r1[:, 0:2, :], op0=ALU.mult, op1=ALU.mult)
            stt(out=q1, in0=q1, scalar=qk_g[:, 2:3], in1=r1[:, 2:10, :], op0=ALU.mult, op1=ALU.mult)\
                .then_inc(sig("qk1_ready"), 1)
            scaled_logits(dve, own, 1, bias_b, (lh0, lh1), P ** -0.5)
            own.mark(tt(lh0, lh0, sel[:, 0, 0:P].unsqueeze(1).to_broadcast([P, OD_HEADS, P]), ALU.add))
            own.link(tt(lh1, lh1, sel[:, 1, :].unsqueeze(1).to_broadcast([P, OD_HEADS, L]), ALU.add))
            maxima(dve, own, 1, (lh0, lh1), small, None)
            probabilities(dve, own, 1, (lh0, lh1), small, False)
            for n in range(8):
                tile = aux_of["out1"] + n
                full(dve, "aux", tile)
                frees(tt(q1[:, n, :], aux[:, tile % AUX, 0:L], gate1[:, n, :], ALU.mult), "aux", tile)
            add_to_x("od_out")
            second_block_vector(dve, own)

        @block.tensor
        def _(pe):
            mm = nc.tensor.matmul

            def begin(banks, tile):
                sems_, n = (lin_free, RING) if banks == "lin" else (aux_free, AUX)
                if isinstance(tile, int) and tile < n:
                    return
                pe.wait_ge(sems_[tile % n], tile // n)

            def fills(ins, banks):
                ins.then_inc(sig(banks + "_full"), 1)

            def linear(name, stage, tiles, kts, rhs, width=L, m=P, between=None, norm=None):
                count = dict((x, y) for x, y, _ in STREAM)[name]
                first, tile0 = block_of[name], lin_of[stage]

                def one(i, k):
                    b = first + k
                    pe.wait_ge(w_in[b % RING], (i + (b // RING + 1)) * 16)
                    for j in range(tiles):
                        tile = tile0 + k * tiles + j
                        bank = tile % RING
                        if not isinstance(i, int) or tile + i * RING * tiles >= RING:
                            pe.wait_ge(lin_free[bank], i * tiles + tile // RING)
                        for kt in range(kts):
                            at = (j * kts + kt) * m
                            if norm is not None and isinstance(i, int) and i == k == j == 0:
                                pe.wait_ge(sig("hn_ready"), KT * norm + kt + 1)
                            ins = mm(lin[0:m, bank, 0:width], ring[:, b % RING, at:at + m], rhs(kt),
                                     start=kt == 0, stop=kt == kts - 1)
                        fills(ins, "lin")
                    if between is not None:
                        between(k + RING * i)

                if between is not None:
                    for n in range(count):
                        one(n // RING, n % RING)
                else:
                    rounds(pe, count, one)

            def ssm_linear():
                first, tile0 = block_of["ssm_in"], lin_of["ssm_in"]
                for n in range(24):
                    b = first + n
                    pe.wait_ge(w_in[b % RING], 16 * (b // RING + 1))
                    width = 2 * L if n < 12 else L
                    for j in range(2):
                        tile = tile0 + 2 * n + j
                        begin("lin", tile)
                        for kt in range(KT):
                            at = (j * KT + kt) * P
                            ins = mm(lin[:, tile % RING, 0:width], ring[:, b % RING, at:at + P], hn[:, kt, 0:width],
                                     start=kt == 0, stop=kt == KT - 1)
                        fills(ins, "lin")

            ada_at = [0]

            def ada_groups(n):
                pe.wait_ge(sig("ada_copied"), n + 1)
                for j in range(2):
                    at = L + (2 * n + j) * 2
                    ins = mm(modp[:, at:at + 2], ada_sb[:, j * P:(j + 1) * P], group_sum[:], start=True, stop=True)
                ins.then_inc(sig("ada_summed"), 1)

            def ada(blocks):
                for n in range(ada_at[0], ada_at[0] + blocks):
                    b = block_of["ada0"] + n if n < 24 else block_of["ada1"] + n - 24
                    if n == 0:
                        pe.wait_ge(sig("silu_c"), 1)
                    else:
                        pe.wait_ge(sig("ada_copied"), n)
                    pe.wait_ge(w_in[b % RING], 16 * (b // RING + 1))
                    for kt in range(KT):
                        rows = slice(32 * (kt % 4), 32 * (kt % 4) + 32)
                        ins = mm(modp[rows, 0:L], sc_c[:, kt, :], ring[:, b % RING, kt * L:(kt + 1) * L],
                                 start=kt < 4, stop=kt >= 4)
                    ins.then_inc(sig("ada_used"), 1)
                    if n:
                        ada_groups(n - 1)
                ada_at[0] += blocks

            def sums(name, mat, src, tiles, width):
                for n, parts in enumerate(tiles):
                    tile = aux_of[name] + n
                    begin("aux", tile)
                    for m, terms in enumerate(parts):
                        for q, kt in enumerate(terms):
                            ins = mm(aux[:, tile % AUX, m * width:(m + 1) * width], mat[:], src(kt),
                                     start=q == 0, stop=q == len(terms) - 1)
                    fills(ins, "aux")

            def norm(k, width):
                tile = aux_of[f"norm{k}"]
                begin("aux", tile)
                pe.wait_ge(sig("square_sums"), k + 1)
                for n in range(width // P):
                    ins = mm(aux[:, tile % AUX, n:n + 1], hn[:, 0, n * P:(n + 1) * P], ones[:, 0:1],
                             start=True, stop=True)
                fills(ins, "aux")
                begin("aux", tile + 1)
                pe.wait_ge(sig("rms"), k + 1)
                for n in range(width // P):
                    ins = mm(aux[:, (tile + 1) % AUX, n * P:(n + 1) * P], rcol[:, n:n + 1].to_broadcast([P, P]),
                             ident[:], start=True, stop=True)
                fills(ins, "aux")

            pe.wait_ge(sig("rel_in"), 32)
            for h in range(EV_HEADS):
                tile = aux_of["bias"] + h
                begin("aux", tile)
                fills(mm(aux[:, tile % AUX, 0:3 * P], relb[:, h, :], hot, start=True, stop=True), "aux")
            pe.wait_ge(sig("made"), 1)
            pe.wait_ge(sig("norm_in"), 32)
            norm(0, L)
            linear("ev_in", "ev_in", 2, KT, lambda kt: hn[:, kt, 0:L], norm=0)
            pe.wait_ge(sig("bd_ready"), 1)
            for part in range(2):
                tile = aux_of["s5_bb"] + part
                begin("aux", tile)
                for n in range(4):
                    ins = nc.tensor.transpose(aux[:, tile % AUX, n * P:(n + 1) * P],
                                              bd[:, part, 4 * n:4 * n + 4, :].rearrange("p a b -> p (a b)"), ident[:])
                fills(ins, "aux")
            pe.wait_ge(sig("squares_qk0"), 1)
            sums("qk_norm0", pair, lambda n: sq0[:, n, :], [[[0], [1]], [[2], [3]], [[4]]], L)

            def tokens(name, src, n_src):
                tile = aux_of[name]
                begin("aux", tile)
                for qt in range(QT):
                    for n in range(n_src):
                        at = (qt * n_src + n) * P
                        ins = nc.tensor.transpose(aux[:, tile % AUX, at:at + P], src(n)[:, qt * P:(qt + 1) * P],
                                                  ident[:])
                fills(ins, "aux")

            tokens("v_tok0", lambda n: va, 1)

            def scores(layer, q, k):
                for n in range(6):
                    tile = aux_of[f"scores{layer}"] + n
                    begin("aux", tile)
                    qt, heads, width = (0, range(4 * n, 4 * n + 4), P) if n < 2 else \
                        (1, range(2 * (n - 2), 2 * (n - 2) + 2), L)
                    for m, h in enumerate(heads):
                        ins = mm(aux[:, tile % AUX, m * width:(m + 1) * width], q(h, qt), k(h)[:, 0:width],
                                 start=True, stop=True)
                    fills(ins, "aux")

            def transposed_probs(layer, logits):
                pe.wait_ge(sig(f"probs{layer}"), 1)
                for h in range(8):
                    tile = aux_of[f"probs{layer}"] + h
                    begin("aux", tile)
                    for n, src in enumerate((logits[0][:, h, :], logits[1][:, h, 0:P], logits[1][:, h, P:L])):
                        ins = nc.tensor.transpose(aux[:, tile % AUX, n * P:(n + 1) * P], src, ident[:])
                    fills(ins, "aux")

            half = lambda ap, s: ap[64 * s:64 * s + 64]
            pe.wait_ge(sig("qk0_ready"), 1)
            scores(0, lambda h, qt: half(qa[:, h % 4, qt * P:(qt + 1) * P], h // 4), lambda h: half(ka, h // 4))
            ada(4)
            transposed_probs(0, (lg0, lg1))
            for j in range(4):
                tile = aux_of["out0"] + j
                begin("aux", tile)
                for s in range(2):
                    h = j + 4 * s
                    taken(pe, "aux", aux_of["probs0"] + h)
                    rows = slice(64 * s, 64 * s + 64)
                    mm(aux[rows, tile % AUX, 0:L], v_tok[:, 0, rows], pt[:, h, 0:L], start=True, stop=False)
                    ins = mm(aux[rows, tile % AUX, P:L], v_tok[:, 1, rows], pt[:, h, L:3 * P], start=False, stop=True)
                fills(ins, "aux")
            taken(pe, "aux", aux_of["s5_bb"] + 1)

            def s5_out(j):
                pe.wait_ge(sig("x_states"), j + 1)
                rows = slice(32 * (j % 4), 32 * (j % 4) + 32)
                tile = lin_of["s5_y"] + j // 4
                if j % 4 == 0:
                    begin("lin", tile)
                mm(lin[rows, tile % RING, 0:L], c_bd[:, 0, j, :], s5x[:, j % 2, 0, :], start=True, stop=False)
                mm(lin[rows, tile % RING, 0:L], c_bd[:, 1, j, :], s5x[:, j % 2, 1, :], start=False, stop=True)\
                    .then_inc(sig("s5_used"), 1)

            for j in range(SSM_TILES):
                tile = aux_of["s5_bu"] + j
                begin("aux", tile)
                rows = slice(32 * (j % 4), 32 * (j % 4) + 32)
                for part in range(2):
                    ins = mm(aux[:, tile % AUX, part * L:(part + 1) * L], bb_t[rows, part, j // 4, :],
                             u[rows, j // 4, :], start=True, stop=True)
                fills(ins, "aux")
                ada((j + 1) * 20 // SSM_TILES - j * 20 // SSM_TILES)
                if j >= 2:
                    s5_out(j - 2)
            s5_out(SSM_TILES - 2)
            s5_out(SSM_TILES - 1)
            pe.wait_ge(sig("s5_gelu"), 1)
            linear("glu", "glu", 4, 4, lambda kt: u[:, kt, :])
            pe.wait_ge(sig("cat_ready"), 4)
            linear("ev_out", "ev_out", 2, KT, lambda kt: cat[:, kt, :])
            norm(1, L)
            pe.wait_ge(sig("hn_ready"), 2 * KT)
            b = block_of["od_small"]
            pe.wait_ge(w_in[b % RING], 16 * (b // RING + 1))
            tile = aux_of["wi"]
            begin("aux", tile)
            for qt in range(QT):
                for kt in range(KT):
                    at = KT * P + kt * 8
                    ins = mm(aux[:, tile % AUX, qt * 8:qt * 8 + 8], hn[:, kt, qt * P:(qt + 1) * P],
                             ring[:, b % RING, at:at + 8], start=kt == 0, stop=kt == KT - 1)
            fills(ins, "aux")
            linear("od_small", "od_ki", 1, KT, lambda kt: hn[:, kt, 0:L])

            def index(n):
                if not 2 <= n < 8:
                    return
                m = n - 2
                tile = aux_of["index"] + m
                begin("aux", tile)
                if m == 0:
                    taken(pe, "lin", lin_of["od_in"] + 3)
                qt, heads, width = index_heads(m)
                for q, h in enumerate(heads):
                    ins = mm(aux[:, tile % AUX, q * width:(q + 1) * width],
                             half(qi[:, h // 2, qt * P:(qt + 1) * P], h % 2), half(ki, h % 2)[:, 0:width],
                             start=True, stop=True)
                fills(ins, "aux")

            linear("od_in", "od_in", 2, KT, lambda kt: hn[:, kt, 0:L], between=index)
            pe.wait_ge(sig("squares_qk1"), 1)
            sums("kq_norm1", ones, lambda n: sq1[:, n, :], [[[2 * n], [2 * n + 1]] for n in range(5)], L)
            tokens("v_tok1", lambda n: v1[:, n], 2)
            ada(24)
            ada_groups(47)
            pe.wait_ge(sig("qk1_ready"), 1)
            scores(1, lambda h, qt: q1[:, h, qt * P:(qt + 1) * P], lambda h: k1[:, h // 4, :])
            transposed_probs(1, (lh0, lh1))
            for h in range(OD_HEADS):
                tile = aux_of["out1"] + h
                begin("aux", tile)
                taken(pe, "aux", aux_of["probs1"] + h)
                cols = slice((h // 4) * P, (h // 4 + 1) * P)
                mm(aux[:, tile % AUX, 0:L], v_tok1[:, 0, cols], pt1[:, h, 0:L], start=True, stop=False)
                ins = mm(aux[:, tile % AUX, P:L], v_tok1[:, 1, cols], pt1[:, h, L:3 * P], start=False, stop=True)
                fills(ins, "aux")
            for n in range(AUX):
                taken(pe, "aux", aux_of["out1"] + OD_HEADS - 1 - n)
            linear("od_out", "od_out", 2, KT, lambda kt: q1[:, kt, :])
            both = slice(0, 2 * L)

            norm(2, 2 * L)
            linear("qkv", "qkv", 2, KT, lambda kt: hn[:, kt, :], 2 * L, norm=2)
            pe.wait_ge(sig("at_in"), 48)
            for n in range(RING):
                taken(pe, "lin", lin_of["qkv"] + 11 - n)
            for n in range(5):
                tile = aux_of["rope"] + n
                begin("aux", tile)
                part = (k2 if n == 0 else q2[:, 2 * n - 2:2 * n])[:, :, 0:L]
                fills(mm(aux[:, tile % AUX, :], rope_perm, part, start=True, stop=True), "aux")
            for n in range(2):
                tile = aux_of["v_tok2"] + n
                begin("aux", tile)
                for m in range(4):
                    tok = (2 * n + m // 2) * P
                    ins = nc.tensor.transpose(aux[:, tile % AUX, m * P:(m + 1) * P], v2[:, m % 2, tok:tok + P], ident[:])
                fills(ins, "aux")
            pe.wait_ge(sig("masks2"), 1)
            pe.wait_ge(sig("roped"), 1)
            for i in range(AT_HEADS + 2):
                if i < AT_HEADS:
                    n, s = i // 2, i % 2
                    q, k = half(q2[:, n], s), half(k2[:, n // 4], s)
                    for qt in range(QT):
                        tile = score_tile(i, qt)
                        begin("aux", tile)
                        mm(aux[:, tile % AUX, :], q[:, qt * P:(qt + 1) * P], k, start=True, stop=False)
                        cut = slice((1 - qt) * P, (2 - qt) * P)
                        fills(mm(aux[:, tile % AUX, cut], ident_b, mask_b2[:, qt, :], start=False, stop=True), "aux")
                    tile = score_tile(i, 2)
                    begin("aux", tile)
                    for qt in range(QT):
                        ins = mm(aux[:, tile % AUX, qt * L:(qt + 1) * L], q[:, L + qt * P:L + (qt + 1) * P],
                                 k[:, L:2 * L], start=True, stop=True)
                    fills(ins, "aux")
                if 1 <= i <= AT_HEADS:
                    h = i - 1
                    pe.wait_ge(sig("probs2"), h + 1)
                    for n in range(3):
                        tile = turned_tile(h, n)
                        begin("aux", tile)
                        for m in range(2):
                            for qt in range(QT):
                                src = p2[:, h % 3, qt, (2 * n + m) * P:(2 * n + m + 1) * P] if n < 2 else \
                                    p2[:, h % 3, 2, qt * L + m * P:qt * L + (m + 1) * P]
                                at = m * L + qt * P
                                ins = nc.tensor.transpose(aux[:, tile % AUX, at:at + P], src, ident[:])
                        fills(ins, "aux")
                if i >= 2:
                    h = i - 2
                    n, s = h // 2, h % 2
                    rows = slice(64 * s, 64 * s + 64)
                    cols = slice((n // 4) * P + 64 * s, (n // 4) * P + 64 * s + 64)
                    tile = lin_of["attn"] + n
                    if s == 0:
                        begin("lin", tile)
                    for m in range(3):
                        taken(pe, "aux", turned_tile(h, m))
                    for kt in range(4):
                        mm(lin[rows, tile % RING, 0:L], v_tok2[:, kt, cols],
                           pt2[:, h % 2, kt // 2, (kt % 2) * L:(kt % 2 + 1) * L], start=kt == 0, stop=kt == 3)
                    for m in range(2):
                        ins = mm(lin[rows, tile % RING, L:2 * L], v_tok2[:, 2 + m, cols],
                                 pt2[:, h % 2, 2, m * L:(m + 1) * L], start=m == 0, stop=m == 1)
                    if s == 0:
                        ins.then_inc(sig("attn_even"), 1)
                    else:
                        fills(ins, "lin")
            for n in range(RING):
                taken(pe, "lin", lin_of["attn"] + 7 - n)
            linear("w_o", "w_o", 2, KT, lambda kt: q2[:, kt, :], 2 * L)

            def feed_forward(n, k, width):
                norm(k, width)
                linear(f"ffn{n}_in", f"ffn{n}_in", 2, KT, lambda kt: hn[:, kt, 0:width], width, norm=k)
                for m in range(RING):
                    taken(pe, "lin", lin_of[f"ffn{n}_out"] - 1 - m)
                linear(f"ffn{n}_out", f"ffn{n}_out", 1, FT, lambda kt: hid[:, kt, 0:width], width)

            feed_forward(0, 3, 2 * L)
            norm(4, 2 * L)
            linear("ssm_dt", "ssm_dt", 1, KT, lambda kt: hn[:, kt, :], 2 * L, m=2 * M_HEADS, norm=4)
            ssm_linear()
            pe.wait_ge(sig("dt_rows"), 1)
            tile = aux_of["ssm_rows"]
            begin("aux", tile)
            for n, src in enumerate((rows_g[0:64, 0:L], dt2[:, 0:L], dt2[:, L:2 * L])):
                for qt in range(QT):
                    at = (n * QT + qt) * 64
                    ins = nc.tensor.transpose(aux[:, tile % AUX, at:at + 64], src[:, qt * P:(qt + 1) * P],
                                              ident[0:64, 0:64])
            fills(ins, "aux")

            def turn(name, n, per_row, src):
                for q in range(n):
                    tile = aux_of[name] + q
                    begin("aux", tile)
                    for m in range(4):
                        tok = (q // per_row) * P
                        ins = nc.tensor.transpose(aux[:, tile % AUX, m * P:(m + 1) * P],
                                                  src((q % per_row) * 4 + m)[:, tok:tok + P], ident[:])
                    fills(ins, "aux")

            pe.wait_ge(sig("convolved"), 32)
            turn("bc_tok", 4, 2, lambda n: bm[:, n, L:2 * L])
            turn("xc_tok", 8, 4, lambda n: xc[:, n, :])
            for n in range(AUX):
                taken(pe, "aux", aux_of["xc_tok"] + 7 - n)
            for g in range(GROUPS):
                tile = aux_of["states"] + g
                begin("aux", tile)
                pe.wait_ge(sig("x_weighted"), g + 1)
                for d in range(2):
                    for qt in range(QT):
                        ins = mm(aux[:, tile % AUX, d * L:(d + 1) * L], bc_tok[:, qt, g * P:(g + 1) * P],
                                 xw[:, d, qt, :], start=qt == 0, stop=qt == 1)
                fills(ins, "aux")
            turn("x_tok", 8, 4, lambda n: ys[:, n, :])
            for n in range(AUX):
                taken(pe, "aux", aux_of["x_tok"] + 7 - n)
            for h in range(M_HEADS + 1):
                if h < M_HEADS:
                    g = h // 4
                    if h % 4 == 0:
                        tile = cb_tile(g)
                        begin("aux", tile)
                        for qt in range(QT):
                            ins = mm(aux[:, tile % AUX, qt * L:(qt + 1) * L], bm[:, g, qt * P:(qt + 1) * P],
                                     cm[:, g, :], start=True, stop=True)
                        fills(ins, "aux")
                    tile = bc_tile(h)
                    begin("aux", tile)
                    for d in range(2):
                        one = ident[0:64, d * 32 + h:d * 32 + h + 1].to_broadcast([64, P])
                        ins = mm(aux[:, tile % AUX, d * L:(d + 1) * L], one, rows_g[0:64, :], start=True, stop=True)
                    fills(ins, "aux")
                if h >= 1:
                    q = h - 1
                    g, rows, bank = q // 4, slice(64 * (q % 2), 64 * (q % 2) + 64), (lin_of["ssm_y"] + q // 2) % RING
                    if q % 2 == 0:
                        begin("lin", lin_of["ssm_y"] + q // 2)
                    pe.wait_ge(sig("mixed"), q + 1)
                    pe.wait_ge(sig("c_decayed"), q + 1)
                    x0, x1 = (x_tok[:, qt, q * 64:(q + 1) * 64] for qt in range(QT))
                    m, f = decay[:, q % 2], from_start[:, q % 2]
                    s0, s1 = (state[:, g, d, (q % 4) * 64:(q % 4 + 1) * 64] for d in range(2))
                    out = lin[rows, bank, 0:L]
                    mm(out, x0, m[:, 0:L], start=True, stop=False)
                    mm(out[:, P:L], x1, m[:, L:3 * P], start=False, stop=False)
                    mm(out[:, 0:P], x0, m[:, 3 * P:4 * P], start=False, stop=False)
                    mm(out, x1, m[:, 4 * P:6 * P], start=False, stop=False)
                    mm(out, s0, f[:, 0], start=False, stop=False)
                    ins = mm(out, s1, f[:, 1], start=False, stop=True)
                    if q % 2 == 0:
                        ins.then_inc(sig("ssm_y_even"), 1)
                    else:
                        fills(ins, "lin")
            pe.wait_ge(sig("y_squares"), 1)
            sums("y_norm", ones, lambda n: y_sq[:, n, :], [[[4 * n, 4 * n + 1], [4 * n + 2, 4 * n + 3]] for n in range(4)], L)
            pe.wait_ge(sig("y_normed"), 1)
            linear("ssm_out", "ssm_out", 1, DT_, lambda kt: ys[:, kt, :])
            feed_forward(1, 5, L)
            norm(6, L)


def host_tiles(w, per_block):
    kk, nn = w.shape
    a = w.reshape(kk // P, P, nn // P // per_block, per_block, P)
    return np.ascontiguousarray(a.transpose(2, 1, 3, 0, 4)).reshape(nn // P // per_block, P, -1)


def columns(v):
    a = v.reshape(v.shape[:-1] + (v.shape[-1] // P, P))
    return np.ascontiguousarray(np.moveaxis(a, -1, 0))


def layout(i):
    o = {}
    o["x"] = np.ascontiguousarray(i["x"][0].T.reshape(KT, P, L).transpose(1, 0, 2))
    pair_q = np.concatenate([np.arange(64) + 64 * h for j in range(4) for h in (j, j + 4)])
    w = i["ev_w_in"][0]
    q, k, v, ga, u, gb = np.split(w, np.cumsum([512, 128, 128, 512, 512]), axis=1)
    o["ev_in"] = host_tiles(np.concatenate([u, k, v, q[:, pair_q], ga[:, pair_q], gb], axis=1), 2)
    w = i["ev_w_out"][0]
    o["ev_out"] = host_tiles(np.concatenate([w[:512][pair_q], w[512:]]), 2)
    w = i["ev_glu_w"][0]
    o["glu"] = host_tiles(np.concatenate([w[:, s * 512 + n * P:s * 512 + (n + 1) * P] for n in range(4) for s in range(2)],
                                         axis=1), 4)
    w = i["od_w_in"][0]
    q, k, v, g, qi, ki, wi = np.split(w, np.cumsum([1024, 256, 256, 1024, 512, 64]), axis=1)
    small = host_tiles(np.concatenate([ki, ki], axis=1), 1)[0]
    wi = wi.reshape(KT, P, 8).transpose(1, 0, 2).reshape(P, 64)
    o["od_small"] = np.concatenate([small, wi], axis=1)[None]
    o["od_in"] = host_tiles(np.concatenate([qi, k, v, q, g], axis=1), 2)
    o["od_out"] = host_tiles(i["od_w_out"][0], 2)
    for n in range(2):
        o[f"ada{n}"] = i["ada_w_2"][n].reshape(KT, P, 24, L).transpose(2, 1, 0, 3).reshape(24, P, KT * L)
    o["gcol"] = columns(i["norm_g"])
    o["modb"] = columns(i["ada_b_2"])
    cc = np.stack([i["c_2"][0], i["c_ctx_2"]]).reshape(2, KT, P).transpose(2, 1, 0)
    o["cc"] = np.concatenate([cc, np.zeros((P, KT, 30), np.float32)], axis=2)
    o["group_sum"] = (np.arange(P)[:, None] % 32 == np.arange(2)[None]).astype(np.float32)
    twice_ = lambda g: np.concatenate([g, g])
    o["qk_g"] = np.stack([twice_(i["ev_q_norm_g"][0]), twice_(i["ev_k_norm_g"][0]), i["od_q_norm_g"][0],
                          i["od_k_norm_g"][0]], axis=1)
    o["sink"] = np.repeat(i["ev_sinks"][0][None], P, axis=0)
    by_state = lambda a: a.reshape(SSM_TILES, P).T
    o["s5_par"] = np.stack([by_state(np.repeat(i["ev_ssm_log_dt"][0][:, None], 64, axis=1)),
                            by_state(i["ev_ssm_a_re"][0]), by_state(i["ev_ssm_a_im"][0])], axis=1)
    o["s5_b"] = np.stack([i[f"ev_ssm_b_{n}"][0].reshape(SSM_TILES, P, 16).transpose(1, 0, 2) for n in ("re", "im")], axis=1)
    o["s5_c"] = np.stack([i[f"ev_ssm_c_{n}"][0].transpose(0, 2, 1).reshape(SSM_TILES, P, 16).transpose(1, 0, 2)
                          for n in ("re", "im")], axis=1)
    o["d_col"] = columns(i["ev_ssm_d"][0].reshape(-1))
    o["glu_b"] = columns(i["ev_glu_b"][0])
    o["relb"] = np.repeat(i["rel_bias"][:, :, None], P, axis=2)
    o["ctx"] = np.ascontiguousarray(i["ctx_2"][0].T.reshape(KT, P, L).transpose(1, 0, 2))
    heads = [h for n in range(2) for j in range(4) for h in (8 * n + j, 8 * n + 4 + j)]
    slots = np.concatenate([np.arange(64) + 64 * h for h in heads])
    q, k, v = np.split(i["attn_w_qkv_2"][0], [1024, 1280], axis=1)
    o["qkv"] = host_tiles(np.concatenate([k, v, q[:, slots]], axis=1), 2)
    o["w_o"] = host_tiles(i["attn_w_o_2"][0][slots], 2)
    o["sink2"] = np.repeat(i["attn_sinks_2"][0][heads][None], P, axis=0)
    for n in range(2):
        gate, up = i["ffn_w_gate_2"][n], i["ffn_w_up_2"][n]
        o[f"ffn{n}_in"] = host_tiles(
            np.stack([gate.reshape(D, FT, P), up.reshape(D, FT, P)], axis=2).reshape(D, 2 * FF), 2)
        o[f"ffn{n}_out"] = host_tiles(i["ffn_w_down_2"][n], 1)
    z, xs, bm, cm, dt = np.split(i["ssm_w_in_2"][0], np.cumsum([DI, DI, 1024, 1024]), axis=1)
    o["ssm_in"] = host_tiles(np.concatenate([bm, xs, cm, z], axis=1), 2)
    o["ssm_dt"] = dt.reshape(KT, P, 64).transpose(1, 0, 2).reshape(1, P, KT * 64)
    o["ssm_out"] = host_tiles(i["ssm_w_out_2"][0], 1)
    taps = np.concatenate([i["ssm_conv_w_2"][0], i["ssm_conv_b_2"]])
    xs, bm, cm = np.split(taps, [DI, DI + 1024], axis=1)
    o["conv_w"] = np.moveaxis(columns(np.concatenate([bm, xs, cm], axis=1)), 1, 2)
    o["g2"] = columns(np.stack([i["norm_mix_g_2"][0], i["norm_ffn_g_2"][0], i["norm_mix_g_2"][1],
                                i["norm_ffn_g_2"][1], i["final_norm_g_2"]]))
    o["ssm_cols"] = columns(np.stack([np.repeat(i["ssm_D_2"][0], 64), i["ssm_norm_g_2"][0]]))
    o["dt_cols"] = np.stack([i["ssm_dt_bias_2"][0].reshape(-1), i["ssm_A_log_2"][0].reshape(-1)], axis=1)
    inv = np.float32(10000.0) ** (-np.arange(16, dtype=np.float32) / np.float32(16))
    feature, token = np.arange(P) % 64, np.arange(L)
    place = np.where((feature // 32 == 0)[:, None], (token // 64)[None], (token % 64)[None]).astype(np.float32)
    angle = place * inv[feature % 16][:, None]
    o["rope_cs"] = np.stack([np.cos(angle), np.sin(angle)], axis=1).astype(np.float32)
    perm = np.zeros((P, P), np.float32)
    for m in range(P):
        perm[m + 16 if m % 32 < 16 else m - 16, m] = -1.0 if m % 32 < 16 else 1.0
    o["rope_perm"] = perm
    a, b = np.arange(P)[:, None], np.arange(P)[None]
    o["mask2"] = np.stack([np.where(b <= a, 0.0, NEG), np.where(b >= a, 0.0, NEG)], axis=1).astype(np.float32)
    o["tri"] = np.stack([b >= a, b <= a], axis=1).astype(np.float32)
    o["hot"] = (t5_bucket(2 * P - 1 - np.arange(3 * P))[None] == np.arange(BUCKETS)[:, None]).astype(np.float32)
    o["ident"] = np.eye(P, dtype=np.float32)
    o["pair"] = np.kron(np.eye(2), np.ones((64, 64))).astype(np.float32)
    q, k = np.arange(P)[:, None], np.arange(L)[None]
    causal = np.where(k <= q + P, 0.0, NEG)
    window = np.where(k > q, causal, NEG)
    o["consts"] = np.concatenate([window, causal, np.repeat(np.arange(L)[None], P, axis=0)], axis=1).astype(np.float32)
    return {n: np.ascontiguousarray(a) for n, a in o.items()}


def kernel(**inputs):
    import concourse.bacc as bacc
    from concourse.bass_utils import run_bass_kernel_spmd

    arrays = layout({n: np.asarray(a) for n, a in inputs.items()})
    nc = bacc.Bacc("TRN2", target_bir_lowering=False, num_devices=1)
    t = {n: nc.dram_tensor(n + "_in", a.shape, mybir.dt.from_np(a.dtype), kind="ExternalInput").ap()
         for n, a in arrays.items()}
    t["skew"] = nc.dram_tensor("skew", (EV_HEADS, P, 3 * P), F32, kind="Internal").ap()
    t["out"] = nc.dram_tensor("out", (P, KT, L), F32, kind="ExternalOutput").ap()
    program(nc, t)
    r = run_bass_kernel_spmd(nc, [{n + "_in": a for n, a in arrays.items()}], core_ids=[0])
    y = np.asarray(r.results[0]["out"])
    return np.ascontiguousarray(y.transpose(2, 1, 0)).reshape(1, L, D)
```

```python
import math
from contextlib import ExitStack

import numpy as np

import concourse.bass as bass
from concourse import mybir

F32 = mybir.dt.float32
BF16 = mybir.dt.bfloat16
F32R = mybir.dt.float32r
ACT = mybir.ActivationFunctionType
ALU = mybir.AluOpType
AX_X = mybir.AxisListType.X

P = 128
D = 1024
KT = D // P
L = 256
QT = L // P
EPS = 1e-6
NEG = -1e30
TAKEN = -3e38
TOPK = 64
BUCKETS = 32
EV_HEADS = 8
OD_HEADS = 8
SSM_TILES = 16
AT_HEADS = 16
FF = 2816
FT = FF // P
FH = FT // 2
DI = 2048
DT_ = DI // P
GROUPS = 8
M_HEADS = 32
RING = 4
AUX = 3
AT_SCALE = 64 ** -0.5
ROUND = 1.5 * 2.0 ** 23
TWO_PI = 2.0 * math.pi
PI2_A = 6.28125
PI2_B = round((TWO_PI - PI2_A) * 2 ** 20) / 2 ** 20
PI2_C = TWO_PI - PI2_A - PI2_B

STREAM = [
    ("ev_in", 9, 2 * KT * P), ("ada0", 24, 2 * KT * P), ("glu", 2, 4 * 4 * P), ("ev_out", 4, 2 * KT * P),
    ("od_small", 1, KT * P + KT * OD_HEADS), ("od_in", 12, 2 * KT * P), ("ada1", 24, 2 * KT * P),
    ("od_out", 4, 2 * KT * P), ("qkv", 6, 2 * KT * P), ("w_o", 4, 2 * KT * P),
    ("ffn0a_in", FH, 2 * KT * P), ("ffn0a_out", KT, FH * P), ("ffn0b_in", FH, 2 * KT * P), ("ffn0b_out", KT, FH * P),
    ("ssm_dt", 1, KT * 2 * M_HEADS), ("ssm_in", 24, 2 * KT * P), ("ssm_out", KT, DT_ * P),
    ("ffn1a_in", FH, 2 * KT * P), ("ffn1a_out", KT, FH * P), ("ffn1b_in", FH, 2 * KT * P), ("ffn1b_out", KT, FH * P),
]
SLOT = 2 * KT * P
SPLIT = [
    ("ffn0a_in", 2 * FH), ("ffn0a_out", KT), ("ffn0b_in", 2 * FH), ("ffn0b_out", KT), ("ssm_dt", 1), ("ssm_in", 48),
    ("ffn1a_in", 2 * FH), ("ffn1a_out", KT), ("ffn1b_in", 2 * FH), ("ffn1b_out", KT),
]
LIN_TILES = [
    ("ev_in", 18), ("s5_y", 4), ("glu", 8), ("ev_out", 8), ("od_ki", 1), ("od_in", 24), ("od_out", 8),
    ("qkv", 12), ("attn", 8), ("w_o", 8), ("ffn0a_in", 2 * FH), ("ffn0a_out", 8), ("ffn0b_in", 2 * FH),
    ("ffn0b_out", 8), ("ssm_dt", 1), ("ssm_in", 48),
    ("ssm_y", 16), ("ssm_out", 8), ("ffn1a_in", 2 * FH), ("ffn1a_out", 8), ("ffn1b_in", 2 * FH), ("ffn1b_out", 8),
]
AUX_TILES = [
    ("bias", 8), ("norm0", 2), ("s5_bb", 2), ("qk_norm0", 3), ("v_tok0", 1), ("scores0", 6), ("probs0", 8),
    ("out0", 4), ("s5_bu", 16),
    ("norm1", 2), ("wi", 1), ("index", 6), ("kq_norm1", 5), ("v_tok1", 1), ("scores1", 6), ("probs1", 8),
    ("out1", 8),
    ("norm2", 2), ("rope", 5), ("v_tok2", 2), ("attention", 6 * AT_HEADS), ("norm3", 2),
    ("norm4", 2), ("ssm_rows", 1), ("bc_tok", 4), ("xc_tok", 8), ("states", GROUPS), ("x_tok", 8),
    ("ssm_heads", M_HEADS + GROUPS), ("y_norm", GROUPS // 2), ("norm5", 2), ("norm6", 2),
]


def bases(table):
    at, out = 0, {}
    for name, n in table:
        out[name] = at
        at += n
    return out


def t5_bucket(dist):
    n = np.maximum(dist, 0)
    nf = np.maximum(n, 1).astype(np.float32)
    half = BUCKETS // 2
    scaled = np.log(nf / np.float32(half)) / np.float32(math.log(1024 / half)) * np.float32(half)
    return np.where(n < half, n, np.minimum(half + scaled.astype(np.int32), BUCKETS - 1))


class Count:

    def __init__(self, eng, sem):
        self.eng, self.sem, self.n = eng, sem, 0

    def mark(self, ins):
        ins.then_inc(self.sem, 1)
        self.n = self.n + 1

    def settle(self):
        self.eng.wait_ge(self.sem, self.n)

    def link(self, ins):
        self.mark(ins)
        self.settle()


class Memory:

    def __init__(self, tensor, at=0):
        self.tensor, self.at = tensor, at

    def take(self, *shape, rows=P):
        n = int(np.prod(shape))
        ap = self.tensor[0:rows, self.at:self.at + n]
        self.at += n
        assert self.at <= self.tensor.shape[1], self.at
        if len(shape) == 2:
            ap = ap.rearrange("p (a b) -> p a b", a=shape[0])
        elif len(shape) == 3:
            ap = ap.rearrange("p (a b c) -> p a b c", a=shape[0], b=shape[1])
        return ap


def rounds(eng, count, body):
    whole = count // RING
    for k in range(min(count, RING)):
        body(0, k)
    if whole > 2:
        with eng.Fori(1, whole) as i:
            for k in range(RING):
                body(i, k)
    else:
        for n in range(RING, whole * RING):
            body(n // RING, n % RING)
    for n in range(max(whole, 1) * RING, count):
        body(n // RING, n % RING)


def twice(ap):
    return ap.unsqueeze(1).to_broadcast([ap.shape[0], 2, ap.shape[1]])


def each(ap, n):
    return ap.unsqueeze(2).to_broadcast([ap.shape[0], ap.shape[1], n])


def program(nc, t):
    with ExitStack() as ctx:
        def sb(name, shape, dt=F32):
            return ctx.enter_context(nc.sbuf_tensor(name, shape, dt))

        sems = {}

        def sig(name):
            if name not in sems:
                sems[name] = ctx.enter_context(nc.semaphore(name))
            return sems[name]

        block_of = bases([(n, c) for n, c, _ in STREAM])
        lin_of = bases(LIN_TILES)
        aux_of = bases(AUX_TILES)
        unit_of = bases(SPLIT)

        ring = sb("ring", [P, RING, SLOT])
        xres = sb("xres", [P, KT, 2 * L])
        rcol = sb("rcol", [P, 2 * QT])
        ident = sb("ident", [P, P])
        ones = sb("ones", [P, P])
        pair = sb("pair", [P, P])
        gcol = sb("gcol", [P, 2, KT])
        mod = sb("mod", [P, 2, 48, 2])
        modb = sb("modb", [P, 2, 48])
        sc_c = sb("sc_c", [P, KT, 32])
        ada_sb = sb("ada_sb", [P, L])
        group_sum = sb("group_sum", [P, 2])
        eps = sb("eps", [P, 1])
        half_pi = sb("half_pi", [P, 1])
        ARENA, HN = 28416, KT * 2 * L

        def places(*tensors):
            with ExitStack() as shared:
                return [shared.enter_context(nc.sbuf_tensor(n, s, dt)) for n, s, dt in tensors]

        arena, hn = places(("arena", [P, ARENA], F32), ("hn", [P, KT, 2 * L], F32))
        W_UNITS = 4
        hid_split, w_split, hn_hi, _, hn_lo = places(
            ("hid_split", [P, 2, FH, 2 * L], F32R), ("w_split", [P, W_UNITS, 2, FH * P], F32R),
            ("hn_hi", [P, KT, 2 * L], F32R), ("hi_end", [P, ARENA - 22528 - HN], F32), ("hn_lo", [P, KT, 2 * L], F32R))
        _, w_split_ssm = places(("ssm_start", [P, 18432], F32), ("w_split_ssm", [P, 2, 2, KT * P], F32R))
        whole_arena = sb("whole_arena", [P, ARENA + HN])
        lin = ctx.enter_context(nc.psum_tensor("lin", [P, RING, 2 * L], F32))
        aux = ctx.enter_context(nc.psum_tensor("aux", [P, AUX, 2 * L], F32))
        modp = ctx.enter_context(nc.psum_tensor("modp", [P, 2 * L], F32))

        mem = Memory(arena)
        bias_a = mem.take(EV_HEADS, L)
        bias_b = mem.take(OD_HEADS, L)
        base = mem.at
        qa = mem.take(4, L)
        ka = mem.take(L)
        va = mem.take(L)
        v_tok = mem.take(QT, P)
        gate_a = mem.take(4, L)
        u = mem.take(4, L)
        gate_b = mem.take(4, L)
        at = mem.at
        sq0 = mem.take(5, L)
        r0 = mem.take(5, L)
        sq_end = mem.at
        mem.at = at
        lg0 = mem.take(EV_HEADS, P)
        lg1 = mem.take(EV_HEADS, L)
        pt = mem.take(EV_HEADS, 3 * P)
        end = mem.at
        mem.at = at
        table = mem.take(EV_HEADS, 3 * P)
        mem.at = max(end, mem.at, sq_end)
        cos_t = mem.take(SSM_TILES, L)
        sin_t = mem.take(SSM_TILES, L)
        s5w = mem.take(2, 2, L)
        s5z = mem.take(2, 2, L)
        s5q = mem.take(2, 2 * L).rearrange("p a (b c) -> p a b c", b=2)
        s5x = mem.take(2, 2, L)
        s5t = mem.take(2, 2 * L)
        cat = hn[:, :, L:2 * L]
        
        par = sb("par", [P, 32, SSM_TILES])
        consts = sb("consts", [P, L + L + L])
        mask_a, mask_b, steps = (consts[:, n * L:(n + 1) * L] for n in range(3))
        b_in = sb("b_in", [P, 2, SSM_TILES, 16])
        bd = s5x.rearrange("p a b c -> p (a b c)").rearrange("p (a b c) -> p a b c", a=2, b=SSM_TILES)
        bb_t = sb("bb_t", [P, 2, 4, P])
        c_bd = sb("c_bd", [P, 2, SSM_TILES, 32])
        d_col = sb("d_col", [P, 4])
        glu_b = sb("glu_b", [P, 8])
        qk_g = sb("qk_g", [P, 4])
        sink = sb("sink", [P, EV_HEADS])
        relb = s5z.rearrange("p a b c -> p (a b c)")[0:BUCKETS].rearrange("p (a b) -> p a b", a=EV_HEADS)
        hot = s5q.rearrange("p a b c -> p (a b c)")[0:BUCKETS, 0:3 * P]
        small = sb("small", [P, 12, 8])
        g2 = sb("g2", [P, 5, KT])
        nsink2_in = sb("nsink2_in", [P, AT_HEADS])
        a_col = sb("a_col", [P, KT, 2])
        ssm_cols = sb("ssm_cols", [P, 2, DT_])
        dt_cols = sb("dt_cols", [2 * M_HEADS, 2])
        stat_ssm = sb("stat_ssm", [P, 4])

        mem = Memory(arena, base)
        q1 = mem.take(OD_HEADS, L)
        k1 = mem.take(2, L)
        v1 = mem.take(2, L)
        gate1 = mem.take(OD_HEADS, L)
        qi = mem.take(4, L)
        ki = mem.take(L)
        wi = mem.take(QT, OD_HEADS)
        v_tok1 = mem.take(QT, 2 * P)
        rel = mem.take(2, 2 * L)
        idx = mem.take(QT, L)
        top = mem.take(QT, 8)
        sel = mem.take(QT, L)
        at = mem.at
        sq1 = mem.take(10, L)
        r1 = mem.take(10, L)
        end = mem.at
        mem.at = at
        lh0 = mem.take(OD_HEADS, P)
        lh1 = mem.take(OD_HEADS, L)
        pt1 = mem.take(OD_HEADS, 3 * P)
        mem.at = max(end, mem.at)

        mem = Memory(arena)
        q2 = mem.take(8, 2 * L)
        k2 = mem.take(2, 2 * L)
        v2 = mem.take(2, 2 * L)
        v_tok2 = mem.take(4, 2 * P)
        rope_cs = mem.take(2, L)
        rope_tmp = mem.take(2, L)
        mask2 = mem.take(2, P)
        rope_perm = mem.take(P)
        p2 = mem.take(3, 3, 2 * L)
        pt2 = mem.take(2, 3, 2 * L)
        stat2 = mem.take(6, AT_HEADS, 4)
        nsink2 = mem.take(2, AT_HEADS)
        ident_b = mem.take(P // 2).bitcast(BF16)
        mask_b2 = mem.take(P).bitcast(BF16).rearrange("p (a b) -> p a b", a=2)
        mem = Memory(arena, 22528 + HN)
        silu_g = mem.take(2, 2 * L)
        mem = Memory(arena)
        zs = mem.take(DT_, L)
        ys = mem.take(DT_, L)
        at = mem.at
        xc = mem.take(DT_, L)
        mem.at = at
        state = mem.take(GROUPS, 2, L)
        bm = mem.take(GROUPS, 2 * L)
        cm = mem.take(GROUPS, L)
        x_tok = mem.take(QT, DI)
        at = mem.at
        xc_tok = mem.take(QT, DI)
        end = mem.at
        mem.at = at
        decay = [mem.take(2, 3 * L)]
        from_start = [mem.take(2, 2, L)]
        decay.append(mem.take(2, 3 * L))
        mem.at = end
        tri = mem.take(2, P)
        rows_g = mem.take(L)
        cols_g = mem.take(3, QT, 2 * M_HEADS)
        conv_w = mem.take(32, 4)
        mem2 = Memory(hn[:].rearrange("p a b -> p (a b)"))
        bc_tok = mem2.take(QT, GROUPS * P)
        xw = mem2.take(2, QT, L)
        mem2 = Memory(mem2.tensor)
        decay.append(mem2.take(2, 3 * L))
        from_start += [mem2.take(2, 2, L) for _ in range(2)]
        cb = bm[:, 0:6, L:2 * L].rearrange("p (a b) c -> p a b c", a=2)
        y_sq = hn[:].rearrange("p a b -> p (a b)").rearrange("p (a b) -> p a b", a=DT_)
        y_rs = cm
        xs_pair = arena[:, DT_ * L:3 * DT_ * L].rearrange("p (s n c) -> p n s c", s=2, n=DT_)
        dt_rows = c_bd[:].rearrange("p a b c -> p (a b c)")[0:64].rearrange("p (a b) -> p a b", a=2)
        dt2, da = dt_rows[:, 0, :], dt_rows[:, 1, :]
        spare = bb_t[:].rearrange("p a b c -> p (a b c)")[0:64].rearrange("p (a b) -> p a b", a=2)
        dt_tmp, dt_tmp2 = spare[:, 0, :], spare[:, 1, :]
        dt_tmp3 = b_in[:].rearrange("p a b c -> p (a b c)")[0:64]
        tot = stat_ssm[0:64, 0:2]
        a_neg = stat_ssm[0:64, 2:3]

        w_in = [sig(f"w_in{n}") for n in range(RING)]
        lin_free = [sig(f"lin_free{n}") for n in range(RING)]
        aux_free = [sig(f"aux_free{n}") for n in range(AUX)]

        def lin_count(tile):
            return tile + 1 - (4 if tile >= lin_of["s5_y"] + 4 else 0)

        def full(eng, banks, tile, later=0):
            eng.wait_ge(sig(banks + "_full"), later + (lin_count(tile) if banks == "lin" else tile + 1))

        def frees(ins, banks, tile):
            sems_, n = (lin_free, RING) if banks == "lin" else (aux_free, AUX)
            ins.then_inc(sems_[tile % n], 1)

        def taken(eng, banks, tile, turns=0):
            sems_, n = (lin_free, RING) if banks == "lin" else (aux_free, AUX)
            eng.wait_ge(sems_[tile % n], turns + (tile // n + 1))

        def score_tile(h, n):
            return aux_of["attention"] + max(6 * h - 3, 0) + n

        def turned_tile(h, n):
            return aux_of["attention"] + (6 * h + 6 if h < AT_HEADS - 1 else 6 * h + 3) + n

        def cb_tile(g):
            return aux_of["ssm_heads"] + 5 * g

        def bc_tile(h):
            return aux_of["ssm_heads"] + 5 * (h // 4) + 1 + h % 4

        def head_done(eng, layer, h):
            if h % 2:
                full(eng, "lin", lin_of[layer] + h // 2)
            else:
                eng.wait_ge(sig(f"{layer}_even"), h // 2 + 1)

        used = []
        for name, n, _ in STREAM:
            if name in unit_of:
                used += [("w_low", unit_of[name] + dict(SPLIT)[name] // n * (m + 1)) for m in range(n)]
            elif name[:3] == "ada":
                used += [("ada_used", int(name[3]) * 24 + m + 1) for m in range(n)]
            else:
                stage = {"od_small": "od_ki"}.get(name, name)
                tiles = dict(LIN_TILES)[stage] // n
                used += [("lin_full", lin_count(lin_of[stage] + tiles * (m + 1) - 1)) for m in range(n)]

        def index_heads(m):
            return (1, (m % 2 + 4 * (m // 2), m % 2 + 4 * (m // 2) + 2), L) if m < 4 else \
                (0, range(m - 4, OD_HEADS, 2), P)

        block = ctx.enter_context(nc.Block())

        @block.sync
        def _(sp):
            sp.dma_start(xres[:, :, 0:L], t["x"]).then_inc(sig("x_in"), 16)
            for name, n, cols in STREAM:
                first = block_of[name]

                def load(i, k):
                    b = first + k
                    if isinstance(i, int):
                        b, i = b + i * RING, 0
                    if b >= RING or not isinstance(i, int):
                        which, value = used[b - RING] if isinstance(i, int) else used[b]
                        if not isinstance(i, int):
                            value = value + (i - 1) * (used[b + RING][1] - used[b][1])
                        sp.wait_ge(sig(which), value)
                    at = b - first + i * RING
                    source = t[name][at] if isinstance(i, int) else \
                        t[name][bass.ds(at, 1)].rearrange("a p n -> p (a n)")
                    sp.dma_start(ring[:, b % RING, 0:cols], source).then_inc(w_in[b % RING], 16)

                rounds(sp, n, load)
            sp.wait_ge(sig("hn_ready"), 7 * KT)
            sp.dma_start(t["out"], hn[:, :, 0:L]).then_inc(sig("stored"), 16)
            sp.wait_ge(sig("stored"), 16)

        def sum_squares(pool, own, k, width):
            total = hn[:, 0, 0:width]
            for kt in range(1, KT):
                pool.wait_ge(sig("squares"), KT * k + kt + 1)
                ins = nc.gpsimd.tensor_tensor(total, total, hn[:, kt, 0:width], ALU.add)
                if kt < KT - 1:
                    own.link(ins)
            ins.then_inc(sig("square_sums"), 1)

        def hidden_parts(pool, own, n, width):
            for m in range(FT):
                taken(pool, "lin", lin_of[f"ffn{n}{'ab'[m // FH]}_in"] + 2 * (m % FH) + 1)
                if m == FH:
                    full(pool, "lin", lin_of[f"ffn{n}a_out"] + KT - 1)
                hi, lo = (hid_split[:, part, m % FH, 0:width] for part in range(2))
                own.link(nc.gpsimd.tensor_copy(hi, silu_g[:, m % 2, 0:width]))
                nc.gpsimd.tensor_tensor(lo, silu_g[:, m % 2, 0:width], hi.bitcast(F32), ALU.subtract)\
                    .then_inc(sig("hid_ready"), 1)

        def unit(name, u):
            n, cols = next((n, c) for x, n, c in STREAM if x == name)
            per_block = dict(SPLIT)[name] // n
            b, cols = block_of[name] + u // per_block, cols // per_block
            if name[:3] == "ssm":
                parts = w_split_ssm[:, (unit_of[name] + u - unit_of["ssm_dt"]) % 2, :, 0:cols]
            else:
                first = unit_of[name[:4] + "a_in"]
                parts = w_split[:, (unit_of[name] + u - first) % W_UNITS, :, 0:cols]
            return parts, ring[:, b % RING, u % per_block * cols:(u % per_block + 1) * cols], b

        def weights_hi(act, name, u):
            parts, w, b = unit(name, u)
            act.wait_ge(w_in[b % RING], 16 * (b // RING + 1))
            first = lin_of["ssm_dt" if name[:3] == "ssm" else name[:4] + "a_in"]
            before = lin_of[name] + u - (2 if name[:3] == "ssm" else W_UNITS)
            if before >= first:
                full(act, "lin", before)
            act.activation(parts[:, 0], w, ACT.Copy).then_inc(sig("w_high"), 1)

        def weights_lo(dve, name, u):
            parts, w, _ = unit(name, u)
            dve.wait_ge(sig("w_high"), unit_of[name] + u + 1)
            dve.tensor_tensor(parts[:, 1], w, parts[:, 0].bitcast(F32), ALU.subtract).then_inc(sig("w_low"), 1)

        @block.gpsimd
        def _(pool):
            own = Count(pool, sig("pool_own"))
            for dst, name in ((relb, "relb"), (hot, "hot")):
                pool.dma_start(dst, t[name]).then_inc(sig("rel_in"), 16)
            for dst, name in ((pair[:], "pair"), (consts[:], "consts"),
                              (qk_g[:], "qk_g"), (sink[:], "sink"), (d_col[:], "d_col"), (glu_b[:], "glu_b"),
                              (sc_c[:], "cc"), (group_sum[:], "group_sum"), (modb[:], "modb"), (g2[:], "g2"), (ssm_cols[:], "ssm_cols"),
                              (dt_cols[:], "dt_cols"), (nsink2_in[:], "sink2"),
                              (xres[:, :, L:2 * L], "ctx")):
                pool.dma_start(dst, t[name]).then_inc(sig("const_in"), 16)
            pool.dma_start(par[:, 0:3, :], t["s5_par"]).then_inc(sig("s5_in"), 16)
            pool.dma_start(b_in[:], t["s5_b"]).then_inc(sig("s5_in"), 16)
            nc.gpsimd.memset(eps[:], EPS)
            nc.gpsimd.memset(half_pi[:], math.pi / 2)
            nc.gpsimd.memset(ones[:], 1.0)
            nc.gpsimd.memset(bd, 0.0)
            nc.gpsimd.memset(c_bd[:], 0.0).then_inc(sig("made"), 1)
            pool.wait_ge(sig("made"), 1)
            for n in range(2):
                for part in range(2):
                    rows = slice(64 * n, 64 * n + 64)
                    pool.dma_start(c_bd[rows, part, :, 16 * n:16 * n + 16], t["s5_c"][rows, part])\
                        .then_inc(sig("c_in"), 16)
            sum_squares(pool, own, 0, L)
            taken(pool, "aux", aux_of["bias"] + EV_HEADS - 1)
            pool.dma_start(t["skew"].rearrange("h p n -> p h n"), table).then_inc(sig("table_out"), 16)
            pool.wait_ge(sig("table_out"), 16)
            skewed = bass.AP(t["skew"].tensor, P - 1, [[3 * P - 1, P], [3 * P * P, EV_HEADS], [1, L]])
            pool.dma_start(bias_b, skewed).then_inc(sig("table_back"), 16)
            for j in range(SSM_TILES):
                p = j % 2
                turned, back = s5q[:, 0], s5q[:, 1]
                z = s5z[:, p]
                pool.wait_ge(sig("z_ready"), j + 1)
                own.mark(nc.gpsimd.tensor_tensor(turned, z, twice(cos_t[:, j, :]), ALU.mult))
                own.link(nc.gpsimd.tensor_tensor(back, z, twice(sin_t[:, j, :]), ALU.mult))
                if j >= 2:
                    pool.wait_ge(sig("s5_used"), j - 1)
                own.mark(nc.gpsimd.tensor_tensor(s5x[:, p, 0, :], turned[:, 0], back[:, 1], ALU.subtract))
                nc.gpsimd.tensor_tensor(s5x[:, p, 1, :], turned[:, 1], back[:, 0], ALU.add)\
                    .then_inc(sig("x_states"), 1)
                pool.wait_ge(sig("x_states"), j + 1)
            sum_squares(pool, own, 1, L)
            sum_squares(pool, own, 2, 2 * L)
            taken(pool, "lin", lin_of["od_out"] + KT - 1)
            for dst, name in ((rope_cs, "rope_cs"), (rope_perm, "rope_perm"), (mask2, "mask2")):
                pool.dma_start(dst, t[name]).then_inc(sig("at_in"), 16)
            sum_squares(pool, own, 3, 2 * L)
            hidden_parts(pool, own, 0, 2 * L)
            sum_squares(pool, own, 4, 2 * L)
            taken(pool, "lin", lin_of["ffn0b_out"] + KT - 1)
            for dst, name in ((conv_w, "conv_w"), (tri, "tri")):
                pool.dma_start(dst, t[name]).then_inc(sig("ssm_in"), 16)
            for h in range(M_HEADS):
                taken(pool, "aux", bc_tile(h))
                since = from_start[h // 2 % 3][:, h % 2]
                nc.gpsimd.tensor_tensor(since, since, twice(cm[:, h // 4, :]), ALU.mult)\
                    .then_inc(sig("c_decayed"), 1)
            sum_squares(pool, own, 5, L)
            hidden_parts(pool, own, 1, L)
            sum_squares(pool, own, 6, L)

        def ada_copies(act, first, n):
            for m in range(first, first + n):
                act.wait_ge(sig("ada_used"), m + 1)
                if m:
                    act.wait_ge(sig("ada_summed"), m)
                act.activation(ada_sb[:], modp[:, 0:L], ACT.Copy).then_inc(sig("ada_copied"), 1)

        def act_norm(act, k, width, after=None, shift=None, split=False, meanwhile=None):
            for kt in range(KT):
                if after is not None:
                    taken(act, "lin", lin_of[after] + kt)
                act.activation(hn[:, kt, 0:width], xres[:, kt, 0:width], ACT.Square).then_inc(sig("squares"), 1)
            if meanwhile is not None:
                meanwhile()
            tile = aux_of[f"norm{k}"]
            full(act, "aux", tile)
            n = width // P
            frees(act.activation(rcol[:, 0:n], aux[:, tile % AUX, 0:n], ACT.Sqrt, scale=1.0 / D, bias=eps[:]), "aux",
                  tile)
            if shift is not None:
                layer, chunk, nth = shift
                for kt in range(KT):
                    act.wait_ge(sig("scaled"), KT * nth + kt + 1)
                    for s in range(width // L):
                        cols = hn[:, kt, s * L:(s + 1) * L]
                        by = mod[:, layer, chunk * KT + kt, s:s + 1]
                        if split:
                            act.activation(hn_hi[:, kt, s * L:(s + 1) * L], cols, ACT.Identity, bias=by)
                        ins = act.activation(cols, cols, ACT.Identity, bias=by)
                    ins.then_inc(sig("shifted" if split else "hn_ready"), 1)

        def softmax_exps(act, own, layer, logits, stats, sinks):
            act.wait_ge(sig(f"maxima{layer}"), 1)
            for qt in range(QT):
                for h in range(8):
                    ins = act.activation(logits[qt][:, h, :], logits[qt][:, h, :], ACT.Exp,
                                         bias=stats[:, 2 + qt, h:h + 1], accum_out=stats[:, 6 + qt, h:h + 1])
            if sinks:
                own.mark(ins)
                ins = act.activation(stats[:, 8:10, :], stats[:, 4:6, :], ACT.Exp)
            ins.then_inc(sig(f"exps{layer}"), 1)

        def roots(act, name, widths, scale, dst):
            for n, width in enumerate(widths):
                tile = aux_of[name] + n
                full(act, "aux", tile)
                frees(act.activation(dst(n), aux[:, tile % AUX, 0:width], ACT.Sqrt, scale=scale, bias=eps[:]),
                      "aux", tile)

        def copies(act, name, n, src, dst):
            for m in range(n):
                tile = aux_of[name] + m
                full(act, "aux", tile)
                frees(act.activation(dst(m), src(aux[:, tile % AUX]), ACT.Copy), "aux", tile)

        def ffn_units(n):
            units = [(f"ffn{n}{part}", u) for part, count in
                     (("a_in", 2 * FH), ("a_out", KT), ("b_in", 2 * FH), ("b_out", KT)) for u in range(count)]
            return [(*unit_, units[v + W_UNITS] if v + W_UNITS < len(units) else None)
                    for v, unit_ in enumerate(units)]

        def ffn_scalar(act, n, width):
            nth = n * FT
            for stage, u, later in ffn_units(n):
                if later is not None:
                    weights_hi(act, *later)
                if stage[-2:] == "in" and u % 2 == 0:
                    tile = lin_of[stage] + u
                    full(act, "lin", tile)
                    if nth >= 2:
                        act.wait_ge(sig("hid_ready"), nth - 1)
                    frees(act.activation(silu_g[:, nth % 2, 0:width], lin[:, tile % RING, 0:width], ACT.Silu),
                          "lin", tile)
                    nth += 1

        def second_block_scalar(act, own):
            act_norm(act, 2, 2 * L, "od_out", (0, 0, 0))
            into = [k2[:, n] for n in range(2)] + [v2[:, n] for n in range(2)] + [q2[:, n] for n in range(8)]
            for n, dst in enumerate(into):
                tile = lin_of["qkv"] + n
                full(act, "lin", tile)
                frees(act.activation(dst, lin[:, tile % RING, :], ACT.Copy), "lin", tile)
            copies(act, "v_tok2", 2, lambda ps: ps,
                   lambda n: v_tok2[:, 2 * n:2 * n + 2, :].rearrange("p a b -> p (a b)"))
            for i in range(AT_HEADS + 1):
                if i < AT_HEADS:
                    act.wait_ge(sig("maxima2"), i + 1)
                    for n, (part, cols) in enumerate(((0, slice(0, 2 * L)), (1, slice(0, 2 * L)),
                                                      (2, slice(0, L)), (2, slice(L, 2 * L)))):
                        tile = score_tile(i, part)
                        ins = act.activation(p2[:, i % 3, part, cols], aux[:, tile % AUX, cols], ACT.Exp,
                                             scale=AT_SCALE, bias=stat2[:, 1, i, n:n + 1],
                                             accum_out=stat2[:, 2, i, n:n + 1])
                        if n != 2:
                            frees(ins, "aux", tile)
                    act.activation(stat2[:, 3, i, :], stat2[:, 1, i, :], ACT.Exp, bias=nsink2[:, 0, i:i + 1])\
                        .then_inc(sig("exps2"), 1)
                if i >= 1:
                    h = i - 1
                    for n in range(3):
                        tile = turned_tile(h, n)
                        full(act, "aux", tile)
                        if n == 0 and h >= 2:
                            head_done(act, "attn", h - 2)
                        frees(act.activation(pt2[:, h % 2, n, :], aux[:, tile % AUX, :], ACT.Copy), "aux", tile)
            full(act, "lin", lin_of["attn"] + 7)
            for u in range(W_UNITS):
                weights_hi(act, "ffn0a_in", u)
            act_norm(act, 3, 2 * L, "w_o", (0, 3, 1), True)
            ffn_scalar(act, 0, 2 * L)
            def first_weights():
                full(act, "lin", lin_of["ffn0b_out"] + KT - 1)
                weights_hi(act, "ssm_dt", 0)
                weights_hi(act, "ssm_in", 0)

            act_norm(act, 4, 2 * L, "ffn0b_out", (1, 0, 2), True, first_weights)
            weights_hi(act, "ssm_in", 1)
            weights_hi(act, "ssm_in", 2)
            act.wait_ge(sig("dt_abs"), 1)
            own.link(act.activation(dt_tmp, dt_tmp, ACT.Exp, scale=-1.0))
            own.mark(act.activation(dt_tmp2, dt_tmp, ACT.Ln, bias=ones[0:64, 0:1]))
            act.activation(a_neg, dt_cols[:, 1:2], ACT.Exp).then_inc(sig("dt_exp"), 1)
            for n in range(48):
                tile = lin_of["ssm_in"] + n
                if n + 3 < 48:
                    weights_hi(act, "ssm_in", n + 3)
                if n == 3:
                    act.wait_ge(sig("dt_summed"), 1)
                    act.activation(dt_tmp[:, L:2 * L], dt_tmp[:, L:2 * L], ACT.Exp, scale=-1.0, bias=tot[:, 1:2])\
                        .then_inc(sig("dt_weights"), 1)
                if n < 32:
                    taken(act, "lin", tile)
                    dst = bm[:, n, :] if n < 8 else xs_pair[:, n - 8] if n < 24 else cm[:, n - 24, :]
                    act.activation(dst, dst, ACT.Silu).then_inc(sig("convolved"), 1)
                else:
                    full(act, "lin", tile)
                    frees(act.activation(zs[:, n - 32, :], lin[:, tile % RING, 0:L], ACT.Silu), "lin", tile)
            copies(act, "ssm_rows", 1, lambda ps: ps[:, 0:6 * 64], lambda n: cols_g.rearrange("p a b c -> p (a b c)"))
            turned_copies(act, "bc_tok", 4, bc_tok, 2, 0, act.activation)
            turned_copies(act, "xc_tok", 8, xc_tok, 4, 0, act.activation)
            for g in range(GROUPS):
                tile = aux_of["states"] + g
                full(act, "aux", tile)
                frees(act.activation(state[:, g].rearrange("p a b -> p (a b)"), aux[:, tile % AUX, :], ACT.Copy),
                      "aux", tile)
            turned_copies(act, "x_tok", 8, x_tok, 4, 0, act.activation)
            for h in range(M_HEADS):
                between, since = decay[h // 2 % 3][:, h % 2], from_start[h // 2 % 3][:, h % 2]
                act.wait_ge(sig("gaps"), h + 1)
                act.activation(between, between, ACT.Exp).then_inc(sig("decays"), 1)
                if h >= 6:
                    full(act, "lin", lin_of["ssm_y"] + h // 2 - 3)
                tile = bc_tile(h)
                frees(act.activation(since.rearrange("p a b -> p (a b)"), aux[:, tile % AUX, :], ACT.Exp), "aux", tile)
            act.wait_ge(sig("y_gated"), 1)
            act.activation(y_sq, ys, ACT.Square).then_inc(sig("y_squares"), 1)
            roots(act, "y_norm", [2 * L] * 4, 1.0 / L,
                  lambda n: y_rs[:, 2 * n:2 * n + 2, :].rearrange("p a b -> p (a b)"))
            act.wait_ge(sig("y_normed"), 1)
            for u in range(W_UNITS):
                weights_hi(act, "ffn1a_in", u)
            act_norm(act, 5, L, "ssm_out", (1, 3, 3), True)
            ffn_scalar(act, 1, L)
            act_norm(act, 6, L, "ffn1b_out")

        def turned_copies(eng, name, n, dst, per_row, parity, copy):
            for q in range(parity, n, 2):
                tile = aux_of[name] + q
                full(eng, "aux", tile)
                out, src = dst[:, q // per_row, (q % per_row) * 2 * L:(q % per_row + 1) * 2 * L], aux[:, tile % AUX, :]
                frees(copy(out, src, ACT.Copy) if parity == 0 else copy(out, src), "aux", tile)

        def normed(dve, k, width, a, shifted=False, split=None):
            def low(kt):
                dve.wait_ge(sig("shifted"), KT * split + kt + 1)
                dve.tensor_tensor(hn_lo[:, kt, 0:width], hn[:, kt, 0:width], hn_hi[:, kt, 0:width].bitcast(F32),
                                  ALU.subtract).then_inc(sig("hn_ready"), 1)

            tile = aux_of[f"norm{k}"]
            taken(dve, "aux", tile)
            dve.reciprocal(rcol[:, 0:width // P], rcol[:, 0:width // P]).then_inc(sig("rms"), 1)
            full(dve, "aux", tile + 1)
            for kt in range(KT):
                for s in range(width // L):
                    cols = slice(s * L, (s + 1) * L)
                    ins = dve.scalar_tensor_tensor(
                        out=hn[:, kt, cols], in0=xres[:, kt, cols], scalar=a(kt, s),
                        in1=aux[:, (tile + 1) % AUX, cols], op0=ALU.mult, op1=ALU.mult)
                ins.then_inc(sig("scaled" if shifted else "hn_ready"), 1)
                if split is not None and kt >= 2:
                    low(kt - 2)
            if split is not None:
                low(KT - 2)
                low(KT - 1)
            frees(dve.tensor_copy(rcol[:, 0:1], rcol[:, 0:1]), "aux", tile + 1)

        def maxima(dve, own, layer, logits, stats, sinks):
            own.settle()
            own.mark(dve.tensor_reduce(stats[:, 0, :], logits[0], AX_X, ALU.max))
            own.link(dve.tensor_reduce(stats[:, 1, :], logits[1], AX_X, ALU.max))
            if sinks is not None:
                own.link(dve.tensor_tensor(stats[:, 0:2, :], stats[:, 0:2, :], twice(sinks), ALU.max))
            ins = dve.tensor_scalar(stats[:, 2:4, :], stats[:, 0:2, :], -1.0, None, ALU.mult)
            if sinks is not None:
                own.link(ins)
                ins = dve.tensor_tensor(stats[:, 4:6, :], stats[:, 2:4, :], twice(sinks), ALU.add)
            ins.then_inc(sig(f"maxima{layer}"), 1)

        def probabilities(dve, own, layer, logits, stats, sinks):
            dve.wait_ge(sig(f"exps{layer}"), 1)
            if sinks:
                own.link(dve.tensor_tensor(stats[:, 6:8, :], stats[:, 6:8, :], stats[:, 8:10, :], ALU.add))
            own.link(dve.reciprocal(stats[:, 10:12, :], stats[:, 6:8, :]))
            own.mark(dve.tensor_tensor(logits[0], logits[0], each(stats[:, 10, :], P), ALU.mult))
            dve.tensor_tensor(logits[1], logits[1], each(stats[:, 11, :], L), ALU.mult)\
                .then_inc(sig(f"probs{layer}"), 1)

        def scaled_logits(dve, own, layer, bias, logits, scale):
            for n in range(6):
                tile = aux_of[f"scores{layer}"] + n
                full(dve, "aux", tile)
                if n < 2:
                    heads = slice(4 * n, 4 * n + 4)
                    out, add = logits[0][:, heads, :], bias[:, heads, P:L]
                else:
                    heads = slice(2 * (n - 2), 2 * (n - 2) + 2)
                    out, add = logits[1][:, heads, :], bias[:, heads, :]
                frees(dve.scalar_tensor_tensor(
                    out=out, in0=aux[:, tile % AUX].rearrange("p (a b) -> p a b", a=out.shape[1]), scalar=scale,
                    in1=add, op0=ALU.mult, op1=ALU.add), "aux", tile)
            for n in range(3, 6):
                taken(dve, "aux", aux_of[f"scores{layer}"] + n)

        def gated_tile(dve, tile, n, layer, chunk, parts):
            full(dve, "lin", tile)
            for s in range(parts):
                cols = slice(s * L, (s + 1) * L)
                ins = dve.scalar_tensor_tensor(
                    out=xres[:, n, cols], in0=lin[:, tile % RING, cols],
                    scalar=mod[:, layer, chunk * KT + n, s:s + 1], in1=xres[:, n, cols], op0=ALU.mult, op1=ALU.add)
            frees(ins, "lin", tile)

        def gated_add(dve, own, name, layer, chunk, parts):
            for n in range(KT):
                gated_tile(dve, lin_of[name] + n, n, layer, chunk, parts)
            for n in range(RING):
                taken(dve, "lin", lin_of[name] + KT - 1 - n)

        def modulated(dve, own, k, width, layer, chunk, split=None):
            own.link(dve.scalar_tensor_tensor(
                out=a_col[:], in0=mod[:, layer, (chunk + 1) * KT:(chunk + 2) * KT, :], scalar=1.0,
                in1=each(g2[:, k - 2, :], 2), op0=ALU.add, op1=ALU.mult))
            normed(dve, k, width, lambda kt, s: a_col[:, kt, s:s + 1], True, split)

        def ffn_vector(dve, n, width):
            nth = n * FT
            for stage, u, later in ffn_units(n):
                tile = lin_of[stage] + u
                if later is not None:
                    weights_lo(dve, *later)
                if stage[-2:] == "in" and u % 2:
                    full(dve, "lin", tile)
                    taken(dve, "lin", tile - 1)
                    product = silu_g[:, nth % 2, 0:width]
                    frees(dve.tensor_tensor(product, lin[:, tile % RING, 0:width], product, ALU.mult), "lin", tile)
                    nth += 1
                elif stage[-3:] == "out":
                    if stage[4] == "b":
                        taken(dve, "lin", lin_of[f"ffn{n}a_out"] + u)
                    gated_tile(dve, tile, u, n, 5, width // L)
            for m in range(RING):
                taken(dve, "lin", lin_of[f"ffn{n}b_out"] + KT - 1 - m)

        def convolve(dve, own, n):
            tile = lin_of["ssm_in"] + n
            full(dve, "lin", tile)
            if n < 8:
                dst = bm[:, n, :].rearrange("p (a b) -> p a b", a=2)
            elif n < 24:
                dst = xs_pair[:, n - 8]
            else:
                dst = cm[:, n - 24, :].unsqueeze(1)
            src = lin[:, tile % RING, 0:L * dst.shape[1]].rearrange("p (a b) -> p a b", b=L)
            w = lambda m: conv_w[:, n, m:m + 1]
            own.link(dve.tensor_scalar(dst, src, w(1), w(3), ALU.mult, ALU.add))
            own.link(dve.scalar_tensor_tensor(out=dst[:, :, 1:L], in0=src[:, :, 0:L - 1], scalar=w(0),
                                              in1=dst[:, :, 1:L], op0=ALU.mult, op1=ALU.add))
            frees(dve.scalar_tensor_tensor(out=dst[:, :, 0:L - 1], in0=src[:, :, 1:L], scalar=w(2),
                                           in1=dst[:, :, 0:L - 1], op0=ALU.mult, op1=ALU.add), "lin", tile)

        def second_block_vector(dve, own):
            tt, ts, stt = dve.tensor_tensor, dve.tensor_scalar, dve.scalar_tensor_tensor
            dve.wait_ge(sig("ada_summed"), 48)
            own.link(tt(mod[:].rearrange("p a b c -> p (a b) c"), modp[:, L:L + 192].rearrange("p (a b) -> p a b", b=2),
                        each(modb[:].rearrange("p a b -> p (a b)"), 2), ALU.add))
            own.mark(dve.tensor_copy(nsink2[:, 0, :], nsink2_in[:]))
            own.mark(ts(nsink2[:, 1, :], nsink2_in[:], -1.0, None, ALU.mult))
            modulated(dve, own, 2, 2 * L, 0, 0)
            dve.wait_ge(sig("at_in"), 48)
            own.mark(dve.tensor_copy(ident_b, ident[:]))
            dve.tensor_copy(mask_b2, mask2).then_inc(sig("masks2"), 1)
            for n in (0, 1, 2, 3, 4):
                tile = aux_of["rope"] + n
                part = (k2 if n == 0 else q2[:, 2 * n - 2:2 * n])[:, :, 0:L]
                full(dve, "aux", tile)
                frees(tt(rope_tmp, aux[:, tile % AUX].rearrange("p (a b) -> p a b", a=2), twice(rope_cs[:, 1, :]),
                         ALU.mult), "aux", tile)
                own.link(tt(part, part, twice(rope_cs[:, 0, :]), ALU.mult))
                taken(dve, "aux", tile)
                own.link(tt(part, part, rope_tmp, ALU.add))
            dve.sem_inc(sig("roped"), 1)
            for i in range(AT_HEADS + 3):
                if i < AT_HEADS:
                    for n in range(3):
                        tile = score_tile(i, n)
                        full(dve, "aux", tile)
                        if n < 2:
                            own.mark(dve.tensor_reduce(stat2[:, 0, i, n:n + 1], aux[:, tile % AUX, :], AX_X, ALU.max))
                        else:
                            own.link(dve.tensor_reduce(
                                stat2[:, 0, i, 2:4], aux[:, tile % AUX].rearrange("p (a b) -> p a b", a=2), AX_X, ALU.max))
                    ts(stat2[:, 1, i, :], stat2[:, 0, i, :], -AT_SCALE, nsink2[:, 1, i:i + 1], ALU.mult, ALU.min)\
                        .then_inc(sig("maxima2"), 1)
                if 1 <= i <= AT_HEADS:
                    h = i - 1
                    dve.wait_ge(sig("exps2"), h + 1)
                    own.link(tt(stat2[:, 4, h, :], stat2[:, 2, h, :], stat2[:, 3, h, :], ALU.add))
                    own.link(dve.reciprocal(stat2[:, 5, h, :], stat2[:, 4, h, :]))
                    for n, (part, cols) in enumerate(((0, slice(0, 2 * L)), (1, slice(0, 2 * L)),
                                                      (2, slice(0, L)), (2, slice(L, 2 * L)))):
                        p = p2[:, h % 3, part, cols]
                        ins = ts(p, p, stat2[:, 5, h, n:n + 1], None, ALU.mult)
                    ins.then_inc(sig("probs2"), 1)
                if i >= 4 and i % 2 == 0:
                    n = i // 2 - 2
                    tile = lin_of["attn"] + n
                    full(dve, "lin", tile)
                    frees(dve.tensor_copy(q2[:, n, :], lin[:, tile % RING, :]), "lin", tile)
            gated_add(dve, own, "w_o", 0, 2, 2)
            for u in range(W_UNITS):
                weights_lo(dve, "ffn0a_in", u)
            modulated(dve, own, 3, 2 * L, 0, 3, 0)
            ffn_vector(dve, 0, 2 * L)
            weights_lo(dve, "ssm_dt", 0)
            weights_lo(dve, "ssm_in", 0)
            modulated(dve, own, 4, 2 * L, 1, 0, 1)
            weights_lo(dve, "ssm_in", 1)
            tile = lin_of["ssm_dt"]
            full(dve, "lin", tile)
            frees(ts(dt2, lin[0:64, tile % RING, :], dt_cols[:, 0:1], None, ALU.add), "lin", tile)
            taken(dve, "lin", tile)
            stt(out=dt_tmp, in0=dt2, scalar=-1.0, in1=dt2, op0=ALU.mult, op1=ALU.max).then_inc(sig("dt_abs"), 1)
            weights_lo(dve, "ssm_in", 2)
            dve.wait_ge(sig("dt_exp"), 1)
            own.mark(ts(dt2, dt2, 0.0, None, ALU.max))
            own.link(ts(da, dt_tmp, 1.0, None, ALU.add))
            own.mark(tt(dt2, dt2, dt_tmp2, ALU.add))
            own.link(ts(dt_tmp3, da, 1.0, None, ALU.subtract))
            own.link(tt(dt_tmp, dt_tmp, dt_tmp3, ALU.subtract))
            own.link(dve.reciprocal(da, da))
            own.link(tt(da, da, dt_tmp, ALU.mult))
            own.link(tt(dt2, dt2, da, ALU.add))
            own.link(ts(da, dt2, a_neg, -1.0, ALU.mult, ALU.mult))
            weights_lo(dve, "ssm_in", 3)
            dve.wait_ge(sig("ssm_in"), 32)
            convolve(dve, own, 0)
            convolve(dve, own, 1)
            one = ones[0:64, 0:1].to_broadcast([64, L])
            own.mark(dve.tensor_tensor_scan(rows_g[0:64], one, da[:, 0:L], 0.0, ALU.mult, ALU.add))
            own.link(dve.tensor_tensor_scan(dt_tmp[:, L:2 * L], one, da[:, L:2 * L], 0.0, ALU.mult, ALU.add))
            own.mark(dve.tensor_copy(tot[:, 0:1], rows_g[0:64, L - 1:L]))
            own.link(dve.tensor_copy(tot[:, 1:2], dt_tmp[:, 2 * L - 1:2 * L]))
            back = slice(32, 64)
            own.mark(ts(rows_g[back], rows_g[back], -1.0, tot[back, 0:1], ALU.mult, ALU.add))
            own.link(ts(dt_tmp[back, L:2 * L], dt_tmp[back, L:2 * L], -1.0, tot[back, 1:2], ALU.mult, ALU.add))
            own.mark(tt(rows_g[back], rows_g[back], da[back, 0:L], ALU.add))
            tt(dt_tmp[back, L:2 * L], dt_tmp[back, L:2 * L], da[back, L:2 * L], ALU.add).then_inc(sig("dt_summed"), 1)
            for n in range(2, 46):
                weights_lo(dve, "ssm_in", n + 2)
                if n < 32:
                    convolve(dve, own, n)
                if n == 4:
                    dve.wait_ge(sig("dt_weights"), 1)
                    tt(dt2[:, L:2 * L], dt_tmp[:, L:2 * L], dt2[:, L:2 * L], ALU.mult).then_inc(sig("dt_rows"), 1)
            turned_copies(dve, "bc_tok", 4, bc_tok, 2, 1, dve.tensor_copy)
            turned_copies(dve, "xc_tok", 8, xc_tok, 4, 1, dve.tensor_copy)
            for n in range(AUX):
                taken(dve, "aux", aux_of["xc_tok"] + 7 - n)
            taken(dve, "aux", aux_of["ssm_rows"])
            for g in range(GROUPS):
                if g >= 1:
                    full(dve, "aux", aux_of["states"] + g - 1)
                for d in range(2):
                    for qt in range(QT):
                        heads = cols_g[:, 2, qt, d * 32 + 4 * g:d * 32 + 4 * g + 4]
                        ins = tt(xw[:, d, qt].rearrange("p (a b) -> p a b", a=4),
                                 xc_tok[:, qt, g * L:(g + 1) * L].rearrange("p (a b) -> p a b", a=4),
                                 each(heads, 64), ALU.mult)
                ins.then_inc(sig("x_weighted"), 1)
            turned_copies(dve, "x_tok", 8, x_tok, 4, 1, dve.tensor_copy)

            def y_out(n):
                tile = lin_of["ssm_y"] + n
                full(dve, "lin", tile)
                frees(stt(out=ys[:, n], in0=ys[:, n], scalar=ssm_cols[:, 0, n:n + 1], in1=lin[:, tile % RING, 0:L],
                          op0=ALU.mult, op1=ALU.add), "lin", tile)
                taken(dve, "lin", tile)
                return tt(ys[:, n], ys[:, n], zs[:, n], ALU.mult)

            parts = ((0, 0, 0, L, 0), (0, 1, P, L, L), (1, 0, 0, P, 3 * P), (1, 1, 0, L, 4 * P))
            for i in range(DT_ + 3):
                if i < DT_ and i % 2 == 0:
                    g = i // 2
                    tile = cb_tile(g)
                    full(dve, "aux", tile)
                    c, products = cb[:, g % 2], aux[:, tile % AUX]
                    if g == 0:
                        for n in range(AUX):
                            taken(dve, "aux", aux_of["states"] + GROUPS - 1 - n)
                    own.mark(tt(c[:, 0, 0:P], products[:, 0:P], tri[:, 0], ALU.mult))
                    own.mark(dve.tensor_copy(c[:, 0, P:L], products[:, P:L]))
                    own.mark(tt(c[:, 1, 0:P], products[:, 3 * P:4 * P], tri[:, 0], ALU.mult))
                    own.mark(tt(c[:, 1, P:L], products[:, 0:P], tri[:, 1], ALU.mult))
                    own.mark(dve.tensor_copy(c[:, 2, 0:P], products[:, L:3 * P]))
                    frees(tt(c[:, 2, P:L], products[:, 3 * P:4 * P], tri[:, 1], ALU.mult), "aux", tile)
                for h in range(2 * i, 2 * i + 2) if i < DT_ else ():
                    tile = bc_tile(h)
                    full(dve, "aux", tile)
                    if i >= 3:
                        full(dve, "lin", lin_of["ssm_y"] + i - 3)
                    for d, qt, lo_, hi_, at in parts:
                        ins = ts(decay[i % 3][:, h % 2, at:at + hi_ - lo_], aux[:, tile % AUX, d * L + lo_:d * L + hi_],
                                 cols_g[:, 0, qt, d * 32 + h:d * 32 + h + 1], 0.0, ALU.subtract, ALU.min)
                    ins.then_inc(sig("gaps"), 1)
                for h in range(2 * i - 2, 2 * i) if 1 <= i <= DT_ else ():
                    taken(dve, "aux", cb_tile(h // 4))
                    dve.wait_ge(sig("decays"), h + 1)
                    for d, qt, lo_, hi_, at in parts:
                        m = decay[(i - 1) % 3][:, h % 2, at:at + hi_ - lo_]
                        ins = stt(out=m, in0=m, scalar=cols_g[:, 1, qt, d * 32 + h:d * 32 + h + 1],
                                  in1=cb[:, h // 4 % 2, at // L, at % L:at % L + hi_ - lo_], op0=ALU.mult, op1=ALU.mult)
                    ins.then_inc(sig("mixed"), 1)
                if 3 <= i < DT_ + 2:
                    y_out(i - 3)
            y_out(DT_ - 1).then_inc(sig("y_gated"), 1)
            for n in range(3):
                taken(dve, "aux", aux_of["y_norm"] + 3 - n)
            own.link(dve.reciprocal(y_rs, y_rs))
            for n in range(DT_):
                ins = stt(out=ys[:, n], in0=ys[:, n], scalar=ssm_cols[:, 1, n:n + 1], in1=y_rs[:, n // 2],
                          op0=ALU.mult, op1=ALU.mult)
            ins.then_inc(sig("y_normed"), 1)
            gated_add(dve, own, "ssm_out", 1, 2, 1)
            for u in range(W_UNITS):
                weights_lo(dve, "ffn1a_in", u)
            modulated(dve, own, 5, L, 1, 3, 2)
            ffn_vector(dve, 1, L)
            normed(dve, 6, L, lambda kt, s: g2[:, 4, kt:kt + 1])

        @block.scalar
        def _(act):
            own = Count(act, sig("act_own"))
            act.dma_start(ident[:], t["ident"]).then_inc(sig("norm_in"), 16)
            act.dma_start(gcol[:], t["gcol"]).then_inc(sig("norm_in"), 16)
            copies(act, "bias", EV_HEADS, lambda ps: ps[:, 0:3 * P], lambda h: table[:, h, :])
            act.wait_ge(sig("x_in"), 16)
            act.wait_ge(sig("made"), 1)
            act_norm(act, 0, L)
            act.wait_ge(sig("s5_in"), 32)
            act.activation(par[:, 3, :], par[:, 0, :], ACT.Exp).then_inc(sig("s5_dt"), 1)
            act.wait_ge(sig("s5_phase"), 1)
            own.mark(act.activation(par[:, 8, :], par[:, 4, :], ACT.Exp))
            own.mark(act.activation(par[:, 9, :], par[:, 6, :], ACT.Sin))
            act.activation(par[:, 10, :], par[:, 7, :], ACT.Sin, scale=-1.0, bias=half_pi[:])\
                .then_inc(sig("s5_trig"), 1)
            into = [u[:, n] for n in range(4)] + [ka, va] + [qa[:, n] for n in range(4)] + \
                [gate_a[:, n] for n in range(4)] + [gate_b[:, n] for n in range(4)]
            for n, dst in enumerate(into):
                tile = lin_of["ev_in"] + n
                full(act, "lin", tile)
                frees(act.activation(dst, lin[:, tile % RING, 0:L], ACT.Silu if n >= 10 else ACT.Copy), "lin", tile)
                if 2 <= n < 10:
                    for j in range(2 * (n - 2), 2 * (n - 2) + 2):
                        act.wait_ge(sig("turns"), j + 1)
                        own.mark(act.activation(cos_t[:, j, :], cos_t[:, j, :], ACT.Sin, scale=-TWO_PI,
                                                bias=half_pi[:]))
                        act.activation(sin_t[:, j, :], sin_t[:, j, :], ACT.Sin, scale=TWO_PI * (1 - 2e-7))\
                            .then_inc(sig("phases"), 1)
            act.wait_ge(sig("const_in"), 224)
            act.activation(sc_c[:], sc_c[:], ACT.Silu).then_inc(sig("silu_c"), 1)
            copies(act, "s5_bb", 2, lambda ps: ps, lambda n: bb_t[:, n].rearrange("p a b -> p (a b)"))
            taken(act, "lin", lin_of["ev_in"] + 17)
            act.wait_ge(sig("table_out"), 16)
            own.mark(act.activation(sq0[:, 0, :], ka, ACT.Square))
            act.activation(sq0[:, 1:5, :], qa, ACT.Square).then_inc(sig("squares_qk0"), 1)
            roots(act, "qk_norm0", [2 * L, 2 * L, L], 1.0 / 64,
                  lambda n: r0[:, 2 * n:min(2 * n + 2, 5), :].rearrange("p a b -> p (a b)"))
            copies(act, "v_tok0", 1, lambda ps: ps[:, 0:L], lambda n: v_tok.rearrange("p a b -> p (a b)"))
            ada_copies(act, 0, 4)
            softmax_exps(act, own, 0, (lg0, lg1), small, True)
            copies(act, "probs0", EV_HEADS, lambda ps: ps[:, 0:3 * P], lambda h: pt[:, h, :])
            ada_copies(act, 4, 20)
            taken(act, "lin", lin_of["s5_y"] + 3)
            act.activation(u, u, ACT.Gelu_apprx_tanh).then_inc(sig("s5_gelu"), 1)
            for n in range(4):
                tile = lin_of["glu"] + 2 * n + 1
                full(act, "lin", tile)
                frees(act.activation(qa[:, n], lin[:, tile % RING, 0:L], ACT.Sigmoid, bias=glu_b[:, 4 + n:5 + n]),
                      "lin", tile)
            act_norm(act, 1, L, "ev_out")
            into = [ki] + [qi[:, n] for n in range(4)] + [k1[:, n] for n in range(2)] + \
                [v1[:, n] for n in range(2)] + [q1[:, n] for n in range(8)] + [gate1[:, n] for n in range(8)]
            for n, dst in enumerate(into):
                tile = lin_of["od_ki"] + n
                full(act, "lin", tile)
                frees(act.activation(dst, lin[:, tile % RING, 0:L], ACT.Silu if n >= 17 else ACT.Copy), "lin", tile)
                if n >= 6 and n % 2 == 0 and (n - 6) // 2 < 6:
                    m = (n - 6) // 2
                    tile = aux_of["index"] + m
                    full(act, "aux", tile)
                    if m >= 2:
                        act.wait_ge(sig("rel_used"), m - 1)
                    frees(act.activation(rel[:, m % 2], aux[:, tile % AUX], ACT.Relu, scale=64 ** -0.5), "aux", tile)
            taken(act, "lin", lin_of["od_in"] + 23)
            own.mark(act.activation(sq1[:, 0:2, :], k1, ACT.Square))
            act.activation(sq1[:, 2:10, :], q1, ACT.Square).then_inc(sig("squares_qk1"), 1)
            roots(act, "kq_norm1", [2 * L] * 5, 1.0 / P,
                  lambda n: r1[:, 2 * n:2 * n + 2, :].rearrange("p a b -> p (a b)"))
            copies(act, "v_tok1", 1, lambda ps: ps, lambda n: v_tok1.rearrange("p a b -> p (a b)"))
            ada_copies(act, 24, 24)
            softmax_exps(act, own, 1, (lh0, lh1), small, False)
            copies(act, "probs1", OD_HEADS, lambda ps: ps[:, 0:3 * P], lambda h: pt1[:, h, :])
            second_block_scalar(act, own)

        @block.vector
        def _(dve):
            own = Count(dve, sig("dve_own"))
            tt, ts, stt = dve.tensor_tensor, dve.tensor_scalar, dve.scalar_tensor_tensor
            dve.wait_ge(sig("norm_in"), 32)
            normed(dve, 0, L, lambda kt, s: gcol[:, 0, kt:kt + 1])
            dve.wait_ge(sig("const_in"), 224)
            (log_dt, a_re, a_im, dt, z, turn, phase, phase_abs, mag, sin1, cos1, hi, lo, k, den, n_re, n_im,
             f_re, f_im, tmp, tmp2) = (par[:, n, :] for n in range(21))
            dve.wait_ge(sig("s5_dt"), 1)
            own.mark(tt(z, a_re, dt, ALU.mult))
            own.link(tt(phase, a_im, dt, ALU.mult))
            own.link(ts(k, phase, 1.0 / TWO_PI, ROUND, ALU.mult, ALU.add))
            own.link(ts(k, k, ROUND, None, ALU.subtract))
            for part in (PI2_A, PI2_B, PI2_C):
                own.link(stt(out=phase, in0=k, scalar=-part, in1=phase, op0=ALU.mult, op1=ALU.add))
            own.link(ts(phase, phase, math.pi * (1 - 1e-7), -math.pi * (1 - 1e-7), ALU.min, ALU.max))
            own.link(ts(turn, phase, 1.0 / TWO_PI, None, ALU.mult))
            stt(out=phase_abs, in0=phase, scalar=-1.0, in1=phase, op0=ALU.mult, op1=ALU.max).then_inc(sig("s5_phase"), 1)
            own.link(ts(tmp, turn, 4097.0, None, ALU.mult))
            own.link(tt(tmp2, tmp, turn, ALU.subtract))
            own.link(tt(hi, tmp, tmp2, ALU.subtract))
            own.link(tt(lo, turn, hi, ALU.subtract))
            for j in range(SSM_TILES):
                frac, whole = sin_t[:, j, :], cos_t[:, j, :]
                own.link(ts(frac, steps, hi[:, j:j + 1], None, ALU.mult))
                own.link(ts(whole, frac, ROUND, ROUND, ALU.add, ALU.subtract))
                own.link(tt(frac, frac, whole, ALU.subtract))
                own.link(stt(out=frac, in0=steps, scalar=lo[:, j:j + 1], in1=frac, op0=ALU.mult, op1=ALU.add))
                own.link(ts(whole, frac, ROUND, ROUND, ALU.add, ALU.subtract))
                own.link(tt(frac, frac, whole, ALU.subtract))
                stt(out=whole, in0=frac, scalar=-1.0, in1=frac, op0=ALU.mult, op1=ALU.max).then_inc(sig("turns"), 1)
            dve.wait_ge(sig("s5_trig"), 1)
            own.mark(tt(n_re, mag, cos1, ALU.mult))
            own.mark(tt(n_im, mag, sin1, ALU.mult))
            own.mark(tt(den, a_re, a_re, ALU.mult))
            own.link(tt(tmp, a_im, a_im, ALU.mult))
            own.mark(ts(n_re, n_re, 1.0, None, ALU.subtract))
            own.link(tt(den, den, tmp, ALU.add))
            own.mark(dve.reciprocal(den, den))
            own.mark(tt(f_re, n_re, a_re, ALU.mult))
            own.mark(tt(tmp, n_im, a_im, ALU.mult))
            own.mark(tt(f_im, n_im, a_re, ALU.mult))
            own.link(tt(tmp2, n_re, a_im, ALU.mult))
            own.mark(tt(f_re, f_re, tmp, ALU.add))
            own.link(tt(f_im, f_im, tmp2, ALU.subtract))
            own.mark(tt(f_re, f_re, den, ALU.mult))
            own.link(tt(f_im, f_im, den, ALU.mult))
            bt = s5w[:, 0].rearrange("p a b -> p (a b)")[:, 0:256].rearrange("p (a b) -> p a b", a=16)
            for part, (f1, b1, f2, b2, op) in enumerate(((f_re, 0, f_im, 1, ALU.subtract), (f_re, 1, f_im, 0, ALU.add))):
                s5p = s5t[:, part, 0:256].rearrange("p (a b) -> p a b", a=16)
                own.mark(tt(bt, each(f1, 16), b_in[:, b1], ALU.mult))
                own.link(tt(s5p, each(f2, 16), b_in[:, b2], ALU.mult))
                for n in range(2):
                    rows = slice(64 * n, 64 * n + 64)
                    own.link(tt(bd[rows, part, :, 16 * n:16 * n + 16], bt[rows], s5p[rows], op))
            dve.wait_ge(sig("c_in"), 64)
            ts(c_bd[:, 1], c_bd[:, 1], -1.0, None, ALU.mult).then_inc(sig("bd_ready"), 1)
            dve.wait_ge(sig("table_back"), 16)
            own.link(tt(bias_a, bias_b, mask_a.unsqueeze(1).to_broadcast([P, EV_HEADS, L]), ALU.add))
            own.link(tt(bias_b, bias_b, mask_b.unsqueeze(1).to_broadcast([P, EV_HEADS, L]), ALU.add))
            taken(dve, "aux", aux_of["qk_norm0"] + 2)
            own.link(dve.reciprocal(r0, r0))
            stt(out=ka, in0=ka, scalar=qk_g[:, 1:2], in1=r0[:, 0, :], op0=ALU.mult, op1=ALU.mult)
            stt(out=qa, in0=qa, scalar=qk_g[:, 0:1], in1=r0[:, 1:5, :], op0=ALU.mult, op1=ALU.mult)\
                .then_inc(sig("qk0_ready"), 1)
            scaled_logits(dve, own, 0, bias_a, (lg0, lg1), 64 ** -0.5)
            maxima(dve, own, 0, (lg0, lg1), small, sink[:])
            probabilities(dve, own, 0, (lg0, lg1), small, True)
            for n in range(4):
                tile = aux_of["out0"] + n
                full(dve, "aux", tile)
                frees(tt(cat[:, n, :], aux[:, tile % AUX, 0:L], gate_a[:, n, :], ALU.mult), "aux", tile)

            dve.wait_ge(sig("phases"), SSM_TILES)
            for j in range(SSM_TILES):
                p = j % 2
                tile = aux_of["s5_bu"] + j
                bu = aux[:, tile % AUX].rearrange("p (a b) -> p a b", a=2)
                w, ti, z2 = s5w[:, p], s5t[:, p].rearrange("p (a b) -> p a b", a=2), s5z[:, p]
                full(dve, "aux", tile)
                own.mark(tt(w, bu, twice(cos_t[:, j, :]), ALU.mult))
                frees(tt(ti, bu, twice(sin_t[:, j, :]), ALU.mult), "aux", tile)
                taken(dve, "aux", tile)
                own.mark(tt(w[:, 0], w[:, 0], ti[:, 1], ALU.add))
                own.link(tt(w[:, 1], w[:, 1], ti[:, 0], ALU.subtract))
                if j >= 2:
                    dve.wait_ge(sig("x_states"), j - 1)
                decay = mag[:, j:j + 1].to_broadcast([P, L])
                own.mark(dve.tensor_tensor_scan(z2[:, 0], decay, w[:, 0], 0.0, ALU.mult, ALU.add))
                dve.tensor_tensor_scan(z2[:, 1], decay, w[:, 1], 0.0, ALU.mult, ALU.add)\
                    .then_inc(sig("z_ready"), 1)
            for n in range(4):
                tile = lin_of["s5_y"] + n
                dve.wait_ge(sig("s5_used"), 4 * (n + 1))
                frees(stt(out=u[:, n], in0=u[:, n], scalar=d_col[:, n:n + 1], in1=lin[:, tile % RING, 0:L],
                          op0=ALU.mult, op1=ALU.add), "lin", tile)
                taken(dve, "lin", tile)
            for n in range(4):
                tile = lin_of["glu"] + 2 * n
                full(dve, "lin", tile)
                taken(dve, "lin", tile + 1)
                frees(stt(out=qa[:, n], in0=lin[:, tile % RING, 0:L], scalar=glu_b[:, n:n + 1], in1=qa[:, n],
                          op0=ALU.add, op1=ALU.mult), "lin", tile)
                taken(dve, "lin", tile)
                tt(cat[:, 4 + n, :], qa[:, n], gate_b[:, n], ALU.mult).then_inc(sig("cat_ready"), 1)

            def add_to_x(name):
                for n in range(KT):
                    tile = lin_of[name] + n
                    full(dve, "lin", tile)
                    frees(tt(xres[:, n, 0:L], lin[:, tile % RING, 0:L], xres[:, n, 0:L], ALU.add), "lin", tile)
                    taken(dve, "lin", tile)

            add_to_x("ev_out")
            normed(dve, 1, L, lambda kt, s: gcol[:, 1, kt:kt + 1])
            tile = aux_of["wi"]
            full(dve, "aux", tile)
            frees(ts(wi, aux[:, tile % AUX, 0:16].rearrange("p (a b) -> p a b", a=2), OD_HEADS ** -0.5, None,
                     ALU.mult), "aux", tile)
            taken(dve, "aux", tile)
            own.mark(dve.tensor_copy(idx[:, 0, 0:P], mask_b[:, P:L]))
            own.link(dve.tensor_copy(idx[:, 1, :], mask_b))
            for m in range(6):
                taken(dve, "aux", aux_of["index"] + m)
                qt, heads, width = index_heads(m)
                for n, h in enumerate(heads):
                    ins = stt(out=idx[:, qt, 0:width], in0=rel[:, m % 2, n * width:(n + 1) * width],
                              scalar=wi[:, qt, h:h + 1], in1=idx[:, qt, 0:width], op0=ALU.mult, op1=ALU.add)
                    if n < len(heads) - 1:
                        own.link(ins)
                ins.then_inc(sig("rel_used"), 1)
                dve.wait_ge(sig("rel_used"), m + 1)
            for r in range(TOPK // 8):
                for qt, width in ((0, P), (1, L)):
                    own.mark(dve.max(top[:, qt, :], idx[:, qt, 0:width]))
                own.settle()
                for qt, width in ((0, P), (1, L)):
                    own.mark(dve.match_replace(idx[:, qt, 0:width], top[:, qt, :], idx[:, qt, 0:width], TAKEN))
                own.settle()
            for qt, width in ((0, P), (1, L)):
                own.mark(ts(sel[:, qt, 0:width], idx[:, qt, 0:width], TAKEN / 2, NEG, ALU.is_gt, ALU.mult))
            taken(dve, "aux", aux_of["kq_norm1"] + 4)
            own.link(dve.reciprocal(r1, r1))
            stt(out=k1, in0=k1, scalar=qk_g[:, 3:4], in1=r1[:, 0:2, :], op0=ALU.mult, op1=ALU.mult)
            stt(out=q1, in0=q1, scalar=qk_g[:, 2:3], in1=r1[:, 2:10, :], op0=ALU.mult, op1=ALU.mult)\
                .then_inc(sig("qk1_ready"), 1)
            scaled_logits(dve, own, 1, bias_b, (lh0, lh1), P ** -0.5)
            own.mark(tt(lh0, lh0, sel[:, 0, 0:P].unsqueeze(1).to_broadcast([P, OD_HEADS, P]), ALU.add))
            own.link(tt(lh1, lh1, sel[:, 1, :].unsqueeze(1).to_broadcast([P, OD_HEADS, L]), ALU.add))
            maxima(dve, own, 1, (lh0, lh1), small, None)
            probabilities(dve, own, 1, (lh0, lh1), small, False)
            for n in range(8):
                tile = aux_of["out1"] + n
                full(dve, "aux", tile)
                frees(tt(q1[:, n, :], aux[:, tile % AUX, 0:L], gate1[:, n, :], ALU.mult), "aux", tile)
            add_to_x("od_out")
            second_block_vector(dve, own)

        @block.tensor
        def _(pe):
            mm = nc.tensor.matmul

            def begin(banks, tile):
                sems_, n = (lin_free, RING) if banks == "lin" else (aux_free, AUX)
                if isinstance(tile, int) and tile < n:
                    return
                pe.wait_ge(sems_[tile % n], tile // n)

            def fills(ins, banks):
                ins.then_inc(sig(banks + "_full"), 1)

            def linear(name, stage, tiles, kts, rhs, width=L, m=P, between=None, norm=None):
                count = dict((x, y) for x, y, _ in STREAM)[name]
                first, tile0 = block_of[name], lin_of[stage]

                def one(i, k):
                    b = first + k
                    pe.wait_ge(w_in[b % RING], (i + (b // RING + 1)) * 16)
                    for j in range(tiles):
                        tile = tile0 + k * tiles + j
                        bank = tile % RING
                        if not isinstance(i, int) or tile + i * RING * tiles >= RING:
                            pe.wait_ge(lin_free[bank], i * tiles + tile // RING)
                        for kt in range(kts):
                            at = (j * kts + kt) * m
                            if norm is not None and isinstance(i, int) and i == k == j == 0:
                                pe.wait_ge(sig("hn_ready"), KT * norm + kt + 1)
                            ins = mm(lin[0:m, bank, 0:width], ring[:, b % RING, at:at + m], rhs(kt),
                                     start=kt == 0, stop=kt == kts - 1)
                        fills(ins, "lin")
                    if between is not None:
                        between(k + RING * i)

                if between is not None:
                    for n in range(count):
                        one(n // RING, n % RING)
                else:
                    rounds(pe, count, one)

            def split_unit(name, u, kts, x, width, m=P, waits=None):
                parts, _, _ = unit(name, u)
                tile = lin_of[name] + u
                begin("lin", tile)
                pe.wait_ge(sig("w_low"), unit_of[name] + u + 1)
                for kt in range(kts):
                    if waits is not None:
                        pe.wait_ge(sig(waits[0]), waits[1] + kt + 1)
                    hi, lo = (parts[:, part, kt * m:(kt + 1) * m] for part in range(2))
                    x_hi, x_lo = x(kt)
                    mm(lin[0:m, tile % RING, 0:width], hi, x_hi, start=kt == 0, stop=False)
                    mm(lin[0:m, tile % RING, 0:width], hi, x_lo, start=False, stop=False)
                    ins = mm(lin[0:m, tile % RING, 0:width], lo, x_hi, start=False, stop=kt == kts - 1)
                fills(ins, "lin")

            def split_linear(name, kts, x, width, waits=None):
                for u in range(dict(SPLIT)[name]):
                    split_unit(name, u, kts, x, width, waits=waits if u == 0 else None)

            ada_at = [0]

            def ada_groups(n):
                pe.wait_ge(sig("ada_copied"), n + 1)
                for j in range(2):
                    at = L + (2 * n + j) * 2
                    ins = mm(modp[:, at:at + 2], ada_sb[:, j * P:(j + 1) * P], group_sum[:], start=True, stop=True)
                ins.then_inc(sig("ada_summed"), 1)

            def ada(blocks):
                for n in range(ada_at[0], ada_at[0] + blocks):
                    b = block_of["ada0"] + n if n < 24 else block_of["ada1"] + n - 24
                    if n == 0:
                        pe.wait_ge(sig("silu_c"), 1)
                    else:
                        pe.wait_ge(sig("ada_copied"), n)
                    pe.wait_ge(w_in[b % RING], 16 * (b // RING + 1))
                    for kt in range(KT):
                        rows = slice(32 * (kt % 4), 32 * (kt % 4) + 32)
                        ins = mm(modp[rows, 0:L], sc_c[:, kt, :], ring[:, b % RING, kt * L:(kt + 1) * L],
                                 start=kt < 4, stop=kt >= 4)
                    ins.then_inc(sig("ada_used"), 1)
                    if n:
                        ada_groups(n - 1)
                ada_at[0] += blocks

            def sums(name, mat, src, tiles, width):
                for n, parts in enumerate(tiles):
                    tile = aux_of[name] + n
                    begin("aux", tile)
                    for m, terms in enumerate(parts):
                        for q, kt in enumerate(terms):
                            ins = mm(aux[:, tile % AUX, m * width:(m + 1) * width], mat[:], src(kt),
                                     start=q == 0, stop=q == len(terms) - 1)
                    fills(ins, "aux")

            def norm(k, width):
                tile = aux_of[f"norm{k}"]
                begin("aux", tile)
                pe.wait_ge(sig("square_sums"), k + 1)
                for n in range(width // P):
                    ins = mm(aux[:, tile % AUX, n:n + 1], hn[:, 0, n * P:(n + 1) * P], ones[:, 0:1],
                             start=True, stop=True)
                fills(ins, "aux")
                begin("aux", tile + 1)
                pe.wait_ge(sig("rms"), k + 1)
                for n in range(width // P):
                    ins = mm(aux[:, (tile + 1) % AUX, n * P:(n + 1) * P], rcol[:, n:n + 1].to_broadcast([P, P]),
                             ident[:], start=True, stop=True)
                fills(ins, "aux")

            pe.wait_ge(sig("rel_in"), 32)
            for h in range(EV_HEADS):
                tile = aux_of["bias"] + h
                begin("aux", tile)
                fills(mm(aux[:, tile % AUX, 0:3 * P], relb[:, h, :], hot, start=True, stop=True), "aux")
            pe.wait_ge(sig("made"), 1)
            pe.wait_ge(sig("norm_in"), 32)
            norm(0, L)
            linear("ev_in", "ev_in", 2, KT, lambda kt: hn[:, kt, 0:L], norm=0)
            pe.wait_ge(sig("bd_ready"), 1)
            for part in range(2):
                tile = aux_of["s5_bb"] + part
                begin("aux", tile)
                for n in range(4):
                    ins = nc.tensor.transpose(aux[:, tile % AUX, n * P:(n + 1) * P],
                                              bd[:, part, 4 * n:4 * n + 4, :].rearrange("p a b -> p (a b)"), ident[:])
                fills(ins, "aux")
            pe.wait_ge(sig("squares_qk0"), 1)
            sums("qk_norm0", pair, lambda n: sq0[:, n, :], [[[0], [1]], [[2], [3]], [[4]]], L)

            def tokens(name, src, n_src):
                tile = aux_of[name]
                begin("aux", tile)
                for qt in range(QT):
                    for n in range(n_src):
                        at = (qt * n_src + n) * P
                        ins = nc.tensor.transpose(aux[:, tile % AUX, at:at + P], src(n)[:, qt * P:(qt + 1) * P],
                                                  ident[:])
                fills(ins, "aux")

            tokens("v_tok0", lambda n: va, 1)

            def scores(layer, q, k):
                for n in range(6):
                    tile = aux_of[f"scores{layer}"] + n
                    begin("aux", tile)
                    qt, heads, width = (0, range(4 * n, 4 * n + 4), P) if n < 2 else \
                        (1, range(2 * (n - 2), 2 * (n - 2) + 2), L)
                    for m, h in enumerate(heads):
                        ins = mm(aux[:, tile % AUX, m * width:(m + 1) * width], q(h, qt), k(h)[:, 0:width],
                                 start=True, stop=True)
                    fills(ins, "aux")

            def transposed_probs(layer, logits):
                pe.wait_ge(sig(f"probs{layer}"), 1)
                for h in range(8):
                    tile = aux_of[f"probs{layer}"] + h
                    begin("aux", tile)
                    for n, src in enumerate((logits[0][:, h, :], logits[1][:, h, 0:P], logits[1][:, h, P:L])):
                        ins = nc.tensor.transpose(aux[:, tile % AUX, n * P:(n + 1) * P], src, ident[:])
                    fills(ins, "aux")

            half = lambda ap, s: ap[64 * s:64 * s + 64]
            pe.wait_ge(sig("qk0_ready"), 1)
            scores(0, lambda h, qt: half(qa[:, h % 4, qt * P:(qt + 1) * P], h // 4), lambda h: half(ka, h // 4))
            ada(4)
            transposed_probs(0, (lg0, lg1))
            for j in range(4):
                tile = aux_of["out0"] + j
                begin("aux", tile)
                for s in range(2):
                    h = j + 4 * s
                    taken(pe, "aux", aux_of["probs0"] + h)
                    rows = slice(64 * s, 64 * s + 64)
                    mm(aux[rows, tile % AUX, 0:L], v_tok[:, 0, rows], pt[:, h, 0:L], start=True, stop=False)
                    ins = mm(aux[rows, tile % AUX, P:L], v_tok[:, 1, rows], pt[:, h, L:3 * P], start=False, stop=True)
                fills(ins, "aux")
            taken(pe, "aux", aux_of["s5_bb"] + 1)

            def s5_out(j):
                pe.wait_ge(sig("x_states"), j + 1)
                rows = slice(32 * (j % 4), 32 * (j % 4) + 32)
                tile = lin_of["s5_y"] + j // 4
                if j % 4 == 0:
                    begin("lin", tile)
                mm(lin[rows, tile % RING, 0:L], c_bd[:, 0, j, :], s5x[:, j % 2, 0, :], start=True, stop=False)
                mm(lin[rows, tile % RING, 0:L], c_bd[:, 1, j, :], s5x[:, j % 2, 1, :], start=False, stop=True)\
                    .then_inc(sig("s5_used"), 1)

            for j in range(SSM_TILES):
                tile = aux_of["s5_bu"] + j
                begin("aux", tile)
                rows = slice(32 * (j % 4), 32 * (j % 4) + 32)
                for part in range(2):
                    ins = mm(aux[:, tile % AUX, part * L:(part + 1) * L], bb_t[rows, part, j // 4, :],
                             u[rows, j // 4, :], start=True, stop=True)
                fills(ins, "aux")
                ada((j + 1) * 20 // SSM_TILES - j * 20 // SSM_TILES)
                if j >= 2:
                    s5_out(j - 2)
            s5_out(SSM_TILES - 2)
            s5_out(SSM_TILES - 1)
            pe.wait_ge(sig("s5_gelu"), 1)
            linear("glu", "glu", 4, 4, lambda kt: u[:, kt, :])
            pe.wait_ge(sig("cat_ready"), 4)
            linear("ev_out", "ev_out", 2, KT, lambda kt: cat[:, kt, :])
            norm(1, L)
            pe.wait_ge(sig("hn_ready"), 2 * KT)
            b = block_of["od_small"]
            pe.wait_ge(w_in[b % RING], 16 * (b // RING + 1))
            tile = aux_of["wi"]
            begin("aux", tile)
            for qt in range(QT):
                for kt in range(KT):
                    at = KT * P + kt * 8
                    ins = mm(aux[:, tile % AUX, qt * 8:qt * 8 + 8], hn[:, kt, qt * P:(qt + 1) * P],
                             ring[:, b % RING, at:at + 8], start=kt == 0, stop=kt == KT - 1)
            fills(ins, "aux")
            linear("od_small", "od_ki", 1, KT, lambda kt: hn[:, kt, 0:L])

            def index(n):
                if not 2 <= n < 8:
                    return
                m = n - 2
                tile = aux_of["index"] + m
                begin("aux", tile)
                if m == 0:
                    taken(pe, "lin", lin_of["od_in"] + 3)
                qt, heads, width = index_heads(m)
                for q, h in enumerate(heads):
                    ins = mm(aux[:, tile % AUX, q * width:(q + 1) * width],
                             half(qi[:, h // 2, qt * P:(qt + 1) * P], h % 2), half(ki, h % 2)[:, 0:width],
                             start=True, stop=True)
                fills(ins, "aux")

            linear("od_in", "od_in", 2, KT, lambda kt: hn[:, kt, 0:L], between=index)
            pe.wait_ge(sig("squares_qk1"), 1)
            sums("kq_norm1", ones, lambda n: sq1[:, n, :], [[[2 * n], [2 * n + 1]] for n in range(5)], L)
            tokens("v_tok1", lambda n: v1[:, n], 2)
            ada(24)
            ada_groups(47)
            pe.wait_ge(sig("qk1_ready"), 1)
            scores(1, lambda h, qt: q1[:, h, qt * P:(qt + 1) * P], lambda h: k1[:, h // 4, :])
            transposed_probs(1, (lh0, lh1))
            for h in range(OD_HEADS):
                tile = aux_of["out1"] + h
                begin("aux", tile)
                taken(pe, "aux", aux_of["probs1"] + h)
                cols = slice((h // 4) * P, (h // 4 + 1) * P)
                mm(aux[:, tile % AUX, 0:L], v_tok1[:, 0, cols], pt1[:, h, 0:L], start=True, stop=False)
                ins = mm(aux[:, tile % AUX, P:L], v_tok1[:, 1, cols], pt1[:, h, L:3 * P], start=False, stop=True)
                fills(ins, "aux")
            for n in range(AUX):
                taken(pe, "aux", aux_of["out1"] + OD_HEADS - 1 - n)
            linear("od_out", "od_out", 2, KT, lambda kt: q1[:, kt, :])
            both = slice(0, 2 * L)

            norm(2, 2 * L)
            linear("qkv", "qkv", 2, KT, lambda kt: hn[:, kt, :], 2 * L, norm=2)
            pe.wait_ge(sig("at_in"), 48)
            for n in range(RING):
                taken(pe, "lin", lin_of["qkv"] + 11 - n)
            for n in range(5):
                tile = aux_of["rope"] + n
                begin("aux", tile)
                part = (k2 if n == 0 else q2[:, 2 * n - 2:2 * n])[:, :, 0:L]
                fills(mm(aux[:, tile % AUX, :], rope_perm, part, start=True, stop=True), "aux")
            for n in range(2):
                tile = aux_of["v_tok2"] + n
                begin("aux", tile)
                for m in range(4):
                    tok = (2 * n + m // 2) * P
                    ins = nc.tensor.transpose(aux[:, tile % AUX, m * P:(m + 1) * P], v2[:, m % 2, tok:tok + P], ident[:])
                fills(ins, "aux")
            pe.wait_ge(sig("masks2"), 1)
            pe.wait_ge(sig("roped"), 1)
            for i in range(AT_HEADS + 2):
                if i < AT_HEADS:
                    n, s = i // 2, i % 2
                    q, k = half(q2[:, n], s), half(k2[:, n // 4], s)
                    for qt in range(QT):
                        tile = score_tile(i, qt)
                        begin("aux", tile)
                        mm(aux[:, tile % AUX, :], q[:, qt * P:(qt + 1) * P], k, start=True, stop=False)
                        cut = slice((1 - qt) * P, (2 - qt) * P)
                        fills(mm(aux[:, tile % AUX, cut], ident_b, mask_b2[:, qt, :], start=False, stop=True), "aux")
                    tile = score_tile(i, 2)
                    begin("aux", tile)
                    for qt in range(QT):
                        ins = mm(aux[:, tile % AUX, qt * L:(qt + 1) * L], q[:, L + qt * P:L + (qt + 1) * P],
                                 k[:, L:2 * L], start=True, stop=True)
                    fills(ins, "aux")
                if 1 <= i <= AT_HEADS:
                    h = i - 1
                    pe.wait_ge(sig("probs2"), h + 1)
                    for n in range(3):
                        tile = turned_tile(h, n)
                        begin("aux", tile)
                        for m in range(2):
                            for qt in range(QT):
                                src = p2[:, h % 3, qt, (2 * n + m) * P:(2 * n + m + 1) * P] if n < 2 else \
                                    p2[:, h % 3, 2, qt * L + m * P:qt * L + (m + 1) * P]
                                at = m * L + qt * P
                                ins = nc.tensor.transpose(aux[:, tile % AUX, at:at + P], src, ident[:])
                        fills(ins, "aux")
                if i >= 2:
                    h = i - 2
                    n, s = h // 2, h % 2
                    rows = slice(64 * s, 64 * s + 64)
                    cols = slice((n // 4) * P + 64 * s, (n // 4) * P + 64 * s + 64)
                    tile = lin_of["attn"] + n
                    if s == 0:
                        begin("lin", tile)
                    for m in range(3):
                        taken(pe, "aux", turned_tile(h, m))
                    for kt in range(4):
                        mm(lin[rows, tile % RING, 0:L], v_tok2[:, kt, cols],
                           pt2[:, h % 2, kt // 2, (kt % 2) * L:(kt % 2 + 1) * L], start=kt == 0, stop=kt == 3)
                    for m in range(2):
                        ins = mm(lin[rows, tile % RING, L:2 * L], v_tok2[:, 2 + m, cols],
                                 pt2[:, h % 2, 2, m * L:(m + 1) * L], start=m == 0, stop=m == 1)
                    if s == 0:
                        ins.then_inc(sig("attn_even"), 1)
                    else:
                        fills(ins, "lin")
            for n in range(RING):
                taken(pe, "lin", lin_of["attn"] + 7 - n)
            linear("w_o", "w_o", 2, KT, lambda kt: q2[:, kt, :], 2 * L)

            def feed_forward(n, k, width):
                norm(k, width)
                for half_ in range(2):
                    split_linear(f"ffn{n}{'ab'[half_]}_in", KT, lambda kt: (hn_hi[:, kt, 0:width], hn_lo[:, kt, 0:width]),
                                 width, ("hn_ready", KT * k) if half_ == 0 else None)
                    split_linear(f"ffn{n}{'ab'[half_]}_out", FH, lambda kt: (hid_split[:, 0, kt, 0:width],
                                                                          hid_split[:, 1, kt, 0:width]),
                                 width, ("hid_ready", n * FT + half_ * FH))

            feed_forward(0, 3, 2 * L)
            norm(4, 2 * L)
            split_unit("ssm_dt", 0, KT, lambda kt: (hn_hi[:, kt, :], hn_lo[:, kt, :]), 2 * L, 2 * M_HEADS,
                       ("hn_ready", KT * 4))
            for tile in range(48):
                width = 2 * L if tile < 24 else L
                split_unit("ssm_in", tile, KT, lambda kt: (hn_hi[:, kt, 0:width], hn_lo[:, kt, 0:width]), width)
            pe.wait_ge(sig("dt_rows"), 1)
            tile = aux_of["ssm_rows"]
            begin("aux", tile)
            for n, src in enumerate((rows_g[0:64, 0:L], dt2[:, 0:L], dt2[:, L:2 * L])):
                for qt in range(QT):
                    at = (n * QT + qt) * 64
                    ins = nc.tensor.transpose(aux[:, tile % AUX, at:at + 64], src[:, qt * P:(qt + 1) * P],
                                              ident[0:64, 0:64])
            fills(ins, "aux")

            def turn(name, n, per_row, src):
                for q in range(n):
                    tile = aux_of[name] + q
                    begin("aux", tile)
                    for m in range(4):
                        tok = (q // per_row) * P
                        ins = nc.tensor.transpose(aux[:, tile % AUX, m * P:(m + 1) * P],
                                                  src((q % per_row) * 4 + m)[:, tok:tok + P], ident[:])
                    fills(ins, "aux")

            pe.wait_ge(sig("convolved"), 32)
            turn("bc_tok", 4, 2, lambda n: bm[:, n, L:2 * L])
            turn("xc_tok", 8, 4, lambda n: xc[:, n, :])
            for n in range(AUX):
                taken(pe, "aux", aux_of["xc_tok"] + 7 - n)
            for g in range(GROUPS):
                tile = aux_of["states"] + g
                begin("aux", tile)
                pe.wait_ge(sig("x_weighted"), g + 1)
                for d in range(2):
                    for qt in range(QT):
                        ins = mm(aux[:, tile % AUX, d * L:(d + 1) * L], bc_tok[:, qt, g * P:(g + 1) * P],
                                 xw[:, d, qt, :], start=qt == 0, stop=qt == 1)
                fills(ins, "aux")
            turn("x_tok", 8, 4, lambda n: ys[:, n, :])
            for n in range(AUX):
                taken(pe, "aux", aux_of["x_tok"] + 7 - n)
            for i in range(DT_ + 2):
                if i < DT_:
                    g = i // 2
                    if i % 2 == 0:
                        tile = cb_tile(g)
                        begin("aux", tile)
                        for qt in range(QT):
                            ins = mm(aux[:, tile % AUX, qt * L:(qt + 1) * L], bm[:, g, qt * P:(qt + 1) * P],
                                     cm[:, g, :], start=True, stop=True)
                        fills(ins, "aux")
                    for h in (2 * i, 2 * i + 1):
                        tile = bc_tile(h)
                        begin("aux", tile)
                        for d in range(2):
                            one = ident[0:64, d * 32 + h:d * 32 + h + 1].to_broadcast([64, P])
                            ins = mm(aux[:, tile % AUX, d * L:(d + 1) * L], one, rows_g[0:64, :], start=True, stop=True)
                        fills(ins, "aux")
                if i >= 2:
                    n = i - 2
                    tile = lin_of["ssm_y"] + n
                    begin("lin", tile)
                    pe.wait_ge(sig("mixed"), 2 * n + 2)
                    pe.wait_ge(sig("c_decayed"), 2 * n + 2)
                    for key, what in enumerate(("x0", "x1", "x0_back", "x1_back", "state", "state_back")):
                        for e in range(2):
                            h = 2 * n + e
                            m, f = decay[n % 3][:, e], from_start[n % 3][:, e]
                            x0, x1 = (x_tok[:, qt, h * 64:(h + 1) * 64] for qt in range(QT))
                            s0, s1 = (state[:, n // 2, d, (h % 4) * 64:(h % 4 + 1) * 64] for d in range(2))
                            out = lin[64 * e:64 * e + 64, tile % RING, 0:L]
                            dst, mat, src = {
                                "x0": (out, x0, m[:, 0:L]), "x1": (out[:, P:L], x1, m[:, L:3 * P]),
                                "x0_back": (out[:, 0:P], x0, m[:, 3 * P:4 * P]), "x1_back": (out, x1, m[:, 4 * P:6 * P]),
                                "state": (out, s0, f[:, 0]), "state_back": (out, s1, f[:, 1])}[what]
                            ins = mm(dst, mat, src, start=key == 0, stop=key == 5)
                    fills(ins, "lin")
            pe.wait_ge(sig("y_squares"), 1)
            sums("y_norm", ones, lambda n: y_sq[:, n, :], [[[4 * n, 4 * n + 1], [4 * n + 2, 4 * n + 3]] for n in range(4)], L)
            pe.wait_ge(sig("y_normed"), 1)
            linear("ssm_out", "ssm_out", 1, DT_, lambda kt: ys[:, kt, :])
            feed_forward(1, 5, L)
            norm(6, L)


def host_tiles(w, per_block):
    kk, nn = w.shape
    a = w.reshape(kk // P, P, nn // P // per_block, per_block, P)
    return np.ascontiguousarray(a.transpose(2, 1, 3, 0, 4)).reshape(nn // P // per_block, P, -1)


def columns(v):
    a = v.reshape(v.shape[:-1] + (v.shape[-1] // P, P))
    return np.ascontiguousarray(np.moveaxis(a, -1, 0))


def layout(i):
    o = {}
    o["x"] = np.ascontiguousarray(i["x"][0].T.reshape(KT, P, L).transpose(1, 0, 2))
    pair_q = np.concatenate([np.arange(64) + 64 * h for j in range(4) for h in (j, j + 4)])
    w = i["ev_w_in"][0]
    q, k, v, ga, u, gb = np.split(w, np.cumsum([512, 128, 128, 512, 512]), axis=1)
    o["ev_in"] = host_tiles(np.concatenate([u, k, v, q[:, pair_q], ga[:, pair_q], gb], axis=1), 2)
    w = i["ev_w_out"][0]
    o["ev_out"] = host_tiles(np.concatenate([w[:512][pair_q], w[512:]]), 2)
    w = i["ev_glu_w"][0]
    o["glu"] = host_tiles(np.concatenate([w[:, s * 512 + n * P:s * 512 + (n + 1) * P] for n in range(4) for s in range(2)],
                                         axis=1), 4)
    w = i["od_w_in"][0]
    q, k, v, g, qi, ki, wi = np.split(w, np.cumsum([1024, 256, 256, 1024, 512, 64]), axis=1)
    small = host_tiles(np.concatenate([ki, ki], axis=1), 1)[0]
    wi = wi.reshape(KT, P, 8).transpose(1, 0, 2).reshape(P, 64)
    o["od_small"] = np.concatenate([small, wi], axis=1)[None]
    o["od_in"] = host_tiles(np.concatenate([qi, k, v, q, g], axis=1), 2)
    o["od_out"] = host_tiles(i["od_w_out"][0], 2)
    for n in range(2):
        o[f"ada{n}"] = i["ada_w_2"][n].reshape(KT, P, 24, L).transpose(2, 1, 0, 3).reshape(24, P, KT * L)
    o["gcol"] = columns(i["norm_g"])
    o["modb"] = columns(i["ada_b_2"])
    cc = np.stack([i["c_2"][0], i["c_ctx_2"]]).reshape(2, KT, P).transpose(2, 1, 0)
    o["cc"] = np.concatenate([cc, np.zeros((P, KT, 30), np.float32)], axis=2)
    o["group_sum"] = (np.arange(P)[:, None] % 32 == np.arange(2)[None]).astype(np.float32)
    twice_ = lambda g: np.concatenate([g, g])
    o["qk_g"] = np.stack([twice_(i["ev_q_norm_g"][0]), twice_(i["ev_k_norm_g"][0]), i["od_q_norm_g"][0],
                          i["od_k_norm_g"][0]], axis=1)
    o["sink"] = np.repeat(i["ev_sinks"][0][None], P, axis=0)
    by_state = lambda a: a.reshape(SSM_TILES, P).T
    o["s5_par"] = np.stack([by_state(np.repeat(i["ev_ssm_log_dt"][0][:, None], 64, axis=1)),
                            by_state(i["ev_ssm_a_re"][0]), by_state(i["ev_ssm_a_im"][0])], axis=1)
    o["s5_b"] = np.stack([i[f"ev_ssm_b_{n}"][0].reshape(SSM_TILES, P, 16).transpose(1, 0, 2) for n in ("re", "im")], axis=1)
    o["s5_c"] = np.stack([i[f"ev_ssm_c_{n}"][0].transpose(0, 2, 1).reshape(SSM_TILES, P, 16).transpose(1, 0, 2)
                          for n in ("re", "im")], axis=1)
    o["d_col"] = columns(i["ev_ssm_d"][0].reshape(-1))
    o["glu_b"] = columns(i["ev_glu_b"][0])
    o["relb"] = np.repeat(i["rel_bias"][:, :, None], P, axis=2)
    o["ctx"] = np.ascontiguousarray(i["ctx_2"][0].T.reshape(KT, P, L).transpose(1, 0, 2))
    heads = [h for n in range(2) for j in range(4) for h in (8 * n + j, 8 * n + 4 + j)]
    slots = np.concatenate([np.arange(64) + 64 * h for h in heads])
    q, k, v = np.split(i["attn_w_qkv_2"][0], [1024, 1280], axis=1)
    o["qkv"] = host_tiles(np.concatenate([k, v, q[:, slots]], axis=1), 2)
    o["w_o"] = host_tiles(i["attn_w_o_2"][0][slots], 2)
    o["sink2"] = np.repeat(i["attn_sinks_2"][0][heads][None], P, axis=0)
    for n in range(2):
        gate, up = i["ffn_w_gate_2"][n], i["ffn_w_up_2"][n]
        into = host_tiles(
            np.stack([gate.reshape(D, FT, P), up.reshape(D, FT, P)], axis=2).reshape(D, 2 * FF), 2)
        for half, at in (("a", 0), ("b", FH)):
            o[f"ffn{n}{half}_in"] = into[at:at + FH]
            o[f"ffn{n}{half}_out"] = host_tiles(i["ffn_w_down_2"][n][at * P:(at + FH) * P], 1)
    z, xs, bm, cm, dt = np.split(i["ssm_w_in_2"][0], np.cumsum([DI, DI, 1024, 1024]), axis=1)
    o["ssm_in"] = host_tiles(np.concatenate([bm, xs, cm, z], axis=1), 2)
    o["ssm_dt"] = dt.reshape(KT, P, 64).transpose(1, 0, 2).reshape(1, P, KT * 64)
    o["ssm_out"] = host_tiles(i["ssm_w_out_2"][0], 1)
    taps = np.concatenate([i["ssm_conv_w_2"][0], i["ssm_conv_b_2"]])
    xs, bm, cm = np.split(taps, [DI, DI + 1024], axis=1)
    o["conv_w"] = np.moveaxis(columns(np.concatenate([bm, xs, cm], axis=1)), 1, 2)
    o["g2"] = columns(np.stack([i["norm_mix_g_2"][0], i["norm_ffn_g_2"][0], i["norm_mix_g_2"][1],
                                i["norm_ffn_g_2"][1], i["final_norm_g_2"]]))
    o["ssm_cols"] = columns(np.stack([np.repeat(i["ssm_D_2"][0], 64), i["ssm_norm_g_2"][0]]))
    o["dt_cols"] = np.stack([i["ssm_dt_bias_2"][0].reshape(-1), i["ssm_A_log_2"][0].reshape(-1)], axis=1)
    inv = np.float32(10000.0) ** (-np.arange(16, dtype=np.float32) / np.float32(16))
    feature, token = np.arange(P) % 64, np.arange(L)
    place = np.where((feature // 32 == 0)[:, None], (token // 64)[None], (token % 64)[None]).astype(np.float32)
    angle = place * inv[feature % 16][:, None]
    o["rope_cs"] = np.stack([np.cos(angle), np.sin(angle)], axis=1).astype(np.float32)
    perm = np.zeros((P, P), np.float32)
    for m in range(P):
        perm[m + 16 if m % 32 < 16 else m - 16, m] = -1.0 if m % 32 < 16 else 1.0
    o["rope_perm"] = perm
    a, b = np.arange(P)[:, None], np.arange(P)[None]
    o["mask2"] = np.stack([np.where(b <= a, 0.0, NEG), np.where(b >= a, 0.0, NEG)], axis=1).astype(np.float32)
    o["tri"] = np.stack([b >= a, b <= a], axis=1).astype(np.float32)
    o["hot"] = (t5_bucket(2 * P - 1 - np.arange(3 * P))[None] == np.arange(BUCKETS)[:, None]).astype(np.float32)
    o["ident"] = np.eye(P, dtype=np.float32)
    o["pair"] = np.kron(np.eye(2), np.ones((64, 64))).astype(np.float32)
    q, k = np.arange(P)[:, None], np.arange(L)[None]
    causal = np.where(k <= q + P, 0.0, NEG)
    window = np.where(k > q, causal, NEG)
    o["consts"] = np.concatenate([window, causal, np.repeat(np.arange(L)[None], P, axis=0)], axis=1).astype(np.float32)
    return {n: np.ascontiguousarray(a) for n, a in o.items()}


def kernel(**inputs):
    import concourse.bacc as bacc
    from concourse.bass_utils import run_bass_kernel_spmd

    arrays = layout({n: np.asarray(a) for n, a in inputs.items()})
    nc = bacc.Bacc("TRN2", target_bir_lowering=False, num_devices=1)
    t = {n: nc.dram_tensor(n + "_in", a.shape, mybir.dt.from_np(a.dtype), kind="ExternalInput").ap()
         for n, a in arrays.items()}
    t["skew"] = nc.dram_tensor("skew", (EV_HEADS, P, 3 * P), F32, kind="Internal").ap()
    t["out"] = nc.dram_tensor("out", (P, KT, L), F32, kind="ExternalOutput").ap()
    program(nc, t)
    r = run_bass_kernel_spmd(nc, [{n + "_in": a for n, a in arrays.items()}], core_ids=[0])
    y = np.asarray(r.results[0]["out"])
    return np.ascontiguousarray(y.transpose(2, 1, 0)).reshape(1, L, D)
```

```python
import math
from contextlib import ExitStack

import numpy as np

import concourse.bass as bass
from concourse import mybir

F32 = mybir.dt.float32
BF16 = mybir.dt.bfloat16
F32R = mybir.dt.float32r
ACT = mybir.ActivationFunctionType
ALU = mybir.AluOpType
AX_X = mybir.AxisListType.X

P = 128
D = 1024
KT = D // P
L = 256
QT = L // P
EPS = 1e-6
NEG = -1e30
TAKEN = -3e38
TOPK = 64
BUCKETS = 32
EV_HEADS = 8
OD_HEADS = 8
SSM_TILES = 16
AT_HEADS = 16
FF = 2816
FT = FF // P
FH = FT // 2
DI = 2048
DT_ = DI // P
GROUPS = 8
M_HEADS = 32
RING = 4
AUX = 3
AT_SCALE = 64 ** -0.5
ROUND = 1.5 * 2.0 ** 23
TWO_PI = 2.0 * math.pi
PI2_A = 6.28125
PI2_B = round((TWO_PI - PI2_A) * 2 ** 20) / 2 ** 20
PI2_C = TWO_PI - PI2_A - PI2_B

STREAM = [
    ("ev_in", 9, 2 * KT * P), ("ada0", 24, 2 * KT * P), ("glu", 2, 4 * 4 * P), ("ev_out", 4, 2 * KT * P),
    ("od_small", 1, KT * P + KT * OD_HEADS), ("od_in", 24, 2 * KT * P), ("ada1", 12, 2 * KT * P),
    ("od_out", 4, 2 * KT * P), ("qkv", 6, 2 * KT * P), ("w_o", 4, 2 * KT * P),
    ("ffn0a_in", FH, 2 * KT * P), ("ffn0a_out", KT, FH * P), ("ffn0b_in", FH, 2 * KT * P), ("ffn0b_out", KT, FH * P),
    ("ssm_dt", 1, KT * 2 * M_HEADS), ("ssm_in", 24, 2 * KT * P), ("ssm_out", KT, DT_ * P),
    ("ffn1a_in", FH, 2 * KT * P), ("ffn1a_out", KT, FH * P), ("ffn1b_in", FH, 2 * KT * P), ("ffn1b_out", KT, FH * P),
]
SLOT = 2 * KT * P
SPLIT = [
    ("od_in", 24), ("qkv", 12), ("w_o", 8),
    ("ffn0a_in", 2 * FH), ("ffn0a_out", KT), ("ffn0b_in", 2 * FH), ("ffn0b_out", KT), ("ssm_dt", 1), ("ssm_in", 48),
    ("ffn1a_in", 2 * FH), ("ffn1a_out", KT), ("ffn1b_in", 2 * FH), ("ffn1b_out", KT),
]
LIN_TILES = [
    ("ev_in", 18), ("s5_y", 4), ("glu", 8), ("ev_out", 8), ("od_ki", 1), ("od_in", 24), ("od_out", 8),
    ("qkv", 12), ("attn", 3 * AT_HEADS + 8), ("w_o", 8), ("ffn0a_in", 2 * FH), ("ffn0a_out", 8), ("ffn0b_in", 2 * FH),
    ("ffn0b_out", 8), ("ssm_dt", 1), ("ssm_in", 48),
    ("ssm_y", 16), ("ssm_out", 8), ("ffn1a_in", 2 * FH), ("ffn1a_out", 8), ("ffn1b_in", 2 * FH), ("ffn1b_out", 8),
]
AUX_TILES = [
    ("bias", 8), ("norm0", 2), ("s5_bb", 2), ("qk_norm0", 1 + 3), ("v_tok0", 1), ("scores0", 6), ("probs0", 8),
    ("out0", 4), ("s5_bu", 16),
    ("norm1", 2), ("wi", 1), ("index", 6), ("kq_norm1", 1 + 5), ("v_tok1", 1), ("scores1", 6), ("probs1", 8),
    ("out1", 8),
    ("norm2", 2), ("rope", 5), ("v_tok2", 2), ("attention", 3 * AT_HEADS), ("norm3", 2),
    ("norm4", 2), ("ssm_rows", 1), ("bc_tok", 4), ("xc_tok", 8), ("states", GROUPS), ("x_tok", 8),
    ("ssm_heads", M_HEADS + GROUPS), ("y_norm", 1 + GROUPS // 2), ("norm5", 2), ("norm6", 2),
]


def bases(table):
    at, out = 0, {}
    for name, n in table:
        out[name] = at
        at += n
    return out


def t5_bucket(dist):
    n = np.maximum(dist, 0)
    nf = np.maximum(n, 1).astype(np.float32)
    half = BUCKETS // 2
    scaled = np.log(nf / np.float32(half)) / np.float32(math.log(1024 / half)) * np.float32(half)
    return np.where(n < half, n, np.minimum(half + scaled.astype(np.int32), BUCKETS - 1))


class Count:

    def __init__(self, eng, sem):
        self.eng, self.sem, self.n = eng, sem, 0

    def mark(self, ins):
        ins.then_inc(self.sem, 1)
        self.n = self.n + 1

    def settle(self):
        self.eng.wait_ge(self.sem, self.n)

    def link(self, ins):
        self.mark(ins)
        self.settle()


class Memory:

    def __init__(self, tensor, at=0):
        self.tensor, self.at = tensor, at

    def take(self, *shape, rows=P):
        n = int(np.prod(shape))
        ap = self.tensor[0:rows, self.at:self.at + n]
        self.at += n
        assert self.at <= self.tensor.shape[1], self.at
        if len(shape) == 2:
            ap = ap.rearrange("p (a b) -> p a b", a=shape[0])
        elif len(shape) == 3:
            ap = ap.rearrange("p (a b c) -> p a b c", a=shape[0], b=shape[1])
        return ap


def rounds(eng, count, body):
    whole = count // RING
    for k in range(min(count, RING)):
        body(0, k)
    if whole > 2:
        with eng.Fori(1, whole) as i:
            for k in range(RING):
                body(i, k)
    else:
        for n in range(RING, whole * RING):
            body(n // RING, n % RING)
    for n in range(max(whole, 1) * RING, count):
        body(n // RING, n % RING)


def twice(ap):
    return ap.unsqueeze(1).to_broadcast([ap.shape[0], 2, ap.shape[1]])


def each(ap, n):
    return ap.unsqueeze(2).to_broadcast([ap.shape[0], ap.shape[1], n])


def program(nc, t):
    with ExitStack() as ctx:
        def sb(name, shape, dt=F32):
            return ctx.enter_context(nc.sbuf_tensor(name, shape, dt))

        sems = {}

        def sig(name):
            if name not in sems:
                sems[name] = ctx.enter_context(nc.semaphore(name))
            return sems[name]

        block_of = bases([(n, c) for n, c, _ in STREAM])
        lin_of = bases(LIN_TILES)
        aux_of = bases(AUX_TILES)
        unit_of = bases(SPLIT)

        ring = sb("ring", [P, RING, SLOT])
        xres = sb("xres", [P, KT, 2 * L])
        rcol = sb("rcol", [P, 2 * QT])
        ident = sb("ident", [P, P])
        ones = sb("ones", [P, P])
        pair = sb("pair", [P, P])
        gcol = sb("gcol", [P, 2, KT])
        mod = sb("mod", [P, 2, 48, 2])
        modb = sb("modb", [P, 2, 48])
        sc_c = sb("sc_c", [P, KT, 32])
        ada_sb = sb("ada_sb", [P, L])
        group_sum = sb("group_sum", [P, 2])
        eps = sb("eps", [P, 1])
        half_pi = sb("half_pi", [P, 1])
        ARENA, HN = 31488, KT * 2 * L

        def places(*tensors):
            with ExitStack() as shared:
                return [shared.enter_context(nc.sbuf_tensor(n, s, dt)) for n, s, dt in tensors]

        arena, hn = places(("arena", [P, ARENA], F32), ("hn", [P, KT, 2 * L], F32))
        W_UNITS = 4
        hid_split, w_split, hn_hi, _, hn_lo = places(
            ("hid_split", [P, 2, FH, 2 * L], F32R), ("w_split", [P, W_UNITS, 2, FH * P], F32R),
            ("hn_hi", [P, KT, 2 * L], F32R), ("hi_end", [P, ARENA - 22528 - HN], F32), ("hn_lo", [P, KT, 2 * L], F32R))
        out_lo = hid_split[:, 0, 0:KT]
        _, od_hi, w_split_od = places(
            ("od_start", [P, 20480], F32), ("od_hi", [P, KT, L], F32R), ("w_split_od", [P, W_UNITS, 2, KT * P], F32R))
        od_lo = hn_lo[:, :, L:2 * L]
        _, rows_split, ident_split = places(
            ("rows_start", [P, 27648], F32), ("rows_split", [P, 2, L], F32R), ("ident_split", [P, 2 * M_HEADS], F32R))
        _, w_split_ssm = places(("ssm_start", [P, 18432], F32), ("w_split_ssm", [P, 2, 2, KT * P], F32R))
        whole_arena = sb("whole_arena", [P, ARENA + HN])
        lin = ctx.enter_context(nc.psum_tensor("lin", [P, RING, 2 * L], F32))
        aux = ctx.enter_context(nc.psum_tensor("aux", [P, AUX, 2 * L], F32))
        modp = ctx.enter_context(nc.psum_tensor("modp", [P, 2 * L], F32))

        mem = Memory(arena)
        bias_a = mem.take(EV_HEADS, L)
        bias_b = mem.take(OD_HEADS, L)
        base = mem.at
        qa = mem.take(4, L)
        ka = mem.take(L)
        va = mem.take(L)
        v_tok = mem.take(QT, P)
        gate_a = mem.take(4, L)
        u = mem.take(4, L)
        gate_b = mem.take(4, L)
        at = sq0_at = mem.at
        sq0 = mem.take(5, L)
        sq_end = mem.at
        mem.at = at
        lg0 = mem.take(EV_HEADS, P)
        lg1 = mem.take(EV_HEADS, L)
        pt = mem.take(EV_HEADS, 3 * P)
        end = mem.at
        mem.at = at
        table = mem.take(EV_HEADS, 3 * P)
        mem.at = max(end, mem.at, sq_end)
        cos_t = mem.take(SSM_TILES, L)
        sin_t = mem.take(SSM_TILES, L)
        s5w = mem.take(2, 2, L)
        s5z = mem.take(2, 2, L)
        s5q = mem.take(2, 2 * L).rearrange("p a (b c) -> p a b c", b=2)
        s5x = mem.take(2, 2, L)
        s5t = mem.take(2, 2 * L)
        s5_back = mem.take(2, 2, L)
        s5_states = Memory(arena, sq0_at).take(8, 2, L)
        cat = hn[:, :, L:2 * L]

        par = sb("par", [P, 32, SSM_TILES])
        consts = sb("consts", [P, L + L + L])
        mask_a, mask_b, steps = (consts[:, n * L:(n + 1) * L] for n in range(3))
        b_in = sb("b_in", [P, 2, SSM_TILES, 16])
        bd = s5x.rearrange("p a b c -> p (a b c)").rearrange("p (a b c) -> p a b c", a=2, b=SSM_TILES)
        bb_t = sb("bb_t", [P, 2, 4, P])
        c_bd = sb("c_bd", [P, 2, SSM_TILES, 32])
        d_col = sb("d_col", [P, 4])
        glu_b = sb("glu_b", [P, 8])
        qk_g = sb("qk_g", [P, 4])
        sink = sb("sink", [P, EV_HEADS])
        relb = s5z.rearrange("p a b c -> p (a b c)")[0:BUCKETS].rearrange("p (a b) -> p a b", a=EV_HEADS)
        hot = s5q.rearrange("p a b c -> p (a b c)")[0:BUCKETS, 0:3 * P]
        small = sb("small", [P, 12, 8])
        g2 = sb("g2", [P, 5, KT])
        nsink2_in = sb("nsink2_in", [P, AT_HEADS])
        a_col = sb("a_col", [P, KT, 2])
        ssm_cols = sb("ssm_cols", [P, 2, DT_])
        dt_cols = sb("dt_cols", [2 * M_HEADS, 2])
        stat_ssm = sb("stat_ssm", [P, 4])

        mem = Memory(arena, base)
        q1 = mem.take(OD_HEADS, L)
        k1 = mem.take(2, L)
        v1 = mem.take(2, L)
        gate1 = mem.take(OD_HEADS, L)
        qi = mem.take(4, L)
        ki = mem.take(L)
        wi = mem.take(QT, OD_HEADS)
        v_tok1 = mem.take(QT, 2 * P)
        rel = mem.take(2, 2 * L)
        idx = mem.take(QT, L)
        top = mem.take(QT, 8)
        sel = mem.take(QT, L)
        at = mem.at
        sq1 = mem.take(10, L)
        end = mem.at
        mem.at = at
        lh0 = mem.take(OD_HEADS, P)
        lh1 = mem.take(OD_HEADS, L)
        pt1 = mem.take(OD_HEADS, 3 * P)
        mem.at = max(end, mem.at)

        mem = Memory(arena)
        q2 = mem.take(8, 2 * L)
        k2 = mem.take(2, 2 * L)
        v2 = mem.take(2, 2 * L)
        v_tok2 = mem.take(4, 2 * P)
        rope_cs = mem.take(2, L)
        rope_tmp = mem.take(2, L)
        mask2 = mem.take(2, P)
        rope_perm = mem.take(P)
        stat2 = mem.take(6, AT_HEADS, 4)
        nsink2 = mem.take(2, AT_HEADS)
        ident_b = mem.take(P // 2).bitcast(BF16)
        mask_b2 = mem.take(P).bitcast(BF16).rearrange("p (a b) -> p a b", a=2)
        p2 = mem.take(3, 3, 2 * L)
        mem.at = 22528 + HN
        pt2 = mem.take(3, 3, 2 * L)
        mem = Memory(arena, 22528 + HN)
        silu_g = mem.take(2, 2 * L)
        mem = Memory(arena)
        zs = mem.take(DT_, L)
        ys = mem.take(DT_, L)
        at = mem.at
        xc = mem.take(DT_, L)
        mem.at = at
        state = mem.take(GROUPS, 2, L)
        bm = mem.take(GROUPS, 2 * L)
        cm = mem.take(GROUPS, L)
        x_tok = mem.take(QT, DI)
        at = mem.at
        xc_tok = mem.take(QT, DI)
        end = mem.at
        mem.at = at
        decay = [mem.take(2, 3 * L)]
        from_start = [mem.take(2, 2, L)]
        decay.append(mem.take(2, 3 * L))
        mem.at = end
        tri = mem.take(2, P)
        rows_g = mem.take(L)
        cols_g = mem.take(3, QT, 2 * M_HEADS)
        conv_w = mem.take(32, 4)
        mem2 = Memory(hn[:].rearrange("p a b -> p (a b)"))
        bc_tok = mem2.take(QT, GROUPS * P)
        xw = mem2.take(2, QT, L)
        mem2 = Memory(mem2.tensor)
        decay.append(mem2.take(2, 3 * L))
        from_start += [mem2.take(2, 2, L) for _ in range(2)]
        cb = bm[:, 0:6, L:2 * L].rearrange("p (a b) c -> p a b c", a=2)
        y_sq = zs
        xs_pair = arena[:, DT_ * L:3 * DT_ * L].rearrange("p (s n c) -> p n s c", s=2, n=DT_)
        dt_rows = c_bd[:].rearrange("p a b c -> p (a b c)")[0:64].rearrange("p (a b) -> p a b", a=2)
        dt2, da = dt_rows[:, 0, :], dt_rows[:, 1, :]
        rows_neg = da[:, 0:L]
        spare = bb_t[:].rearrange("p a b c -> p (a b c)")[0:64].rearrange("p (a b) -> p a b", a=2)
        dt_tmp, dt_tmp2 = spare[:, 0, :], spare[:, 1, :]
        dt_tmp3 = b_in[:].rearrange("p a b c -> p (a b c)")[0:64]
        tot = stat_ssm[0:64, 0:2]
        a_neg = stat_ssm[0:64, 2:3]

        w_in = [sig(f"w_in{n}") for n in range(RING)]
        lin_free = [sig(f"lin_free{n}") for n in range(RING)]
        aux_free = [sig(f"aux_free{n}") for n in range(AUX)]

        def lin_count(tile):
            return tile + 1 - (4 if tile >= lin_of["s5_y"] + 4 else 0)

        def full(eng, banks, tile, later=0):
            eng.wait_ge(sig(banks + "_full"), later + (lin_count(tile) if banks == "lin" else tile + 1))

        def frees(ins, banks, tile):
            sems_, n = (lin_free, RING) if banks == "lin" else (aux_free, AUX)
            ins.then_inc(sems_[tile % n], 1)

        def taken(eng, banks, tile, turns=0):
            sems_, n = (lin_free, RING) if banks == "lin" else (aux_free, AUX)
            eng.wait_ge(sems_[tile % n], turns + (tile // n + 1))

        def score_tile(h, n):
            return aux_of["attention"] + 3 * h + n

        def turned_tile(h, n):
            return lin_of["attn"] + 3 * h + h // 2 + n

        def output_tile(n):
            return lin_of["attn"] + 7 * n + 6

        def cb_tile(g):
            return aux_of["ssm_heads"] + 5 * g

        def bc_tile(h):
            return aux_of["ssm_heads"] + 5 * (h // 4) + 1 + h % 4

        used = []
        for name, n, _ in STREAM:
            if name == "od_in":
                used += [("ada_used", 24 + m // 2 + 1) if m % 2 else ("w_low", unit_of[name] + m + 2) for m in range(n)]
            elif name in unit_of:
                used += [("w_low", unit_of[name] + dict(SPLIT)[name] // n * (m + 1)) for m in range(n)]
            elif name[:3] == "ada":
                used += [("ada_used", int(name[3]) * 36 + m + 1) for m in range(n)]
            else:
                stage = {"od_small": "od_ki"}.get(name, name)
                tiles = dict(LIN_TILES)[stage] // n
                used += [("lin_full", lin_count(lin_of[stage] + tiles * (m + 1) - 1)) for m in range(n)]

        def index_heads(m):
            return (1, (m % 2 + 4 * (m // 2), m % 2 + 4 * (m // 2) + 2), L) if m < 4 else \
                (0, range(m - 4, OD_HEADS, 2), P)

        block = ctx.enter_context(nc.Block())

        @block.sync
        def _(sp):
            sp.dma_start(xres[:, :, 0:L], t["x"]).then_inc(sig("x_in"), 16)
            for name, n, cols in STREAM:
                first = block_of[name]

                def load(i, k):
                    b = first + k
                    if isinstance(i, int):
                        b, i = b + i * RING, 0
                    if b >= RING or not isinstance(i, int):
                        which, value = used[b - RING] if isinstance(i, int) else used[b]
                        if not isinstance(i, int):
                            value = value + (i - 1) * (used[b + RING][1] - used[b][1])
                        sp.wait_ge(sig(which), value)
                    at = b - first + i * RING
                    source = t[name][at] if isinstance(i, int) else \
                        t[name][bass.ds(at, 1)].rearrange("a p n -> p (a n)")
                    sp.dma_start(ring[:, b % RING, 0:cols], source).then_inc(w_in[b % RING], 16)

                rounds(sp, n, load)
            sp.wait_ge(sig("hn_ready"), 7 * KT)
            sp.dma_start(t["out"], hn[:, :, 0:L]).then_inc(sig("stored"), 16)
            sp.wait_ge(sig("stored"), 16)

        def sum_squares(pool, own, k, width):
            total = hn[:, 0, 0:width]
            for kt in range(1, KT):
                pool.wait_ge(sig("squares"), KT * k + kt + 1)
                ins = nc.gpsimd.tensor_tensor(total, total, hn[:, kt, 0:width], ALU.add)
                if kt < KT - 1:
                    own.link(ins)
            ins.then_inc(sig("square_sums"), 1)

        def hidden_parts(pool, own, n, width):
            for m in range(FT):
                taken(pool, "lin", lin_of[f"ffn{n}{'ab'[m // FH]}_in"] + 2 * (m % FH) + 1)
                if m == FH:
                    full(pool, "lin", lin_of[f"ffn{n}a_out"] + KT - 1)
                hi, lo = (hid_split[:, part, m % FH, 0:width] for part in range(2))
                own.link(nc.gpsimd.tensor_copy(hi, silu_g[:, m % 2, 0:width]))
                nc.gpsimd.tensor_tensor(lo, silu_g[:, m % 2, 0:width], hi.bitcast(F32), ALU.subtract)\
                    .then_inc(sig("hid_ready"), 1)

        def chain(name):
            if name[:3] == "ssm":
                return "ssm_dt", w_split_ssm, 2, 0
            if name[:4] == "ffn1":
                return "ffn1a_in", w_split, W_UNITS, 0
            if name == "od_in":
                return name, w_split_od, W_UNITS, 0
            return ("qkv", w_split, W_UNITS, 0) if name == "qkv" else ("w_o", w_split, W_UNITS, 1)

        def unit(name, u):
            n, cols = next((n, c) for x, n, c in STREAM if x == name)
            every = 2 if name == "od_in" else 1
            per_block = dict(SPLIT)[name] // n * every
            b, cols = block_of[name] + u // per_block * every, cols // per_block
            first, memory, places_, shift = chain(name)
            parts = memory[:, (unit_of[name] + u - unit_of[first] + shift) % places_, :, 0:cols]
            return parts, ring[:, b % RING, u % per_block * cols:(u % per_block + 1) * cols], b

        def weights_hi(act, name, u):
            parts, w, b = unit(name, u)
            act.wait_ge(w_in[b % RING], 16 * (b // RING + 1))
            before = lin_of[name] + u - chain(name)[2]
            if before >= lin_of[chain(name)[0]]:
                full(act, "lin", before)
            act.activation(parts[:, 0], w, ACT.Copy).then_inc(sig("w_high"), 1)

        def weights_lo(dve, name, u):
            parts, w, _ = unit(name, u)
            dve.wait_ge(sig("w_high"), unit_of[name] + u + 1)
            dve.tensor_tensor(parts[:, 1], w, parts[:, 0].bitcast(F32), ALU.subtract).then_inc(sig("w_low"), 1)

        @block.gpsimd
        def _(pool):
            own = Count(pool, sig("pool_own"))
            nc.gpsimd.memset(eps[:], EPS)
            nc.gpsimd.memset(half_pi[:], math.pi / 2)
            nc.gpsimd.memset(ones[:], 1.0)
            nc.gpsimd.memset(bd, 0.0)
            nc.gpsimd.memset(c_bd[:], 0.0).then_inc(sig("made"), 1)
            pool.dma_start(par[:, 0:3, :], t["s5_par"]).then_inc(sig("s5_in"), 16)
            pool.dma_start(b_in[:], t["s5_b"]).then_inc(sig("s5_in"), 16)
            pool.dma_start(consts[:], t["consts"]).then_inc(sig("steps_in"), 16)
            sum_squares(pool, own, 0, L)
            taken(pool, "aux", aux_of["bias"] + EV_HEADS - 1)
            pool.dma_start(t["skew"].rearrange("h p n -> p h n"), table).then_inc(sig("table_out"), 16)
            pool.wait_ge(sig("made"), 1)
            for n in range(2):
                for part in range(2):
                    rows = slice(64 * n, 64 * n + 64)
                    pool.dma_start(c_bd[rows, part, :, 16 * n:16 * n + 16], t["s5_c"][rows, part])\
                        .then_inc(sig("c_in"), 16)
            for dst, name in ((pair[:], "pair"), (qk_g[:], "qk_g"), (sink[:], "sink"), (d_col[:], "d_col"),
                              (glu_b[:], "glu_b"), (sc_c[:], "cc"), (group_sum[:], "group_sum"), (modb[:], "modb"),
                              (g2[:], "g2"), (ssm_cols[:], "ssm_cols"), (dt_cols[:], "dt_cols"),
                              (nsink2_in[:], "sink2"), (xres[:, :, L:2 * L], "ctx")):
                pool.dma_start(dst, t[name]).then_inc(sig("const_in"), 16)
            pool.wait_ge(sig("table_out"), 16)
            skewed = bass.AP(t["skew"].tensor, P - 1, [[3 * P - 1, P], [3 * P * P, EV_HEADS], [1, L]])
            pool.dma_start(bias_b, skewed).then_inc(sig("table_back"), 16)
            for j in range(SSM_TILES):
                p = j % 2
                turned, back = s5q[:, p], s5_back[:, p]
                z = s5z[:, p]
                pool.wait_ge(sig("z_ready"), j + 1)
                own.link(nc.gpsimd.tensor_tensor(turned, z, twice(cos_t[:, j, :]), ALU.mult))
                pool.wait_ge(sig("z_turned"), j + 1)
                if j >= 8:
                    pool.wait_ge(sig("s5_used"), j // 4 - 1)
                own.mark(nc.gpsimd.tensor_tensor(s5_states[:, j % 8, 0, :], turned[:, 0], back[:, 1], ALU.subtract))
                nc.gpsimd.tensor_tensor(s5_states[:, j % 8, 1, :], turned[:, 1], back[:, 0], ALU.add)\
                    .then_inc(sig("x_states"), 1)
                pool.wait_ge(sig("x_states"), j + 1)
            for m in range(2):
                weights_lo(pool, "od_in", m)
            sum_squares(pool, own, 1, L)
            for kt in range(KT):
                pool.wait_ge(sig("od_high"), kt + 1)
                pool.tensor_tensor(od_lo[:, kt, :], hn[:, kt, 0:L], od_hi[:, kt, :].bitcast(F32), ALU.subtract)\
                    .then_inc(sig("od_low"), 1)
            for m in range(2, 24):
                weights_lo(pool, "od_in", m)
            sum_squares(pool, own, 2, 2 * L)
            taken(pool, "lin", lin_of["od_out"] + KT - 1)
            for dst, name in ((rope_cs, "rope_cs"), (rope_perm, "rope_perm"), (mask2, "mask2")):
                pool.dma_start(dst, t[name]).then_inc(sig("at_in"), 16)
            sum_squares(pool, own, 3, 2 * L)
            hidden_parts(pool, own, 0, 2 * L)
            sum_squares(pool, own, 4, 2 * L)
            taken(pool, "lin", lin_of["ffn0b_out"] + KT - 1)
            for dst, name in ((conv_w, "conv_w"), (tri, "tri")):
                pool.dma_start(dst, t[name]).then_inc(sig("ssm_in"), 16)
            def gate_y(n):
                taken(pool, "lin", lin_of["ssm_y"] + n)
                nc.gpsimd.tensor_tensor(ys[:, n], ys[:, n], zs[:, n], ALU.mult).then_inc(sig("y_gated"), 1)

            for h in range(M_HEADS):
                taken(pool, "aux", bc_tile(h))
                since = from_start[h // 2 % 3][:, h % 2]
                nc.gpsimd.tensor_tensor(since, since, twice(cm[:, h // 4, :]), ALU.mult)\
                    .then_inc(sig("c_decayed"), 1)
                if h % 2 and h >= 9:
                    gate_y(h // 2 - 4)
            for n in range(DT_ - 4, DT_):
                gate_y(n)
            sum_squares(pool, own, 5, L)
            hidden_parts(pool, own, 1, L)
            sum_squares(pool, own, 6, L)

        def ada_copies(act, first, n):
            for m in range(first, first + n):
                act.wait_ge(sig("ada_used"), m + 1)
                if m:
                    act.wait_ge(sig("ada_summed"), m)
                act.activation(ada_sb[:], modp[:, 0:L], ACT.Copy).then_inc(sig("ada_copied"), 1)

        def act_norm(act, k, width, after=None, shift=None, split=False, meanwhile=None, before=None):
            for kt in range(KT):
                if before is not None:
                    before(kt)
                if after is not None:
                    taken(act, "lin", lin_of[after] + kt)
                act.activation(hn[:, kt, 0:width], xres[:, kt, 0:width], ACT.Square).then_inc(sig("squares"), 1)
            if meanwhile is not None:
                meanwhile()
            tile = aux_of[f"norm{k}"]
            full(act, "aux", tile)
            n = width // P
            frees(act.activation(rcol[:, 0:n], aux[:, tile % AUX, 0:n], ACT.Sqrt, scale=1.0 / D, bias=eps[:]), "aux",
                  tile)
            if shift is not None:
                layer, chunk, nth = shift
                for kt in range(KT):
                    act.wait_ge(sig("scaled"), KT * nth + kt + 1)
                    for s in range(width // L):
                        cols = hn[:, kt, s * L:(s + 1) * L]
                        by = mod[:, layer, chunk * KT + kt, s:s + 1]
                        if split:
                            act.activation(hn_hi[:, kt, s * L:(s + 1) * L], cols, ACT.Identity, bias=by)
                        ins = act.activation(cols, cols, ACT.Identity, bias=by)
                    ins.then_inc(sig("shifted" if split else "hn_ready"), 1)

        def softmax_exps(act, own, layer, logits, stats, sinks):
            act.wait_ge(sig(f"maxima{layer}"), 1)
            for qt in range(QT):
                for h in range(8):
                    ins = act.activation(logits[qt][:, h, :], logits[qt][:, h, :], ACT.Exp,
                                         bias=stats[:, 2 + qt, h:h + 1], accum_out=stats[:, 6 + qt, h:h + 1])
            if sinks:
                own.mark(ins)
                ins = act.activation(stats[:, 8:10, :], stats[:, 4:6, :], ACT.Exp)
            ins.then_inc(sig(f"exps{layer}"), 1)

        head_roots = small[:].rearrange("p a b -> p (a b)")[:, 0:32]

        def roots(act, name, n, scale):
            tile = aux_of[name]
            full(act, "aux", tile)
            frees(act.activation(head_roots[:, 0:n], aux[:, tile % AUX, 0:n], ACT.Sqrt, scale=scale, bias=eps[:]),
                  "aux", tile)

        def inverses(dve, name, n):
            taken(dve, "aux", aux_of[name])
            dve.reciprocal(head_roots[:, 0:n], head_roots[:, 0:n]).then_inc(sig(name), 1)

        def over_roots(dve, name, things):
            for n, (thing, by) in enumerate(things):
                tile = aux_of[name] + 1 + n // 2
                full(dve, "aux", tile)
                ins = dve.scalar_tensor_tensor(out=thing, in0=thing, scalar=by,
                                               in1=aux[:, tile % AUX, n % 2 * L:n % 2 * L + thing.shape[-1]],
                                               op0=ALU.mult, op1=ALU.mult)
                if n % 2 or n == len(things) - 1:
                    frees(ins, "aux", tile)

        def copies(act, name, n, src, dst):
            for m in range(n):
                tile = aux_of[name] + m
                full(act, "aux", tile)
                frees(act.activation(dst(m), src(aux[:, tile % AUX]), ACT.Copy), "aux", tile)

        def ffn_units(n):
            units = [(f"ffn{n}{part}", u) for part, count in
                     (("a_in", 2 * FH), ("a_out", KT), ("b_in", 2 * FH), ("b_out", KT)) for u in range(count)]
            return [(*unit_, units[v + W_UNITS] if v + W_UNITS < len(units) else None)
                    for v, unit_ in enumerate(units)]

        def ffn_scalar(act, n, width):
            nth = n * FT
            for stage, u, later in ffn_units(n):
                if later is not None:
                    weights_hi(act, *later)
                if stage[-2:] == "in" and u % 2 == 0:
                    tile = lin_of[stage] + u
                    full(act, "lin", tile)
                    if nth >= 2:
                        act.wait_ge(sig("hid_ready"), nth - 1)
                    frees(act.activation(silu_g[:, nth % 2, 0:width], lin[:, tile % RING, 0:width], ACT.Silu),
                          "lin", tile)
                    nth += 1

        def second_block_scalar(act, own):
            full(act, "aux", aux_of["out1"] + 7)
            for u in range(W_UNITS):
                weights_hi(act, "qkv", u)
            act_norm(act, 2, 2 * L, "od_out", (0, 0, 0), True)
            into = [k2[:, n] for n in range(2)] + [v2[:, n] for n in range(2)] + [q2[:, n] for n in range(8)]
            for n, dst in enumerate(into):
                tile = lin_of["qkv"] + n
                if n + W_UNITS < 12:
                    weights_hi(act, "qkv", n + W_UNITS)
                full(act, "lin", tile)
                frees(act.activation(dst, lin[:, tile % RING, :], ACT.Copy), "lin", tile)
            copies(act, "v_tok2", 2, lambda ps: ps,
                   lambda n: v_tok2[:, 2 * n:2 * n + 2, :].rearrange("p a b -> p (a b)"))
            for i in range(AT_HEADS + 2):
                if i < AT_HEADS:
                    act.wait_ge(sig("maxima2"), i + 1)
                    for n, (part, cols) in enumerate(((0, slice(0, 2 * L)), (1, slice(0, 2 * L)),
                                                      (2, slice(0, L)), (2, slice(L, 2 * L)))):
                        tile = score_tile(i, part)
                        ins = act.activation(p2[:, i % 3, part, cols], aux[:, tile % AUX, cols], ACT.Exp,
                                             scale=AT_SCALE, bias=stat2[:, 1, i, n:n + 1],
                                             accum_out=stat2[:, 2, i, n:n + 1])
                        if n != 2:
                            frees(ins, "aux", tile)
                    act.activation(stat2[:, 3, i, :], stat2[:, 1, i, :], ACT.Exp, bias=nsink2[:, 0, i:i + 1])\
                        .then_inc(sig("exps2"), 1)
                if i >= 2:
                    h = i - 2
                    for n in range(3):
                        tile = turned_tile(h, n)
                        full(act, "lin", tile)
                        frees(act.activation(pt2[:, h % 3, n, :], lin[:, tile % RING, :], ACT.Copy), "lin", tile)
                if 8 <= i < 11:
                    weights_hi(act, "w_o", i - 8)
            full(act, "lin", output_tile(7))
            weights_hi(act, "w_o", 3)

            def next_weights(n):
                weights_hi(act, *(("w_o", n + W_UNITS) if n < W_UNITS else ("ffn0a_in", n - W_UNITS)))

            act_norm(act, 3, 2 * L, "w_o", (0, 3, 1), True, before=next_weights)
            ffn_scalar(act, 0, 2 * L)
            def first_weights():
                full(act, "lin", lin_of["ffn0b_out"] + KT - 1)
                weights_hi(act, "ssm_dt", 0)
                weights_hi(act, "ssm_in", 0)

            act_norm(act, 4, 2 * L, "ffn0b_out", (1, 0, 2), True, first_weights)
            weights_hi(act, "ssm_in", 1)
            weights_hi(act, "ssm_in", 2)
            act.wait_ge(sig("dt_abs"), 1)
            own.link(act.activation(dt_tmp, dt_tmp, ACT.Exp, scale=-1.0))
            own.mark(act.activation(dt_tmp2, dt_tmp, ACT.Ln, bias=ones[0:64, 0:1]))
            act.activation(a_neg, dt_cols[:, 1:2], ACT.Exp).then_inc(sig("dt_exp"), 1)
            for n in range(48):
                tile = lin_of["ssm_in"] + n
                if n + 3 < 48:
                    weights_hi(act, "ssm_in", n + 3)
                if n == 3:
                    act.wait_ge(sig("dt_summed"), 1)
                    act.activation(dt_tmp[:, L:2 * L], dt_tmp[:, L:2 * L], ACT.Exp, scale=-1.0, bias=tot[:, 1:2])\
                        .then_inc(sig("dt_weights"), 1)
                if n < 32:
                    taken(act, "lin", tile)
                    dst = bm[:, n, :] if n < 8 else xs_pair[:, n - 8] if n < 24 else cm[:, n - 24, :]
                    act.activation(dst, dst, ACT.Silu).then_inc(sig("convolved"), 1)
                else:
                    full(act, "lin", tile)
                    frees(act.activation(zs[:, n - 32, :], lin[:, tile % RING, 0:L], ACT.Silu), "lin", tile)
            copies(act, "ssm_rows", 1, lambda ps: ps[:, 0:6 * 64], lambda n: cols_g.rearrange("p a b c -> p (a b c)"))
            turned_copies(act, "bc_tok", 4, bc_tok, 2, 0, act.activation)
            turned_copies(act, "xc_tok", 8, xc_tok, 4, 0, act.activation)
            for g in range(GROUPS):
                tile = aux_of["states"] + g
                full(act, "aux", tile)
                frees(act.activation(state[:, g].rearrange("p a b -> p (a b)"), aux[:, tile % AUX, :], ACT.Copy),
                      "aux", tile)
            turned_copies(act, "x_tok", 8, x_tok, 4, 0, act.activation)
            def square_y(n):
                act.wait_ge(sig("y_gated"), n + 1)
                act.activation(y_sq[:, n], ys[:, n], ACT.Square).then_inc(sig("y_squares"), 1)

            for h in range(M_HEADS):
                between, since = decay[h // 2 % 3][:, h % 2], from_start[h // 2 % 3][:, h % 2]
                tile = bc_tile(h)
                act.wait_ge(sig("gaps"), h + 1)
                if h >= 6:
                    full(act, "lin", lin_of["ssm_y"] + h // 2 - 3)
                for d, qt, lo_, hi_, at in (parts[0], parts[3]):
                    own.mark(act.activation(between[:, at:at + L], aux[:, tile % AUX, d * L:(d + 1) * L], ACT.Relu,
                                            bias=cols_g[:, 0, qt, d * 32 + h:d * 32 + h + 1]))
                own.settle()
                act.activation(between, between, ACT.Exp, scale=-1.0).then_inc(sig("decays"), 1)
                frees(act.activation(since.rearrange("p a b -> p (a b)"), aux[:, tile % AUX, :], ACT.Exp, scale=-1.0),
                      "aux", tile)
                if h % 2 and h >= 13:
                    square_y(h // 2 - 6)
            for n in range(DT_ - 6, DT_):
                square_y(n)
            roots(act, "y_norm", 2 * GROUPS, 1.0 / L)
            taken(act, "aux", aux_of["y_norm"])
            for u in range(W_UNITS):
                weights_hi(act, "ffn1a_in", u)
            act_norm(act, 5, L, "ssm_out", (1, 3, 3), True)
            ffn_scalar(act, 1, L)
            act_norm(act, 6, L, "ffn1b_out")

        parts = ((0, 0, 0, L, 0), (0, 1, P, L, L), (1, 0, 0, P, 3 * P), (1, 1, 0, L, 4 * P))

        def turned_copies(eng, name, n, dst, per_row, parity, copy):
            for q in range(parity, n, 2):
                tile = aux_of[name] + q
                full(eng, "aux", tile)
                out, src = dst[:, q // per_row, (q % per_row) * 2 * L:(q % per_row + 1) * 2 * L], aux[:, tile % AUX, :]
                frees(copy(out, src, ACT.Copy) if parity == 0 else copy(out, src), "aux", tile)

        def normed(dve, k, width, a, shifted=False, split=None):
            def low(kt):
                dve.wait_ge(sig("shifted"), KT * split + kt + 1)
                dve.tensor_tensor(hn_lo[:, kt, 0:width], hn[:, kt, 0:width], hn_hi[:, kt, 0:width].bitcast(F32),
                                  ALU.subtract).then_inc(sig("hn_ready"), 1)

            tile = aux_of[f"norm{k}"]
            taken(dve, "aux", tile)
            dve.reciprocal(rcol[:, 0:width // P], rcol[:, 0:width // P]).then_inc(sig("rms"), 1)
            full(dve, "aux", tile + 1)
            for kt in range(KT):
                for s in range(width // L):
                    cols = slice(s * L, (s + 1) * L)
                    ins = dve.scalar_tensor_tensor(
                        out=hn[:, kt, cols], in0=xres[:, kt, cols], scalar=a(kt, s),
                        in1=aux[:, (tile + 1) % AUX, cols], op0=ALU.mult, op1=ALU.mult)
                ins.then_inc(sig("scaled" if shifted else "hn_ready"), 1)
                if split is not None and kt >= 2:
                    low(kt - 2)
            if split is not None:
                low(KT - 2)
                low(KT - 1)
            frees(dve.tensor_copy(rcol[:, 0:1], rcol[:, 0:1]), "aux", tile + 1)

        def maxima(dve, own, layer, logits, stats, sinks):
            own.settle()
            own.mark(dve.tensor_reduce(stats[:, 0, :], logits[0], AX_X, ALU.max))
            own.link(dve.tensor_reduce(stats[:, 1, :], logits[1], AX_X, ALU.max))
            if sinks is not None:
                own.link(dve.tensor_tensor(stats[:, 0:2, :], stats[:, 0:2, :], twice(sinks), ALU.max))
            ins = dve.tensor_scalar(stats[:, 2:4, :], stats[:, 0:2, :], -1.0, None, ALU.mult)
            if sinks is not None:
                own.link(ins)
                ins = dve.tensor_tensor(stats[:, 4:6, :], stats[:, 2:4, :], twice(sinks), ALU.add)
            ins.then_inc(sig(f"maxima{layer}"), 1)

        def probabilities(dve, own, layer, logits, stats, sinks):
            dve.wait_ge(sig(f"exps{layer}"), 1)
            if sinks:
                own.link(dve.tensor_tensor(stats[:, 6:8, :], stats[:, 6:8, :], stats[:, 8:10, :], ALU.add))
            own.link(dve.reciprocal(stats[:, 10:12, :], stats[:, 6:8, :]))
            own.mark(dve.tensor_tensor(logits[0], logits[0], each(stats[:, 10, :], P), ALU.mult))
            dve.tensor_tensor(logits[1], logits[1], each(stats[:, 11, :], L), ALU.mult)\
                .then_inc(sig(f"probs{layer}"), 1)

        def scaled_logits(dve, own, layer, bias, logits, scale):
            for n in range(6):
                tile = aux_of[f"scores{layer}"] + n
                full(dve, "aux", tile)
                if n < 2:
                    heads = slice(4 * n, 4 * n + 4)
                    out, add = logits[0][:, heads, :], bias[:, heads, P:L]
                else:
                    heads = slice(2 * (n - 2), 2 * (n - 2) + 2)
                    out, add = logits[1][:, heads, :], bias[:, heads, :]
                frees(dve.scalar_tensor_tensor(
                    out=out, in0=aux[:, tile % AUX].rearrange("p (a b) -> p a b", a=out.shape[1]), scalar=scale,
                    in1=add, op0=ALU.mult, op1=ALU.add), "aux", tile)
            for n in range(3, 6):
                taken(dve, "aux", aux_of[f"scores{layer}"] + n)

        def gated_tile(dve, tile, n, layer, chunk, parts):
            full(dve, "lin", tile)
            for s in range(parts):
                cols = slice(s * L, (s + 1) * L)
                ins = dve.scalar_tensor_tensor(
                    out=xres[:, n, cols], in0=lin[:, tile % RING, cols],
                    scalar=mod[:, layer, chunk * KT + n, s:s + 1], in1=xres[:, n, cols], op0=ALU.mult, op1=ALU.add)
            frees(ins, "lin", tile)

        def gated_add(dve, own, name, layer, chunk, parts):
            for n in range(KT):
                gated_tile(dve, lin_of[name] + n, n, layer, chunk, parts)
            for n in range(RING):
                taken(dve, "lin", lin_of[name] + KT - 1 - n)

        def modulated(dve, own, k, width, layer, chunk, split=None):
            own.link(dve.scalar_tensor_tensor(
                out=a_col[:], in0=mod[:, layer, (chunk + 1) * KT:(chunk + 2) * KT, :], scalar=1.0,
                in1=each(g2[:, k - 2, :], 2), op0=ALU.add, op1=ALU.mult))
            normed(dve, k, width, lambda kt, s: a_col[:, kt, s:s + 1], True, split)

        def ffn_vector(dve, n, width):
            nth = n * FT
            for stage, u, later in ffn_units(n):
                tile = lin_of[stage] + u
                if later is not None:
                    weights_lo(dve, *later)
                if stage[-2:] == "in" and u % 2:
                    full(dve, "lin", tile)
                    taken(dve, "lin", tile - 1)
                    product = silu_g[:, nth % 2, 0:width]
                    frees(dve.tensor_tensor(product, lin[:, tile % RING, 0:width], product, ALU.mult), "lin", tile)
                    nth += 1
                elif stage[-3:] == "out":
                    if stage[4] == "b":
                        taken(dve, "lin", lin_of[f"ffn{n}a_out"] + u)
                    gated_tile(dve, tile, u, n, 5, width // L)
            for m in range(RING):
                taken(dve, "lin", lin_of[f"ffn{n}b_out"] + KT - 1 - m)

        def convolve(dve, own, n):
            tile = lin_of["ssm_in"] + n
            full(dve, "lin", tile)
            if n < 8:
                dst = bm[:, n, :].rearrange("p (a b) -> p a b", a=2)
            elif n < 24:
                dst = xs_pair[:, n - 8]
            else:
                dst = cm[:, n - 24, :].unsqueeze(1)
            src = lin[:, tile % RING, 0:L * dst.shape[1]].rearrange("p (a b) -> p a b", b=L)
            w = lambda m: conv_w[:, n, m:m + 1]
            own.link(dve.tensor_scalar(dst, src, w(1), w(3), ALU.mult, ALU.add))
            own.link(dve.scalar_tensor_tensor(out=dst[:, :, 1:L], in0=src[:, :, 0:L - 1], scalar=w(0),
                                              in1=dst[:, :, 1:L], op0=ALU.mult, op1=ALU.add))
            frees(dve.scalar_tensor_tensor(out=dst[:, :, 0:L - 1], in0=src[:, :, 1:L], scalar=w(2),
                                           in1=dst[:, :, 0:L - 1], op0=ALU.mult, op1=ALU.add), "lin", tile)

        def second_block_vector(dve, own):
            tt, ts, stt = dve.tensor_tensor, dve.tensor_scalar, dve.scalar_tensor_tensor
            dve.wait_ge(sig("ada_summed"), 48)
            own.link(tt(mod[:].rearrange("p a b c -> p (a b) c"), modp[:, L:L + 192].rearrange("p (a b) -> p a b", b=2),
                        each(modb[:].rearrange("p a b -> p (a b)"), 2), ALU.add))
            own.mark(dve.tensor_copy(nsink2[:, 0, :], nsink2_in[:]))
            own.mark(ts(nsink2[:, 1, :], nsink2_in[:], -1.0, None, ALU.mult))
            for u in range(W_UNITS):
                weights_lo(dve, "qkv", u)
            modulated(dve, own, 2, 2 * L, 0, 0, 0)
            for u in range(W_UNITS, 12):
                weights_lo(dve, "qkv", u)
            dve.wait_ge(sig("at_in"), 48)
            own.mark(dve.tensor_copy(ident_b, ident[:]))
            dve.tensor_copy(mask_b2, mask2).then_inc(sig("masks2"), 1)
            for n in (0, 1, 2, 3, 4):
                tile = aux_of["rope"] + n
                part = (k2 if n == 0 else q2[:, 2 * n - 2:2 * n])[:, :, 0:L]
                full(dve, "aux", tile)
                frees(tt(rope_tmp, aux[:, tile % AUX].rearrange("p (a b) -> p a b", a=2), twice(rope_cs[:, 1, :]),
                         ALU.mult), "aux", tile)
                own.link(tt(part, part, twice(rope_cs[:, 0, :]), ALU.mult))
                taken(dve, "aux", tile)
                own.link(tt(part, part, rope_tmp, ALU.add))
            dve.sem_inc(sig("roped"), 1)
            for i in range(AT_HEADS + 3):
                if i < AT_HEADS:
                    for n in range(3):
                        tile = score_tile(i, n)
                        full(dve, "aux", tile)
                        if n < 2:
                            own.mark(dve.tensor_reduce(stat2[:, 0, i, n:n + 1], aux[:, tile % AUX, :], AX_X, ALU.max))
                        else:
                            own.link(dve.tensor_reduce(
                                stat2[:, 0, i, 2:4], aux[:, tile % AUX].rearrange("p (a b) -> p a b", a=2), AX_X, ALU.max))
                    ts(stat2[:, 1, i, :], stat2[:, 0, i, :], -AT_SCALE, nsink2[:, 1, i:i + 1], ALU.mult, ALU.min)\
                        .then_inc(sig("maxima2"), 1)
                if 1 <= i <= AT_HEADS:
                    h = i - 1
                    dve.wait_ge(sig("exps2"), h + 1)
                    own.link(tt(stat2[:, 4, h, :], stat2[:, 2, h, :], stat2[:, 3, h, :], ALU.add))
                    own.link(dve.reciprocal(stat2[:, 5, h, :], stat2[:, 4, h, :]))
                    for n, (part, cols) in enumerate(((0, slice(0, 2 * L)), (1, slice(0, 2 * L)),
                                                      (2, slice(0, L)), (2, slice(L, 2 * L)))):
                        p = p2[:, h % 3, part, cols]
                        ins = ts(p, p, stat2[:, 5, h, n:n + 1], None, ALU.mult)
                    ins.then_inc(sig("probs2"), 1)
                if 9 <= i < 12:
                    weights_lo(dve, "w_o", i - 9)
                if i >= 4 and i % 2 == 0:
                    n = i // 2 - 2
                    tile = output_tile(n)
                    full(dve, "lin", tile)
                    own.link(dve.tensor_copy(hn_hi[:, n, :], lin[:, tile % RING, :]))
                    frees(tt(out_lo[:, n, :], lin[:, tile % RING, :], hn_hi[:, n, :].bitcast(F32), ALU.subtract),
                          "lin", tile)
            weights_lo(dve, "w_o", 3)
            for n in range(KT):
                weights_lo(dve, *(("w_o", n + W_UNITS) if n < W_UNITS else ("ffn0a_in", n - W_UNITS)))
                gated_tile(dve, lin_of["w_o"] + n, n, 0, 2, 2)
            for n in range(RING):
                taken(dve, "lin", lin_of["w_o"] + KT - 1 - n)
            modulated(dve, own, 3, 2 * L, 0, 3, 1)
            ffn_vector(dve, 0, 2 * L)
            weights_lo(dve, "ssm_dt", 0)
            weights_lo(dve, "ssm_in", 0)
            modulated(dve, own, 4, 2 * L, 1, 0, 2)
            weights_lo(dve, "ssm_in", 1)
            tile = lin_of["ssm_dt"]
            full(dve, "lin", tile)
            frees(ts(dt2, lin[0:64, tile % RING, :], dt_cols[:, 0:1], None, ALU.add), "lin", tile)
            taken(dve, "lin", tile)
            stt(out=dt_tmp, in0=dt2, scalar=-1.0, in1=dt2, op0=ALU.mult, op1=ALU.max).then_inc(sig("dt_abs"), 1)
            weights_lo(dve, "ssm_in", 2)
            dve.wait_ge(sig("dt_exp"), 1)
            own.mark(ts(dt2, dt2, 0.0, None, ALU.max))
            own.link(ts(da, dt_tmp, 1.0, None, ALU.add))
            own.mark(tt(dt2, dt2, dt_tmp2, ALU.add))
            own.link(ts(dt_tmp3, da, 1.0, None, ALU.subtract))
            own.link(tt(dt_tmp, dt_tmp, dt_tmp3, ALU.subtract))
            own.link(dve.reciprocal(da, da))
            own.link(tt(da, da, dt_tmp, ALU.mult))
            own.link(tt(dt2, dt2, da, ALU.add))
            own.link(ts(da, dt2, a_neg, -1.0, ALU.mult, ALU.mult))
            weights_lo(dve, "ssm_in", 3)
            dve.wait_ge(sig("ssm_in"), 32)
            convolve(dve, own, 0)
            convolve(dve, own, 1)
            one = ones[0:64, 0:1].to_broadcast([64, L])
            own.mark(dve.tensor_tensor_scan(rows_g[0:64], one, da[:, 0:L], 0.0, ALU.mult, ALU.add))
            own.link(dve.tensor_tensor_scan(dt_tmp[:, L:2 * L], one, da[:, L:2 * L], 0.0, ALU.mult, ALU.add))
            own.mark(dve.tensor_copy(tot[:, 0:1], rows_g[0:64, L - 1:L]))
            own.link(dve.tensor_copy(tot[:, 1:2], dt_tmp[:, 2 * L - 1:2 * L]))
            back = slice(32, 64)
            own.mark(ts(rows_g[back], rows_g[back], -1.0, tot[back, 0:1], ALU.mult, ALU.add))
            own.link(ts(dt_tmp[back, L:2 * L], dt_tmp[back, L:2 * L], -1.0, tot[back, 1:2], ALU.mult, ALU.add))
            own.mark(tt(rows_g[back], rows_g[back], da[back, 0:L], ALU.add))
            tt(dt_tmp[back, L:2 * L], dt_tmp[back, L:2 * L], da[back, L:2 * L], ALU.add).then_inc(sig("dt_summed"), 1)
            for n in range(2, 46):
                weights_lo(dve, "ssm_in", n + 2)
                if n < 32:
                    convolve(dve, own, n)
                if n == 4:
                    dve.wait_ge(sig("dt_weights"), 1)
                    own.mark(dve.tensor_copy(ident_split[0:64], ident[0:64, 0:64]))
                    own.link(ts(rows_neg, rows_g[0:64], -1.0, None, ALU.mult))
                    own.link(dve.tensor_copy(rows_split[0:64, 0], rows_neg))
                    tt(rows_split[0:64, 1], rows_neg, rows_split[0:64, 0].bitcast(F32), ALU.subtract)
                    tt(dt2[:, L:2 * L], dt_tmp[:, L:2 * L], dt2[:, L:2 * L], ALU.mult).then_inc(sig("dt_rows"), 1)
            turned_copies(dve, "bc_tok", 4, bc_tok, 2, 1, dve.tensor_copy)
            turned_copies(dve, "xc_tok", 8, xc_tok, 4, 1, dve.tensor_copy)
            for n in range(AUX):
                taken(dve, "aux", aux_of["xc_tok"] + 7 - n)
            taken(dve, "aux", aux_of["ssm_rows"])
            for g in range(GROUPS):
                if g >= 1:
                    full(dve, "aux", aux_of["states"] + g - 1)
                for d in range(2):
                    for qt in range(QT):
                        heads = cols_g[:, 2, qt, d * 32 + 4 * g:d * 32 + 4 * g + 4]
                        ins = tt(xw[:, d, qt].rearrange("p (a b) -> p a b", a=4),
                                 xc_tok[:, qt, g * L:(g + 1) * L].rearrange("p (a b) -> p a b", a=4),
                                 each(heads, 64), ALU.mult)
                ins.then_inc(sig("x_weighted"), 1)
            turned_copies(dve, "x_tok", 8, x_tok, 4, 1, dve.tensor_copy)

            def y_out(n):
                tile = lin_of["ssm_y"] + n
                full(dve, "lin", tile)
                frees(stt(out=ys[:, n], in0=ys[:, n], scalar=ssm_cols[:, 0, n:n + 1], in1=lin[:, tile % RING, 0:L],
                          op0=ALU.mult, op1=ALU.add), "lin", tile)

            for i in range(DT_ + 3):
                if i < DT_ and i % 2 == 0:
                    g = i // 2
                    tile = cb_tile(g)
                    full(dve, "aux", tile)
                    c, products = cb[:, g % 2], aux[:, tile % AUX]
                    if g == 0:
                        for n in range(AUX):
                            taken(dve, "aux", aux_of["states"] + GROUPS - 1 - n)
                    own.mark(tt(c[:, 0, 0:P], products[:, 0:P], tri[:, 0], ALU.mult))
                    own.mark(dve.tensor_copy(c[:, 0, P:L], products[:, P:L]))
                    own.mark(tt(c[:, 1, 0:P], products[:, 3 * P:4 * P], tri[:, 0], ALU.mult))
                    own.mark(tt(c[:, 1, P:L], products[:, 0:P], tri[:, 1], ALU.mult))
                    own.mark(dve.tensor_copy(c[:, 2, 0:P], products[:, L:3 * P]))
                    frees(tt(c[:, 2, P:L], products[:, 3 * P:4 * P], tri[:, 1], ALU.mult), "aux", tile)
                for h in range(2 * i, 2 * i + 2) if i < DT_ else ():
                    tile = bc_tile(h)
                    full(dve, "aux", tile)
                    if i >= 3:
                        full(dve, "lin", lin_of["ssm_y"] + i - 3)
                    for d, qt, lo_, hi_, at in parts[1:3]:
                        ins = ts(decay[i % 3][:, h % 2, at:at + hi_ - lo_], aux[:, tile % AUX, d * L + lo_:d * L + hi_],
                                 cols_g[:, 0, qt, d * 32 + h:d * 32 + h + 1], 0.0, ALU.add, ALU.max)
                    ins.then_inc(sig("gaps"), 1)
                for h in range(2 * i - 2, 2 * i) if 1 <= i <= DT_ else ():
                    taken(dve, "aux", cb_tile(h // 4))
                    dve.wait_ge(sig("decays"), h + 1)
                    for d, qt, lo_, hi_, at in parts:
                        m = decay[(i - 1) % 3][:, h % 2, at:at + hi_ - lo_]
                        ins = stt(out=m, in0=m, scalar=cols_g[:, 1, qt, d * 32 + h:d * 32 + h + 1],
                                  in1=cb[:, h // 4 % 2, at // L, at % L:at % L + hi_ - lo_], op0=ALU.mult, op1=ALU.mult)
                    ins.then_inc(sig("mixed"), 1)
                if 3 <= i < DT_ + 2:
                    y_out(i - 3)
            y_out(DT_ - 1)
            inverses(dve, "y_norm", 2 * GROUPS)
            for n in range(DT_):
                tile = aux_of["y_norm"] + 1 + n // 4
                full(dve, "aux", tile)
                ins = stt(out=ys[:, n], in0=ys[:, n], scalar=ssm_cols[:, 1, n:n + 1],
                          in1=aux[:, tile % AUX, n // 2 % 2 * L:(n // 2 % 2 + 1) * L], op0=ALU.mult, op1=ALU.mult)
                if n % 4 == 3:
                    frees(ins, "aux", tile)
            gated_add(dve, own, "ssm_out", 1, 2, 1)
            for u in range(W_UNITS):
                weights_lo(dve, "ffn1a_in", u)
            modulated(dve, own, 5, L, 1, 3, 3)
            ffn_vector(dve, 1, L)
            normed(dve, 6, L, lambda kt, s: g2[:, 4, kt:kt + 1])

        @block.scalar
        def _(act):
            own = Count(act, sig("act_own"))
            for dst, name in ((relb, "relb"), (hot, "hot")):
                act.dma_start(dst, t[name]).then_inc(sig("rel_in"), 16)
            act.dma_start(ident[:], t["ident"]).then_inc(sig("norm_in"), 16)
            act.dma_start(gcol[:], t["gcol"]).then_inc(sig("norm_in"), 16)
            copies(act, "bias", EV_HEADS, lambda ps: ps[:, 0:3 * P], lambda h: table[:, h, :])
            act.wait_ge(sig("x_in"), 16)
            act.wait_ge(sig("made"), 1)
            act_norm(act, 0, L)
            act.wait_ge(sig("s5_in"), 32)
            act.activation(par[:, 3, :], par[:, 0, :], ACT.Exp).then_inc(sig("s5_dt"), 1)
            act.wait_ge(sig("s5_phase"), 1)
            own.mark(act.activation(par[:, 8, :], par[:, 4, :], ACT.Exp))
            own.mark(act.activation(par[:, 9, :], par[:, 6, :], ACT.Sin))
            act.activation(par[:, 10, :], par[:, 7, :], ACT.Sin, scale=-1.0, bias=half_pi[:])\
                .then_inc(sig("s5_trig"), 1)
            into = [u[:, n] for n in range(4)] + [ka, va] + [qa[:, n] for n in range(4)] + \
                [gate_a[:, n] for n in range(4)] + [gate_b[:, n] for n in range(4)]
            for n, dst in enumerate(into):
                tile = lin_of["ev_in"] + n
                full(act, "lin", tile)
                frees(act.activation(dst, lin[:, tile % RING, 0:L], ACT.Silu if n >= 10 else ACT.Copy), "lin", tile)
                if 2 <= n < 10:
                    for j in range(2 * (n - 2), 2 * (n - 2) + 2):
                        act.wait_ge(sig("turns"), j + 1)
                        own.mark(act.activation(cos_t[:, j, :], cos_t[:, j, :], ACT.Sin, scale=-TWO_PI,
                                                bias=half_pi[:]))
                        act.activation(sin_t[:, j, :], sin_t[:, j, :], ACT.Sin, scale=TWO_PI * (1 - 2e-7))\
                            .then_inc(sig("phases"), 1)
            act.wait_ge(sig("const_in"), 208)
            act.activation(sc_c[:], sc_c[:], ACT.Silu).then_inc(sig("silu_c"), 1)
            copies(act, "s5_bb", 2, lambda ps: ps, lambda n: bb_t[:, n].rearrange("p a b -> p (a b)"))
            taken(act, "lin", lin_of["ev_in"] + 17)
            act.wait_ge(sig("table_out"), 16)
            own.mark(act.activation(sq0[:, 0, :], ka, ACT.Square))
            act.activation(sq0[:, 1:5, :], qa, ACT.Square).then_inc(sig("squares_qk0"), 1)
            roots(act, "qk_norm0", 20, 1.0 / 64)
            copies(act, "v_tok0", 1, lambda ps: ps[:, 0:L], lambda n: v_tok.rearrange("p a b -> p (a b)"))
            ada_copies(act, 0, 4)
            softmax_exps(act, own, 0, (lg0, lg1), small, True)
            ada_copies(act, 4, 4)
            copies(act, "probs0", EV_HEADS, lambda ps: ps[:, 0:3 * P], lambda h: pt[:, h, :])
            ada_copies(act, 8, SSM_TILES)
            taken(act, "lin", lin_of["s5_y"] + 3)
            act.activation(u, u, ACT.Gelu_apprx_tanh).then_inc(sig("s5_gelu"), 1)
            for n in range(4):
                tile = lin_of["glu"] + 2 * n + 1
                full(act, "lin", tile)
                frees(act.activation(qa[:, n], lin[:, tile % RING, 0:L], ACT.Sigmoid, bias=glu_b[:, 4 + n:5 + n]),
                      "lin", tile)
            for m in range(2):
                weights_hi(act, "od_in", m)
            act_norm(act, 1, L, "ev_out")
            for kt in range(KT):
                act.wait_ge(sig("hn_ready"), KT + kt + 1)
                act.activation(od_hi[:, kt, :], hn[:, kt, 0:L], ACT.Copy).then_inc(sig("od_high"), 1)
            for m in range(2, W_UNITS):
                weights_hi(act, "od_in", m)
            into = [ki] + [qi[:, n] for n in range(4)] + [k1[:, n] for n in range(2)] + \
                [v1[:, n] for n in range(2)] + [q1[:, n] for n in range(8)] + [gate1[:, n] for n in range(8)]
            for n, dst in enumerate(into):
                tile = lin_of["od_ki"] + n
                if 1 <= n <= 24 - W_UNITS:
                    weights_hi(act, "od_in", n - 1 + W_UNITS)
                full(act, "lin", tile)
                frees(act.activation(dst, lin[:, tile % RING, 0:L], ACT.Silu if n >= 17 else ACT.Copy), "lin", tile)
                if n >= 6 and n % 2 == 0 and (n - 6) // 2 < 6:
                    m = (n - 6) // 2
                    tile = aux_of["index"] + m
                    full(act, "aux", tile)
                    if m >= 2:
                        act.wait_ge(sig("rel_used"), m - 1)
                    frees(act.activation(rel[:, m % 2], aux[:, tile % AUX], ACT.Relu, scale=64 ** -0.5), "aux", tile)
                if n >= 2 and n % 2 == 0:
                    ada_copies(act, 24 + n // 2 - 1, 1)
            taken(act, "lin", lin_of["od_in"] + 23)
            own.mark(act.activation(sq1[:, 0:2, :], k1, ACT.Square))
            act.activation(sq1[:, 2:10, :], q1, ACT.Square).then_inc(sig("squares_qk1"), 1)
            roots(act, "kq_norm1", 20, 1.0 / P)
            copies(act, "v_tok1", 1, lambda ps: ps, lambda n: v_tok1.rearrange("p a b -> p (a b)"))
            ada_copies(act, 36, 12)
            softmax_exps(act, own, 1, (lh0, lh1), small, False)
            copies(act, "probs1", OD_HEADS, lambda ps: ps[:, 0:3 * P], lambda h: pt1[:, h, :])
            second_block_scalar(act, own)

        @block.vector
        def _(dve):
            own = Count(dve, sig("dve_own"))
            tt, ts, stt = dve.tensor_tensor, dve.tensor_scalar, dve.scalar_tensor_tensor
            dve.wait_ge(sig("norm_in"), 32)
            normed(dve, 0, L, lambda kt, s: gcol[:, 0, kt:kt + 1])
            dve.wait_ge(sig("steps_in"), 16)
            (log_dt, a_re, a_im, dt, z, turn, phase, phase_abs, mag, sin1, cos1, hi, lo, k, den, n_re, n_im,
             f_re, f_im, tmp, tmp2) = (par[:, n, :] for n in range(21))
            dve.wait_ge(sig("s5_dt"), 1)
            own.mark(tt(z, a_re, dt, ALU.mult))
            own.link(tt(phase, a_im, dt, ALU.mult))
            own.link(ts(k, phase, 1.0 / TWO_PI, ROUND, ALU.mult, ALU.add))
            own.link(ts(k, k, ROUND, None, ALU.subtract))
            for part in (PI2_A, PI2_B, PI2_C):
                own.link(stt(out=phase, in0=k, scalar=-part, in1=phase, op0=ALU.mult, op1=ALU.add))
            own.link(ts(phase, phase, math.pi * (1 - 1e-7), -math.pi * (1 - 1e-7), ALU.min, ALU.max))
            own.link(ts(turn, phase, 1.0 / TWO_PI, None, ALU.mult))
            stt(out=phase_abs, in0=phase, scalar=-1.0, in1=phase, op0=ALU.mult, op1=ALU.max).then_inc(sig("s5_phase"), 1)
            own.link(ts(tmp, turn, 4097.0, None, ALU.mult))
            own.link(tt(tmp2, tmp, turn, ALU.subtract))
            own.link(tt(hi, tmp, tmp2, ALU.subtract))
            own.link(tt(lo, turn, hi, ALU.subtract))
            for j in range(SSM_TILES):
                frac, whole = sin_t[:, j, :], cos_t[:, j, :]
                own.link(ts(frac, steps, hi[:, j:j + 1], None, ALU.mult))
                own.link(ts(whole, frac, ROUND, ROUND, ALU.add, ALU.subtract))
                own.link(tt(frac, frac, whole, ALU.subtract))
                own.link(stt(out=frac, in0=steps, scalar=lo[:, j:j + 1], in1=frac, op0=ALU.mult, op1=ALU.add))
                own.link(ts(whole, frac, ROUND, ROUND, ALU.add, ALU.subtract))
                own.link(tt(frac, frac, whole, ALU.subtract))
                stt(out=whole, in0=frac, scalar=-1.0, in1=frac, op0=ALU.mult, op1=ALU.max).then_inc(sig("turns"), 1)
            dve.wait_ge(sig("s5_trig"), 1)
            own.mark(tt(n_re, mag, cos1, ALU.mult))
            own.mark(tt(n_im, mag, sin1, ALU.mult))
            own.mark(tt(den, a_re, a_re, ALU.mult))
            own.link(tt(tmp, a_im, a_im, ALU.mult))
            own.mark(ts(n_re, n_re, 1.0, None, ALU.subtract))
            own.link(tt(den, den, tmp, ALU.add))
            own.mark(dve.reciprocal(den, den))
            own.mark(tt(f_re, n_re, a_re, ALU.mult))
            own.mark(tt(tmp, n_im, a_im, ALU.mult))
            own.mark(tt(f_im, n_im, a_re, ALU.mult))
            own.link(tt(tmp2, n_re, a_im, ALU.mult))
            own.mark(tt(f_re, f_re, tmp, ALU.add))
            own.link(tt(f_im, f_im, tmp2, ALU.subtract))
            own.mark(tt(f_re, f_re, den, ALU.mult))
            own.link(tt(f_im, f_im, den, ALU.mult))
            bt = s5w[:, 0].rearrange("p a b -> p (a b)")[:, 0:256].rearrange("p (a b) -> p a b", a=16)
            for part, (f1, b1, f2, b2, op) in enumerate(((f_re, 0, f_im, 1, ALU.subtract), (f_re, 1, f_im, 0, ALU.add))):
                s5p = s5t[:, part, 0:256].rearrange("p (a b) -> p a b", a=16)
                own.mark(tt(bt, each(f1, 16), b_in[:, b1], ALU.mult))
                own.link(tt(s5p, each(f2, 16), b_in[:, b2], ALU.mult))
                for n in range(2):
                    rows = slice(64 * n, 64 * n + 64)
                    own.link(tt(bd[rows, part, :, 16 * n:16 * n + 16], bt[rows], s5p[rows], op))
            dve.wait_ge(sig("c_in"), 64)
            ts(c_bd[:, 1], c_bd[:, 1], -1.0, None, ALU.mult).then_inc(sig("bd_ready"), 1)
            dve.wait_ge(sig("const_in"), 208)
            dve.wait_ge(sig("table_back"), 16)
            own.link(tt(bias_a, bias_b, mask_a.unsqueeze(1).to_broadcast([P, EV_HEADS, L]), ALU.add))
            own.link(tt(bias_b, bias_b, mask_b.unsqueeze(1).to_broadcast([P, EV_HEADS, L]), ALU.add))
            inverses(dve, "qk_norm0", 20)
            over_roots(dve, "qk_norm0", [(ka, qk_g[:, 1:2])] + [(qa[:, n], qk_g[:, 0:1]) for n in range(4)])
            scaled_logits(dve, own, 0, bias_a, (lg0, lg1), 64 ** -0.5)
            maxima(dve, own, 0, (lg0, lg1), small, sink[:])
            probabilities(dve, own, 0, (lg0, lg1), small, True)
            for n in range(4):
                tile = aux_of["out0"] + n
                full(dve, "aux", tile)
                frees(tt(cat[:, n, :], aux[:, tile % AUX, 0:L], gate_a[:, n, :], ALU.mult), "aux", tile)

            dve.wait_ge(sig("phases"), SSM_TILES)
            for j in range(SSM_TILES):
                p = j % 2
                tile = aux_of["s5_bu"] + j
                bu = aux[:, tile % AUX].rearrange("p (a b) -> p a b", a=2)
                w, ti, z2 = s5w[:, p], s5t[:, p].rearrange("p (a b) -> p a b", a=2), s5z[:, p]
                full(dve, "aux", tile)
                own.mark(tt(w, bu, twice(cos_t[:, j, :]), ALU.mult))
                frees(tt(ti, bu, twice(sin_t[:, j, :]), ALU.mult), "aux", tile)
                taken(dve, "aux", tile)
                own.mark(tt(w[:, 0], w[:, 0], ti[:, 1], ALU.add))
                own.link(tt(w[:, 1], w[:, 1], ti[:, 0], ALU.subtract))
                if j >= 2:
                    dve.wait_ge(sig("x_states"), j - 1)
                decay = mag[:, j:j + 1].to_broadcast([P, L])
                own.mark(dve.tensor_tensor_scan(z2[:, 0], decay, w[:, 0], 0.0, ALU.mult, ALU.add))
                dve.tensor_tensor_scan(z2[:, 1], decay, w[:, 1], 0.0, ALU.mult, ALU.add)\
                    .then_inc(sig("z_ready"), 1)
                dve.wait_ge(sig("z_ready"), j + 1)
                tt(s5_back[:, p], z2, twice(sin_t[:, j, :]), ALU.mult).then_inc(sig("z_turned"), 1)
            for n in range(4):
                tile = lin_of["s5_y"] + n
                dve.wait_ge(sig("s5_used"), n + 1)
                frees(stt(out=u[:, n], in0=u[:, n], scalar=d_col[:, n:n + 1], in1=lin[:, tile % RING, 0:L],
                          op0=ALU.mult, op1=ALU.add), "lin", tile)
                taken(dve, "lin", tile)
            for n in range(4):
                tile = lin_of["glu"] + 2 * n
                full(dve, "lin", tile)
                taken(dve, "lin", tile + 1)
                frees(stt(out=qa[:, n], in0=lin[:, tile % RING, 0:L], scalar=glu_b[:, n:n + 1], in1=qa[:, n],
                          op0=ALU.add, op1=ALU.mult), "lin", tile)
                taken(dve, "lin", tile)
                tt(cat[:, 4 + n, :], qa[:, n], gate_b[:, n], ALU.mult).then_inc(sig("cat_ready"), 1)

            def add_to_x(name):
                for n in range(KT):
                    tile = lin_of[name] + n
                    full(dve, "lin", tile)
                    frees(tt(xres[:, n, 0:L], lin[:, tile % RING, 0:L], xres[:, n, 0:L], ALU.add), "lin", tile)
                    taken(dve, "lin", tile)

            add_to_x("ev_out")
            normed(dve, 1, L, lambda kt, s: gcol[:, 1, kt:kt + 1])
            tile = aux_of["wi"]
            full(dve, "aux", tile)
            frees(ts(wi, aux[:, tile % AUX, 0:16].rearrange("p (a b) -> p a b", a=2), OD_HEADS ** -0.5, None,
                     ALU.mult), "aux", tile)
            taken(dve, "aux", tile)
            own.mark(dve.tensor_copy(idx[:, 0, 0:P], mask_b[:, P:L]))
            own.link(dve.tensor_copy(idx[:, 1, :], mask_b))
            for m in range(6):
                taken(dve, "aux", aux_of["index"] + m)
                qt, heads, width = index_heads(m)
                for n, h in enumerate(heads):
                    ins = stt(out=idx[:, qt, 0:width], in0=rel[:, m % 2, n * width:(n + 1) * width],
                              scalar=wi[:, qt, h:h + 1], in1=idx[:, qt, 0:width], op0=ALU.mult, op1=ALU.add)
                    if n < len(heads) - 1:
                        own.link(ins)
                ins.then_inc(sig("rel_used"), 1)
                dve.wait_ge(sig("rel_used"), m + 1)
            for r in range(TOPK // 8):
                for qt, width in ((0, P), (1, L)):
                    own.mark(dve.max(top[:, qt, :], idx[:, qt, 0:width]))
                own.settle()
                for qt, width in ((0, P), (1, L)):
                    own.mark(dve.match_replace(idx[:, qt, 0:width], top[:, qt, :], idx[:, qt, 0:width], TAKEN))
                own.settle()
            for qt, width in ((0, P), (1, L)):
                own.mark(ts(sel[:, qt, 0:width], idx[:, qt, 0:width], TAKEN / 2, NEG, ALU.is_gt, ALU.mult))
            inverses(dve, "kq_norm1", 20)
            over_roots(dve, "kq_norm1", [(k1[:, n], qk_g[:, 3:4]) for n in range(2)] +
                       [(q1[:, n], qk_g[:, 2:3]) for n in range(8)])
            scaled_logits(dve, own, 1, bias_b, (lh0, lh1), P ** -0.5)
            own.mark(tt(lh0, lh0, sel[:, 0, 0:P].unsqueeze(1).to_broadcast([P, OD_HEADS, P]), ALU.add))
            own.link(tt(lh1, lh1, sel[:, 1, :].unsqueeze(1).to_broadcast([P, OD_HEADS, L]), ALU.add))
            maxima(dve, own, 1, (lh0, lh1), small, None)
            probabilities(dve, own, 1, (lh0, lh1), small, False)
            for n in range(8):
                tile = aux_of["out1"] + n
                full(dve, "aux", tile)
                frees(tt(q1[:, n, :], aux[:, tile % AUX, 0:L], gate1[:, n, :], ALU.mult), "aux", tile)
            add_to_x("od_out")
            second_block_vector(dve, own)

        @block.tensor
        def _(pe):
            mm = nc.tensor.matmul

            def begin(banks, tile):
                sems_, n = (lin_free, RING) if banks == "lin" else (aux_free, AUX)
                if isinstance(tile, int) and tile < n:
                    return
                pe.wait_ge(sems_[tile % n], tile // n)

            def fills(ins, banks):
                ins.then_inc(sig(banks + "_full"), 1)

            def linear(name, stage, tiles, kts, rhs, width=L, m=P, norm=None, ready=None):
                count = dict((x, y) for x, y, _ in STREAM)[name]
                first, tile0 = block_of[name], lin_of[stage]

                def one(i, k):
                    b = first + k
                    pe.wait_ge(w_in[b % RING], (i + (b // RING + 1)) * 16)
                    for j in range(tiles):
                        tile = tile0 + k * tiles + j
                        bank = tile % RING
                        if not isinstance(i, int) or tile + i * RING * tiles >= RING:
                            pe.wait_ge(lin_free[bank], i * tiles + tile // RING)
                        for kt in range(kts):
                            at = (j * kts + kt) * m
                            if norm is not None and isinstance(i, int) and i == k == j == 0:
                                pe.wait_ge(sig("hn_ready"), KT * norm + kt + 1)
                            if ready is not None and isinstance(i, int) and i == k == j == 0:
                                ready(kt)
                            ins = mm(lin[0:m, bank, 0:width], ring[:, b % RING, at:at + m], rhs(kt),
                                     start=kt == 0, stop=kt == kts - 1)
                        fills(ins, "lin")

                rounds(pe, count, one)

            def split_unit(name, u, kts, x, width, m=P, waits=None):
                parts, _, _ = unit(name, u)
                tile = lin_of[name] + u
                begin("lin", tile)
                pe.wait_ge(sig("w_low"), unit_of[name] + u + 1)
                for kt in range(kts):
                    if waits is not None:
                        pe.wait_ge(sig(waits[0]), waits[1] + kt + 1)
                    hi, lo = (parts[:, part, kt * m:(kt + 1) * m] for part in range(2))
                    x_hi, x_lo = x(kt)
                    mm(lin[0:m, tile % RING, 0:width], hi, x_hi, start=kt == 0, stop=False)
                    mm(lin[0:m, tile % RING, 0:width], hi, x_lo, start=False, stop=False)
                    ins = mm(lin[0:m, tile % RING, 0:width], lo, x_hi, start=False, stop=kt == kts - 1)
                fills(ins, "lin")

            def split_linear(name, kts, x, width, waits=None):
                for u in range(dict(SPLIT)[name]):
                    split_unit(name, u, kts, x, width, waits=waits if u == 0 else None)

            ada_at = [0]

            def ada_groups(n):
                pe.wait_ge(sig("ada_copied"), n + 1)
                for j in range(2):
                    at = L + (2 * n + j) * 2
                    ins = mm(modp[:, at:at + 2], ada_sb[:, j * P:(j + 1) * P], group_sum[:], start=True, stop=True)
                ins.then_inc(sig("ada_summed"), 1)

            def ada(blocks):
                for n in range(ada_at[0], ada_at[0] + blocks):
                    b = block_of["ada0"] + n if n < 24 else block_of["od_in"] + 2 * (n - 24) + 1 if n < 36 else \
                        block_of["ada1"] + n - 36
                    if n == 0:
                        pe.wait_ge(sig("silu_c"), 1)
                    else:
                        pe.wait_ge(sig("ada_copied"), n)
                    pe.wait_ge(w_in[b % RING], 16 * (b // RING + 1))
                    for kt in range(KT):
                        rows = slice(32 * (kt % 4), 32 * (kt % 4) + 32)
                        ins = mm(modp[rows, 0:L], sc_c[:, kt, :], ring[:, b % RING, kt * L:(kt + 1) * L],
                                 start=kt < 4, stop=kt >= 4)
                    ins.then_inc(sig("ada_used"), 1)
                    if n:
                        ada_groups(n - 1)
                ada_at[0] += blocks

            def head_norms(name, groups, parts, src, squares=None):
                tile = aux_of[name]
                begin("aux", tile)
                select = pair[:, 0:P:P // 2] if parts == 2 else ones[:, 0:1]
                for n, terms in enumerate(groups):
                    if squares is not None:
                        pe.wait_ge(sig(squares), terms[-1] + 1)
                    for qt in range(QT):
                        at = (n * QT + qt) * parts
                        for kt in terms:
                            ins = mm(aux[:, tile % AUX, at:at + parts], src(kt)[:, qt * P:(qt + 1) * P], select,
                                     start=kt == terms[0], stop=kt == terms[-1])
                fills(ins, "aux")
                pe.wait_ge(sig(name), 1)
                for n in range(len(groups)):
                    if n % 2 == 0:
                        tile += 1
                        begin("aux", tile)
                    for qt in range(QT):
                        at = (n % 2 * QT + qt) * P
                        col = (n * QT + qt) * parts
                        for part in range(parts):
                            rows = slice(part * P // parts, (part + 1) * P // parts)
                            ins = mm(aux[rows, tile % AUX, at:at + P],
                                     head_roots[:, col + part:col + part + 1].to_broadcast([P, P // parts]), ident[:],
                                     start=True, stop=True)
                    if n % 2 or n == len(groups) - 1:
                        fills(ins, "aux")

            def norm(k, width):
                tile = aux_of[f"norm{k}"]
                begin("aux", tile)
                pe.wait_ge(sig("square_sums"), k + 1)
                for n in range(width // P):
                    ins = mm(aux[:, tile % AUX, n:n + 1], hn[:, 0, n * P:(n + 1) * P], ones[:, 0:1],
                             start=True, stop=True)
                fills(ins, "aux")
                begin("aux", tile + 1)
                pe.wait_ge(sig("rms"), k + 1)
                for n in range(width // P):
                    ins = mm(aux[:, (tile + 1) % AUX, n * P:(n + 1) * P], rcol[:, n:n + 1].to_broadcast([P, P]),
                             ident[:], start=True, stop=True)
                fills(ins, "aux")

            pe.wait_ge(sig("rel_in"), 32)
            for h in range(EV_HEADS):
                tile = aux_of["bias"] + h
                begin("aux", tile)
                fills(mm(aux[:, tile % AUX, 0:3 * P], relb[:, h, :], hot, start=True, stop=True), "aux")
            pe.wait_ge(sig("made"), 1)
            pe.wait_ge(sig("norm_in"), 32)
            norm(0, L)
            linear("ev_in", "ev_in", 2, KT, lambda kt: hn[:, kt, 0:L], norm=0)
            pe.wait_ge(sig("bd_ready"), 1)
            for part in range(2):
                tile = aux_of["s5_bb"] + part
                begin("aux", tile)
                for n in range(4):
                    ins = nc.tensor.transpose(aux[:, tile % AUX, n * P:(n + 1) * P],
                                              bd[:, part, 4 * n:4 * n + 4, :].rearrange("p a b -> p (a b)"), ident[:])
                fills(ins, "aux")
            pe.wait_ge(sig("squares_qk0"), 1)
            head_norms("qk_norm0", [[n] for n in range(5)], 2, lambda n: sq0[:, n, :])

            def tokens(name, src, n_src):
                tile = aux_of[name]
                begin("aux", tile)
                for qt in range(QT):
                    for n in range(n_src):
                        at = (qt * n_src + n) * P
                        ins = nc.tensor.transpose(aux[:, tile % AUX, at:at + P], src(n)[:, qt * P:(qt + 1) * P],
                                                  ident[:])
                fills(ins, "aux")

            tokens("v_tok0", lambda n: va, 1)

            def scores(layer, q, k):
                for n in range(6):
                    tile = aux_of[f"scores{layer}"] + n
                    begin("aux", tile)
                    qt, heads, width = (0, range(4 * n, 4 * n + 4), P) if n < 2 else \
                        (1, range(2 * (n - 2), 2 * (n - 2) + 2), L)
                    for m, h in enumerate(heads):
                        ins = mm(aux[:, tile % AUX, m * width:(m + 1) * width], q(h, qt), k(h)[:, 0:width],
                                 start=True, stop=True)
                    fills(ins, "aux")

            def transposed_probs(layer, logits):
                pe.wait_ge(sig(f"probs{layer}"), 1)
                for h in range(8):
                    tile = aux_of[f"probs{layer}"] + h
                    begin("aux", tile)
                    for n, src in enumerate((logits[0][:, h, :], logits[1][:, h, 0:P], logits[1][:, h, P:L])):
                        ins = nc.tensor.transpose(aux[:, tile % AUX, n * P:(n + 1) * P], src, ident[:])
                    fills(ins, "aux")

            half = lambda ap, s: ap[64 * s:64 * s + 64]
            for n in range(3):
                taken(pe, "aux", aux_of["qk_norm0"] + 1 + n)
            scores(0, lambda h, qt: half(qa[:, h % 4, qt * P:(qt + 1) * P], h // 4), lambda h: half(ka, h // 4))
            ada(8)
            transposed_probs(0, (lg0, lg1))
            for j in range(4):
                tile = aux_of["out0"] + j
                begin("aux", tile)
                for s in range(2):
                    h = j + 4 * s
                    taken(pe, "aux", aux_of["probs0"] + h)
                    rows = slice(64 * s, 64 * s + 64)
                    mm(aux[rows, tile % AUX, 0:L], v_tok[:, 0, rows], pt[:, h, 0:L], start=True, stop=False)
                    ins = mm(aux[rows, tile % AUX, P:L], v_tok[:, 1, rows], pt[:, h, L:3 * P], start=False, stop=True)
                fills(ins, "aux")
            taken(pe, "aux", aux_of["s5_bb"] + 1)

            def s5_out(n):
                pe.wait_ge(sig("x_states"), 4 * n + 4)
                tile = lin_of["s5_y"] + n
                begin("lin", tile)
                for part in range(2):
                    for j in range(4 * n, 4 * n + 4):
                        rows = slice(32 * (j % 4), 32 * (j % 4) + 32)
                        ins = mm(lin[rows, tile % RING, 0:L], c_bd[:, part, j, :], s5_states[:, j % 8, part, :],
                                 start=part == 0, stop=part == 1)
                ins.then_inc(sig("s5_used"), 1)

            for j in range(SSM_TILES):
                tile = aux_of["s5_bu"] + j
                begin("aux", tile)
                rows = slice(32 * (j % 4), 32 * (j % 4) + 32)
                for part in range(2):
                    ins = mm(aux[:, tile % AUX, part * L:(part + 1) * L], bb_t[rows, part, j // 4, :],
                             u[rows, j // 4, :], start=True, stop=True)
                fills(ins, "aux")
                ada(1)
                if j % 4 == 1 and j > 4:
                    s5_out(j // 4 - 1)
            s5_out(SSM_TILES // 4 - 1)
            pe.wait_ge(sig("s5_gelu"), 1)
            linear("glu", "glu", 4, 4, lambda kt: u[:, kt, :])
            pe.wait_ge(sig("cat_ready"), 4)
            linear("ev_out", "ev_out", 2, KT, lambda kt: cat[:, kt, :])
            norm(1, L)
            pe.wait_ge(sig("hn_ready"), 2 * KT)
            b = block_of["od_small"]
            pe.wait_ge(w_in[b % RING], 16 * (b // RING + 1))
            tile = aux_of["wi"]
            begin("aux", tile)
            for qt in range(QT):
                for kt in range(KT):
                    at = KT * P + kt * 8
                    ins = mm(aux[:, tile % AUX, qt * 8:qt * 8 + 8], hn[:, kt, qt * P:(qt + 1) * P],
                             ring[:, b % RING, at:at + 8], start=kt == 0, stop=kt == KT - 1)
            fills(ins, "aux")
            linear("od_small", "od_ki", 1, KT, lambda kt: hn[:, kt, 0:L])

            def index(n):
                if not 2 <= n < 8:
                    return
                m = n - 2
                tile = aux_of["index"] + m
                begin("aux", tile)
                if m == 0:
                    taken(pe, "lin", lin_of["od_in"] + 3)
                qt, heads, width = index_heads(m)
                for q, h in enumerate(heads):
                    ins = mm(aux[:, tile % AUX, q * width:(q + 1) * width],
                             half(qi[:, h // 2, qt * P:(qt + 1) * P], h % 2), half(ki, h % 2)[:, 0:width],
                             start=True, stop=True)
                fills(ins, "aux")

            def between(n):
                index(n)
                ada(1)

            for n in range(12):
                for m in (2 * n, 2 * n + 1):
                    split_unit("od_in", m, KT, lambda kt: (od_hi[:, kt, :], od_lo[:, kt, :]), L,
                               waits=("od_low", 0) if m == 0 else None)
                between(n)
            pe.wait_ge(sig("squares_qk1"), 1)
            head_norms("kq_norm1", [[n] for n in range(10)], 1, lambda n: sq1[:, n, :])
            tokens("v_tok1", lambda n: v1[:, n], 2)
            ada(6)
            for n in range(5):
                taken(pe, "aux", aux_of["kq_norm1"] + 1 + n)
            scores(1, lambda h, qt: q1[:, h, qt * P:(qt + 1) * P], lambda h: k1[:, h // 4, :])
            ada(6)
            ada_groups(47)
            transposed_probs(1, (lh0, lh1))
            for h in range(OD_HEADS):
                tile = aux_of["out1"] + h
                begin("aux", tile)
                taken(pe, "aux", aux_of["probs1"] + h)
                cols = slice((h // 4) * P, (h // 4 + 1) * P)
                mm(aux[:, tile % AUX, 0:L], v_tok1[:, 0, cols], pt1[:, h, 0:L], start=True, stop=False)
                ins = mm(aux[:, tile % AUX, P:L], v_tok1[:, 1, cols], pt1[:, h, L:3 * P], start=False, stop=True)
                fills(ins, "aux")
            for n in range(AUX):
                taken(pe, "aux", aux_of["out1"] + OD_HEADS - 1 - n)
            linear("od_out", "od_out", 2, KT, lambda kt: q1[:, kt, :])
            both = slice(0, 2 * L)

            norm(2, 2 * L)
            split_linear("qkv", KT, lambda kt: (hn_hi[:, kt, :], hn_lo[:, kt, :]), 2 * L, ("hn_ready", KT * 2))
            pe.wait_ge(sig("at_in"), 48)
            for n in range(RING):
                taken(pe, "lin", lin_of["qkv"] + 11 - n)
            for n in range(5):
                tile = aux_of["rope"] + n
                begin("aux", tile)
                part = (k2 if n == 0 else q2[:, 2 * n - 2:2 * n])[:, :, 0:L]
                fills(mm(aux[:, tile % AUX, :], rope_perm, part, start=True, stop=True), "aux")
            for n in range(2):
                tile = aux_of["v_tok2"] + n
                begin("aux", tile)
                for m in range(4):
                    tok = (2 * n + m // 2) * P
                    ins = nc.tensor.transpose(aux[:, tile % AUX, m * P:(m + 1) * P], v2[:, m % 2, tok:tok + P], ident[:])
                fills(ins, "aux")
            pe.wait_ge(sig("masks2"), 1)
            pe.wait_ge(sig("roped"), 1)
            for i in range(AT_HEADS + 3):
                if i < AT_HEADS:
                    n, s = i // 2, i % 2
                    q, k = half(q2[:, n], s), half(k2[:, n // 4], s)
                    for qt in range(QT):
                        tile = score_tile(i, qt)
                        begin("aux", tile)
                        mm(aux[:, tile % AUX, :], q[:, qt * P:(qt + 1) * P], k, start=True, stop=False)
                        cut = slice((1 - qt) * P, (2 - qt) * P)
                        fills(mm(aux[:, tile % AUX, cut], ident_b, mask_b2[:, qt, :], start=False, stop=True), "aux")
                    tile = score_tile(i, 2)
                    begin("aux", tile)
                    for qt in range(QT):
                        ins = mm(aux[:, tile % AUX, qt * L:(qt + 1) * L], q[:, L + qt * P:L + (qt + 1) * P],
                                 k[:, L:2 * L], start=True, stop=True)
                    fills(ins, "aux")
                if i >= 4 and i % 2 == 0:
                    n = i // 2 - 2
                    tile = output_tile(n)
                    begin("lin", tile)
                    for s in range(2):
                        for m in range(3):
                            taken(pe, "lin", turned_tile(2 * n + s, m))
                    for tokens_, kts in ((slice(0, L), range(4)), (slice(L, 2 * L), range(4, 6))):
                        for kt in kts:
                            for s in range(2):
                                rows = slice(64 * s, 64 * s + 64)
                                cols = slice((n // 4) * P + 64 * s, (n // 4) * P + 64 * s + 64)
                                ins = mm(lin[rows, tile % RING, tokens_], v_tok2[:, kt if kt < 4 else kt - 2, cols],
                                         pt2[:, (2 * n + s) % 3, kt // 2, (kt % 2) * L:(kt % 2 + 1) * L],
                                         start=kt == kts[0], stop=kt == kts[-1])
                    fills(ins, "lin")
                if 2 <= i < AT_HEADS + 2:
                    h = i - 2
                    pe.wait_ge(sig("probs2"), h + 1)
                    for n in range(3):
                        tile = turned_tile(h, n)
                        begin("lin", tile)
                        for m in range(2):
                            for qt in range(QT):
                                src = p2[:, h % 3, qt, (2 * n + m) * P:(2 * n + m + 1) * P] if n < 2 else \
                                    p2[:, h % 3, 2, qt * L + m * P:qt * L + (m + 1) * P]
                                at = m * L + qt * P
                                ins = nc.tensor.transpose(lin[:, tile % RING, at:at + P], src, ident[:])
                        fills(ins, "lin")
            for n in range(8):
                taken(pe, "lin", output_tile(n))
            split_linear("w_o", KT, lambda kt: (hn_hi[:, kt, :], out_lo[:, kt, :]), 2 * L)

            def feed_forward(n, k, width):
                norm(k, width)
                for half_ in range(2):
                    split_linear(f"ffn{n}{'ab'[half_]}_in", KT, lambda kt: (hn_hi[:, kt, 0:width], hn_lo[:, kt, 0:width]),
                                 width, ("hn_ready", KT * k) if half_ == 0 else None)
                    split_linear(f"ffn{n}{'ab'[half_]}_out", FH, lambda kt: (hid_split[:, 0, kt, 0:width],
                                                                          hid_split[:, 1, kt, 0:width]),
                                 width, ("hid_ready", n * FT + half_ * FH))

            feed_forward(0, 3, 2 * L)
            norm(4, 2 * L)
            split_unit("ssm_dt", 0, KT, lambda kt: (hn_hi[:, kt, :], hn_lo[:, kt, :]), 2 * L, 2 * M_HEADS,
                       ("hn_ready", KT * 4))
            for tile in range(48):
                width = 2 * L if tile < 24 else L
                split_unit("ssm_in", tile, KT, lambda kt: (hn_hi[:, kt, 0:width], hn_lo[:, kt, 0:width]), width)
            pe.wait_ge(sig("dt_rows"), 1)
            tile = aux_of["ssm_rows"]
            begin("aux", tile)
            for n, src in enumerate((rows_g[0:64, 0:L], dt2[:, 0:L], dt2[:, L:2 * L])):
                for qt in range(QT):
                    at = (n * QT + qt) * 64
                    ins = nc.tensor.transpose(aux[:, tile % AUX, at:at + 64], src[:, qt * P:(qt + 1) * P],
                                              ident[0:64, 0:64])
            fills(ins, "aux")

            def turn(name, n, per_row, src):
                for q in range(n):
                    tile = aux_of[name] + q
                    begin("aux", tile)
                    for m in range(4):
                        tok = (q // per_row) * P
                        ins = nc.tensor.transpose(aux[:, tile % AUX, m * P:(m + 1) * P],
                                                  src((q % per_row) * 4 + m)[:, tok:tok + P], ident[:])
                    fills(ins, "aux")

            pe.wait_ge(sig("convolved"), 32)
            turn("bc_tok", 4, 2, lambda n: bm[:, n, L:2 * L])
            turn("xc_tok", 8, 4, lambda n: xc[:, n, :])
            for n in range(AUX):
                taken(pe, "aux", aux_of["xc_tok"] + 7 - n)
            for g in range(GROUPS):
                tile = aux_of["states"] + g
                begin("aux", tile)
                pe.wait_ge(sig("x_weighted"), g + 1)
                for d in range(2):
                    for qt in range(QT):
                        ins = mm(aux[:, tile % AUX, d * L:(d + 1) * L], bc_tok[:, qt, g * P:(g + 1) * P],
                                 xw[:, d, qt, :], start=qt == 0, stop=qt == 1)
                fills(ins, "aux")
            turn("x_tok", 8, 4, lambda n: ys[:, n, :])
            for n in range(AUX):
                taken(pe, "aux", aux_of["x_tok"] + 7 - n)
            for i in range(DT_ + 2):
                if i < DT_:
                    g = i // 2
                    if i % 2 == 0:
                        tile = cb_tile(g)
                        begin("aux", tile)
                        for qt in range(QT):
                            ins = mm(aux[:, tile % AUX, qt * L:(qt + 1) * L], bm[:, g, qt * P:(qt + 1) * P],
                                     cm[:, g, :], start=True, stop=True)
                        fills(ins, "aux")
                    for h in (2 * i, 2 * i + 1):
                        tile = bc_tile(h)
                        begin("aux", tile)
                        for d in range(2):
                            one = ident_split[0:64, d * 32 + h:d * 32 + h + 1].to_broadcast([64, P])
                            for part in range(2):
                                ins = mm(aux[:, tile % AUX, d * L:(d + 1) * L], one, rows_split[0:64, part],
                                         start=part == 0, stop=part == 1)
                        fills(ins, "aux")
                if i >= 2:
                    n = i - 2
                    tile = lin_of["ssm_y"] + n
                    begin("lin", tile)
                    pe.wait_ge(sig("mixed"), 2 * n + 2)
                    pe.wait_ge(sig("c_decayed"), 2 * n + 2)
                    for step in range(6):
                        for e in range(2):
                            h = 2 * n + e
                            m, f = decay[n % 3][:, e], from_start[n % 3][:, e]
                            x0, x1 = (x_tok[:, qt, h * 64:(h + 1) * 64] for qt in range(QT))
                            s0, s1 = (state[:, n // 2, d, (h % 4) * 64:(h % 4 + 1) * 64] for d in range(2))
                            lo_, hi_, mat, src = ((0, L, x0, m[:, 0:L]), (P, L, x1, m[:, L:3 * P]),
                                                 (0, P, x0, m[:, 3 * P:4 * P]), (0, L, x1, m[:, 4 * P:6 * P]),
                                                 (0, L, s0, f[:, 0]), (0, L, s1, f[:, 1]))[step]
                            ins = mm(lin[64 * e:64 * e + 64, tile % RING, lo_:hi_], mat, src, start=step == 0, stop=step == 5)
                    fills(ins, "lin")
            head_norms("y_norm", [[2 * n, 2 * n + 1] for n in range(GROUPS)], 1, lambda n: y_sq[:, n, :], "y_squares")
            linear("ssm_out", "ssm_out", 1, DT_, lambda kt: ys[:, kt, :], ready=lambda kt: taken(
                pe, "aux", aux_of["y_norm"] + 1 + kt // 4))
            feed_forward(1, 5, L)
            norm(6, L)


def host_tiles(w, per_block):
    kk, nn = w.shape
    a = w.reshape(kk // P, P, nn // P // per_block, per_block, P)
    return np.ascontiguousarray(a.transpose(2, 1, 3, 0, 4)).reshape(nn // P // per_block, P, -1)


def columns(v):
    a = v.reshape(v.shape[:-1] + (v.shape[-1] // P, P))
    return np.ascontiguousarray(np.moveaxis(a, -1, 0))


def layout(i):
    o = {}
    o["x"] = np.ascontiguousarray(i["x"][0].T.reshape(KT, P, L).transpose(1, 0, 2))
    pair_q = np.concatenate([np.arange(64) + 64 * h for j in range(4) for h in (j, j + 4)])
    w = i["ev_w_in"][0]
    q, k, v, ga, u, gb = np.split(w, np.cumsum([512, 128, 128, 512, 512]), axis=1)
    o["ev_in"] = host_tiles(np.concatenate([u, k, v, q[:, pair_q], ga[:, pair_q], gb], axis=1), 2)
    w = i["ev_w_out"][0]
    o["ev_out"] = host_tiles(np.concatenate([w[:512][pair_q], w[512:]]), 2)
    w = i["ev_glu_w"][0]
    o["glu"] = host_tiles(np.concatenate([w[:, s * 512 + n * P:s * 512 + (n + 1) * P] for n in range(4) for s in range(2)],
                                         axis=1), 4)
    w = i["od_w_in"][0]
    q, k, v, g, qi, ki, wi = np.split(w, np.cumsum([1024, 256, 256, 1024, 512, 64]), axis=1)
    small = host_tiles(np.concatenate([ki, ki], axis=1), 1)[0]
    wi = wi.reshape(KT, P, 8).transpose(1, 0, 2).reshape(P, 64)
    o["od_small"] = np.concatenate([small, wi], axis=1)[None]
    o["od_in"] = host_tiles(np.concatenate([qi, k, v, q, g], axis=1), 2)
    o["od_out"] = host_tiles(i["od_w_out"][0], 2)
    for n in range(2):
        o[f"ada{n}"] = i["ada_w_2"][n].reshape(KT, P, 24, L).transpose(2, 1, 0, 3).reshape(24, P, KT * L)
    o["od_in"] = np.stack([o["od_in"], o["ada1"][:12]], axis=1).reshape(24, P, KT * L)
    o["ada1"] = o["ada1"][12:]
    o["gcol"] = columns(i["norm_g"])
    o["modb"] = columns(i["ada_b_2"])
    cc = np.stack([i["c_2"][0], i["c_ctx_2"]]).reshape(2, KT, P).transpose(2, 1, 0)
    o["cc"] = np.concatenate([cc, np.zeros((P, KT, 30), np.float32)], axis=2)
    o["group_sum"] = (np.arange(P)[:, None] % 32 == np.arange(2)[None]).astype(np.float32)
    twice_ = lambda g: np.concatenate([g, g])
    o["qk_g"] = np.stack([twice_(i["ev_q_norm_g"][0]), twice_(i["ev_k_norm_g"][0]), i["od_q_norm_g"][0],
                          i["od_k_norm_g"][0]], axis=1)
    o["sink"] = np.repeat(i["ev_sinks"][0][None], P, axis=0)
    by_state = lambda a: a.reshape(SSM_TILES, P).T
    o["s5_par"] = np.stack([by_state(np.repeat(i["ev_ssm_log_dt"][0][:, None], 64, axis=1)),
                            by_state(i["ev_ssm_a_re"][0]), by_state(i["ev_ssm_a_im"][0])], axis=1)
    o["s5_b"] = np.stack([i[f"ev_ssm_b_{n}"][0].reshape(SSM_TILES, P, 16).transpose(1, 0, 2) for n in ("re", "im")], axis=1)
    o["s5_c"] = np.stack([i[f"ev_ssm_c_{n}"][0].transpose(0, 2, 1).reshape(SSM_TILES, P, 16).transpose(1, 0, 2)
                          for n in ("re", "im")], axis=1)
    o["d_col"] = columns(i["ev_ssm_d"][0].reshape(-1))
    o["glu_b"] = columns(i["ev_glu_b"][0])
    o["relb"] = np.repeat(i["rel_bias"][:, :, None], P, axis=2)
    o["ctx"] = np.ascontiguousarray(i["ctx_2"][0].T.reshape(KT, P, L).transpose(1, 0, 2))
    heads = [h for n in range(2) for j in range(4) for h in (8 * n + j, 8 * n + 4 + j)]
    slots = np.concatenate([np.arange(64) + 64 * h for h in heads])
    q, k, v = np.split(i["attn_w_qkv_2"][0], [1024, 1280], axis=1)
    o["qkv"] = host_tiles(np.concatenate([k, v, q[:, slots]], axis=1), 2)
    o["w_o"] = host_tiles(i["attn_w_o_2"][0][slots], 2)
    o["sink2"] = np.repeat(i["attn_sinks_2"][0][heads][None], P, axis=0)
    for n in range(2):
        gate, up = i["ffn_w_gate_2"][n], i["ffn_w_up_2"][n]
        into = host_tiles(
            np.stack([gate.reshape(D, FT, P), up.reshape(D, FT, P)], axis=2).reshape(D, 2 * FF), 2)
        for half, at in (("a", 0), ("b", FH)):
            o[f"ffn{n}{half}_in"] = into[at:at + FH]
            o[f"ffn{n}{half}_out"] = host_tiles(i["ffn_w_down_2"][n][at * P:(at + FH) * P], 1)
    z, xs, bm, cm, dt = np.split(i["ssm_w_in_2"][0], np.cumsum([DI, DI, 1024, 1024]), axis=1)
    o["ssm_in"] = host_tiles(np.concatenate([bm, xs, cm, z], axis=1), 2)
    o["ssm_dt"] = dt.reshape(KT, P, 64).transpose(1, 0, 2).reshape(1, P, KT * 64)
    o["ssm_out"] = host_tiles(i["ssm_w_out_2"][0], 1)
    taps = np.concatenate([i["ssm_conv_w_2"][0], i["ssm_conv_b_2"]])
    xs, bm, cm = np.split(taps, [DI, DI + 1024], axis=1)
    o["conv_w"] = np.moveaxis(columns(np.concatenate([bm, xs, cm], axis=1)), 1, 2)
    o["g2"] = columns(np.stack([i["norm_mix_g_2"][0], i["norm_ffn_g_2"][0], i["norm_mix_g_2"][1],
                                i["norm_ffn_g_2"][1], i["final_norm_g_2"]]))
    o["ssm_cols"] = columns(np.stack([np.repeat(i["ssm_D_2"][0], 64), i["ssm_norm_g_2"][0]]))
    o["dt_cols"] = np.stack([i["ssm_dt_bias_2"][0].reshape(-1), i["ssm_A_log_2"][0].reshape(-1)], axis=1)
    inv = np.float32(10000.0) ** (-np.arange(16, dtype=np.float32) / np.float32(16))
    feature, token = np.arange(P) % 64, np.arange(L)
    place = np.where((feature // 32 == 0)[:, None], (token // 64)[None], (token % 64)[None]).astype(np.float32)
    angle = place * inv[feature % 16][:, None]
    o["rope_cs"] = np.stack([np.cos(angle), np.sin(angle)], axis=1).astype(np.float32)
    perm = np.zeros((P, P), np.float32)
    for m in range(P):
        perm[m + 16 if m % 32 < 16 else m - 16, m] = -1.0 if m % 32 < 16 else 1.0
    o["rope_perm"] = perm
    a, b = np.arange(P)[:, None], np.arange(P)[None]
    o["mask2"] = np.stack([np.where(b <= a, 0.0, NEG), np.where(b >= a, 0.0, NEG)], axis=1).astype(np.float32)
    o["tri"] = np.stack([b >= a, b <= a], axis=1).astype(np.float32)
    o["hot"] = (t5_bucket(2 * P - 1 - np.arange(3 * P))[None] == np.arange(BUCKETS)[:, None]).astype(np.float32)
    o["ident"] = np.eye(P, dtype=np.float32)
    o["pair"] = np.kron(np.eye(2), np.ones((64, 64))).astype(np.float32)
    q, k = np.arange(P)[:, None], np.arange(L)[None]
    causal = np.where(k <= q + P, 0.0, NEG)
    window = np.where(k > q, causal, NEG)
    o["consts"] = np.concatenate([window, causal, np.repeat(np.arange(L)[None], P, axis=0)], axis=1).astype(np.float32)
    return {n: np.ascontiguousarray(a) for n, a in o.items()}


def kernel(**inputs):
    import concourse.bacc as bacc
    from concourse.bass_utils import run_bass_kernel_spmd

    arrays = layout({n: np.asarray(a) for n, a in inputs.items()})
    nc = bacc.Bacc("TRN2", target_bir_lowering=False, num_devices=1)
    t = {n: nc.dram_tensor(n + "_in", a.shape, mybir.dt.from_np(a.dtype), kind="ExternalInput").ap()
         for n, a in arrays.items()}
    t["skew"] = nc.dram_tensor("skew", (EV_HEADS, P, 3 * P), F32, kind="Internal").ap()
    t["out"] = nc.dram_tensor("out", (P, KT, L), F32, kind="ExternalOutput").ap()
    program(nc, t)
    r = run_bass_kernel_spmd(nc, [{n + "_in": a for n, a in arrays.items()}], core_ids=[0])
    y = np.asarray(r.results[0]["out"])
    return np.ascontiguousarray(y.transpose(2, 1, 0)).reshape(1, L, D)
```
